# Optimizing a Trainium2 kernel written in Bass

```python
import jax, jax.numpy as jnp
from jax import lax
import numpy as np
import math
import jax
import jax.numpy as jnp

D_MODEL = 1024
BATCH = 1
SEQ = 256
DEPTH = 2

N_MIXERS = 2
N_A_LAYERS = (DEPTH + N_MIXERS - 1) // N_MIXERS
N_B_LAYERS = DEPTH // N_MIXERS

HG_HEADS = 8
HG_DK = D_MODEL // HG_HEADS
HG_DV = D_MODEL // HG_HEADS
HG_CHUNK = 128
LRU_WIDTH = D_MODEL
LRU_BLOCKS = 4
LRU_BW = LRU_WIDTH // LRU_BLOCKS
CONV_W = 4
CONV_LEFT = 2
LRU_C = 8.0
PEER_HEADS = 8
PEER_NKEYS = 128
PEER_NEXPERTS = PEER_NKEYS * PEER_NKEYS
PEER_DQ = 256
PEER_TOPK = 16
PEER_BLOCK = 128
EPS = 1e-6


def rms_norm(x, gain):
    xf = x.astype(jnp.float32)
    inv = lax.rsqrt(jnp.mean(xf * xf, axis=-1, keepdims=True) + EPS)
    return (xf * inv).astype(x.dtype) * gain

def hgrn2_chunk_scan(q, k, v, log_f):
    B, S, H, DK = q.shape
    DV = v.shape[-1]
    C = HG_CHUNK
    nc = S // C

    def to_chunks(t):
        return t.reshape(B, nc, C, H, t.shape[-1]).transpose(1, 0, 3, 2, 4)

    qc, kc, vc, gc = to_chunks(q), to_chunks(k), to_chunks(v), to_chunks(log_f)
    lower = jnp.tril(jnp.ones((C, C), dtype=bool))[:, :, None]

    def step(state, inp):
        qi, ki, vi, gi = inp
        b = jnp.cumsum(gi.astype(jnp.float32), axis=-2)
        b_last = b[..., -1:, :]
        rel = b[..., :, None, :] - b[..., None, :, :]
        decay = jnp.exp(jnp.where(lower, rel, -jnp.inf))
        attn = jnp.sum((qi[..., :, None, :] * ki[..., None, :, :]) * decay, axis=-1)
        o_intra = jnp.einsum('bhts,bhsv->bhtv', attn, vi)
        o_inter = jnp.einsum('bhtd,bhdv->bhtv', qi * jnp.exp(b), state)
        k_dec = ki * jnp.exp(b_last - b)
        new_state = state * jnp.exp(b_last[..., 0, :])[..., None] + jnp.einsum('bhsd,bhsv->bhdv', k_dec, vi)
        return new_state, o_intra + o_inter

    state0 = jnp.zeros((B, H, DK, DV), jnp.float32)
    _, o = lax.scan(step, state0, (qc, kc, vc, gc))
    return o.transpose(1, 0, 3, 2, 4).reshape(B, S, H, DV)

def hgrn2_mixer(h, w_in, lb, norm_g, w_out):
    B, S, _ = h.shape
    proj = h @ w_in
    q, f_fw, f_bw, i_in, g = jnp.split(proj, 5, axis=-1)

    def heads(t):
        return t.reshape(B, S, HG_HEADS, -1)

    q, v, g = heads(q), heads(i_in), heads(g)

    def gates(f_logit):
        f = lb + (1.0 - lb) * jax.nn.sigmoid(f_logit.astype(jnp.float32))
        return heads(jnp.log(f)), heads(1.0 - f)

    logf_fw, k_fw = gates(f_fw)
    logf_bw, k_bw = gates(f_bw)
    rev = lambda t: t[:, ::-1]
    o_fw = hgrn2_chunk_scan(q, k_fw, v, logf_fw)
    o_bw = rev(hgrn2_chunk_scan(rev(q), rev(k_bw), rev(v), rev(logf_bw)))
    o = rms_norm(o_fw + o_bw, norm_g.reshape(HG_HEADS, HG_DV)) * jax.nn.silu(g)
    return o.reshape(B, S, D_MODEL) @ w_out

def block_diag_linear(x, w, b):
    B, S, _ = x.shape
    xr = x.reshape(B, S, LRU_BLOCKS, LRU_BW)
    return jnp.einsum('bsnk,nkj->bsnj', xr, w).reshape(B, S, LRU_WIDTH) + b

def lin_combine(left, right):
    a_l, b_l = left
    a_r, b_r = right
    return a_l * a_r, a_r * b_l + b_r

def rglru_mixer(h, w_in, conv_w, conv_b, w_a, b_a, w_x, b_x, lam, w_out):
    B, S, _ = h.shape
    proj = h @ w_in
    xb, yb = jnp.split(proj, 2, axis=-1)
    y_gate = jax.nn.gelu(yb)
    xp = jnp.pad(xb, ((0, 0), (CONV_LEFT, CONV_W - 1 - CONV_LEFT), (0, 0)))
    xc = sum(xp[:, j:j + S] * conv_w[j] for j in range(CONV_W)) + conv_b

    def direction(d, reverse):
        r = jax.nn.sigmoid(block_diag_linear(xc, w_a[d], b_a[d]).astype(jnp.float32))
        ig = jax.nn.sigmoid(block_diag_linear(xc, w_x[d], b_x[d]).astype(jnp.float32))
        log_a = -LRU_C * r * jax.nn.softplus(-lam[d].astype(jnp.float32))
        a = jnp.exp(log_a)
        mult = jnp.sqrt(-jnp.expm1(2.0 * log_a))
        _, hs = lax.associative_scan(lin_combine, (a, mult * ig * xc), axis=1, reverse=reverse)
        return hs

    hsum = direction(0, False) + direction(1, True)
    return (hsum * y_gate) @ w_out

def peer_ffn(h, w_q, sub_keys, u_tab, v_tab):
    B, S, D = h.shape
    q = (h @ w_q).reshape(B, S, PEER_HEADS, 2, PEER_DQ // 2)
    scores = jnp.einsum('bshpd,hpkd->bshpk', q, sub_keys).astype(jnp.float32)
    s1, i1 = lax.top_k(scores[..., 0, :], PEER_TOPK)
    s2, i2 = lax.top_k(scores[..., 1, :], PEER_TOPK)
    cand_s = (s1[..., :, None] + s2[..., None, :]).reshape(B, S, PEER_HEADS, PEER_TOPK * PEER_TOPK)
    cand_id = (i1[..., :, None] * PEER_NKEYS + i2[..., None, :]).reshape(B, S, PEER_HEADS, PEER_TOPK * PEER_TOPK)
    top_s, top_pos = lax.top_k(cand_s, PEER_TOPK)
    ids = jnp.take_along_axis(cand_id, top_pos, axis=-1)
    gate = jax.nn.softmax(top_s, axis=-1)

    nb = (B * S) // PEER_BLOCK
    hb = h.reshape(nb, PEER_BLOCK, D)
    idb = ids.reshape(nb, PEER_BLOCK, PEER_HEADS, PEER_TOPK)
    gb = gate.reshape(nb, PEER_BLOCK, PEER_HEADS, PEER_TOPK)

    def block(args):
        hx, idx, g = args
        u = u_tab[idx]
        act = jax.nn.gelu(jnp.einsum('thkd,td->thk', u, hx).astype(jnp.float32))
        return jnp.einsum('thk,thkd->td', g * act, v_tab[idx])

    out = lax.map(block, (hb, idb, gb))
    return out.reshape(B, S, D)

def first_inputs(seed: int = 0) -> dict:
    key = jax.random.key(seed)
    ks = iter(jax.random.split(key, 32))
    D = D_MODEL

    def nrm(shape, scale):
        return jax.random.normal(next(ks), shape, jnp.float32) * scale

    x = nrm((BATCH, SEQ, D), 1.0)
    c = nrm((BATCH, D), 1.0)
    w_ada = nrm((DEPTH, D, 6 * D), 0.5 * D ** -0.5)
    b_ada = nrm((DEPTH, 6 * D), 0.02)
    norm_g = 1.0 + nrm((DEPTH, 2, D), 0.02)
    hg_w_in = nrm((N_A_LAYERS, D, 5 * D), D ** -0.5)
    hg_lb = nrm((N_A_LAYERS, D), 1.0)
    hg_norm_g = 1.0 + nrm((N_A_LAYERS, D), 0.02)
    hg_w_out = nrm((N_A_LAYERS, D, D), D ** -0.5)
    lru_w_in = nrm((N_B_LAYERS, D, 2 * LRU_WIDTH), D ** -0.5)
    lru_conv_w = nrm((N_B_LAYERS, CONV_W, LRU_WIDTH), 0.5)
    lru_conv_b = nrm((N_B_LAYERS, LRU_WIDTH), 0.02)
    lru_w_a = nrm((N_B_LAYERS, 2, LRU_BLOCKS, LRU_BW, LRU_BW), LRU_BW ** -0.5)
    lru_b_a = nrm((N_B_LAYERS, 2, LRU_WIDTH), 0.02)
    lru_w_x = nrm((N_B_LAYERS, 2, LRU_BLOCKS, LRU_BW, LRU_BW), LRU_BW ** -0.5)
    lru_b_x = nrm((N_B_LAYERS, 2, LRU_WIDTH), 0.02)
    a_c = jax.random.uniform(next(ks), (N_B_LAYERS, 2, LRU_WIDTH), jnp.float32, 0.9, 0.999)
    a_base = a_c ** (1.0 / LRU_C)
    lru_lam = jnp.log(a_base) - jnp.log1p(-a_base)
    lru_w_out = nrm((N_B_LAYERS, LRU_WIDTH, D), LRU_WIDTH ** -0.5)
    peer_w_q = nrm((DEPTH, D, PEER_HEADS * PEER_DQ), D ** -0.5)
    peer_keys = nrm((DEPTH, PEER_HEADS, 2, PEER_NKEYS, PEER_DQ // 2), (PEER_DQ // 2) ** -0.5)
    peer_u = nrm((DEPTH, PEER_NEXPERTS, D), D ** -0.5)
    peer_v = nrm((DEPTH, PEER_NEXPERTS, D), PEER_HEADS ** -0.5)
    final_g = 1.0 + nrm((D,), 0.02)
    return {"x": x, "c": c, "w_ada": w_ada, "b_ada": b_ada, "norm_g": norm_g,
            "hg_w_in": hg_w_in, "hg_lb": hg_lb, "hg_norm_g": hg_norm_g, "hg_w_out": hg_w_out,
            "lru_w_in": lru_w_in, "lru_conv_w": lru_conv_w, "lru_conv_b": lru_conv_b,
            "lru_w_a": lru_w_a, "lru_b_a": lru_b_a, "lru_w_x": lru_w_x, "lru_b_x": lru_b_x,
            "lru_lam": lru_lam, "lru_w_out": lru_w_out,
            "peer_w_q": peer_w_q, "peer_keys": peer_keys, "peer_u": peer_u, "peer_v": peer_v,
            "final_g": final_g}

def first_block(x, c, w_ada, b_ada, norm_g, hg_w_in, hg_lb, hg_norm_g, hg_w_out,
              lru_w_in, lru_conv_w, lru_conv_b, lru_w_a, lru_b_a, lru_w_x, lru_b_x,
              lru_lam, lru_w_out, peer_w_q, peer_keys, peer_u, peer_v, final_g):
    p = jax.nn.softmax(hg_lb.astype(jnp.float32), axis=0)
    lbs = jnp.cumsum(p, axis=0) - p[0]
    cond = jax.nn.silu(c)
    for i in range(DEPTH):
        mod = (cond @ w_ada[i] + b_ada[i])[:, None, :]
        sh1, sc1, g1, sh2, sc2, g2 = jnp.split(mod, 6, axis=-1)
        h = rms_norm(x, norm_g[i, 0]) * (1.0 + sc1) + sh1
        j = i // N_MIXERS
        if i % N_MIXERS == 0:
            y = hgrn2_mixer(h, hg_w_in[j], lbs[j], hg_norm_g[j], hg_w_out[j])
        else:
            y = rglru_mixer(h, lru_w_in[j], lru_conv_w[j], lru_conv_b[j], lru_w_a[j], lru_b_a[j],
                            lru_w_x[j], lru_b_x[j], lru_lam[j], lru_w_out[j])
        x = x + g1 * y
        h = rms_norm(x, norm_g[i, 1]) * (1.0 + sc2) + sh2
        x = x + g2 * peer_ffn(h, peer_w_q[i], peer_keys[i], peer_u[i], peer_v[i])
    return rms_norm(x, final_g)


DEEPNORM_ALPHA = (2 * DEPTH) ** 0.25
DEEPNORM_BETA = (8 * DEPTH) ** -0.25
LN_EPS = 1e-5
RMS_EPS = 1e-6
NUM_BUCKETS = 32
REL_MAX_DIST = 2048
REL_HEADS = 4
GDN_HEADS = 6
GDN_DK = 128
GDN_DV = 128
GDN_CONV = 4
GDN_CHUNK = 64
GDN_QK = GDN_HEADS * GDN_DK
GDN_V = GDN_HEADS * GDN_DV
SWA_CONFIGS = ((128, 1), (512, 4), (2048, 16))
SWA_GROUPS = len(SWA_CONFIGS)
SWA_HEADS = 4
SWA_HEAD_DIM = 64
SWA_BLOCK = 128
SWA_QKV = SWA_GROUPS * SWA_HEADS * SWA_HEAD_DIM
SWA_OUT = SWA_HEADS * SWA_HEAD_DIM
DIFF_HEADS = 4
DIFF_HEAD_DIM = 64
DIFF_QK = DIFF_HEADS * 2 * DIFF_HEAD_DIM
DIFF_V = DIFF_HEADS * 2 * DIFF_HEAD_DIM
Q_BLOCK = 128
GLA_HEADS = 4
GLA_DK = 64
GLA_DV = 128
GLA_GATE_RANK = 16
GLA_GATE_TAU = 16.0
GLA_CHUNK = 64
GLA_QK = GLA_HEADS * GLA_DK
GLA_V = GLA_HEADS * GLA_DV
D_FF = 2816
FFN_CONV = 3

EVEN_SIZES = (GDN_QK, GDN_QK, GDN_V, GDN_V, GDN_HEADS, GDN_HEADS, SWA_QKV, SWA_QKV, SWA_QKV)
EVEN_IN = sum(EVEN_SIZES)
EVEN_SPLITS = tuple(int(v) for v in np.cumsum(EVEN_SIZES)[:-1])
EVEN_OUT = GDN_V + SWA_OUT
ODD_SIZES = (DIFF_QK, DIFF_QK, DIFF_V, GLA_QK, GLA_QK, GLA_V, GLA_V, GLA_GATE_RANK)
ODD_IN = sum(ODD_SIZES)
ODD_SPLITS = tuple(int(v) for v in np.cumsum(ODD_SIZES)[:-1])
ODD_OUT = DIFF_V + GLA_V
N_EVEN = (DEPTH + 1) // 2
N_ODD = DEPTH // 2


def layer_norm(x, g, b):
    xf = x.astype(jnp.float32)
    mu = jnp.mean(xf, -1, keepdims=True)
    var = jnp.mean(jnp.square(xf - mu), -1, keepdims=True)
    y = (xf - mu) * lax.rsqrt(var + LN_EPS) * g.astype(jnp.float32) + b.astype(jnp.float32)
    return y.astype(x.dtype)

def rms_norm_2(x, w):
    xf = x.astype(jnp.float32)
    return xf * lax.rsqrt(jnp.mean(xf * xf, -1, keepdims=True) + RMS_EPS) * w.astype(jnp.float32)

def l2_normalize(x):
    return x * lax.rsqrt(jnp.sum(x * x, -1, keepdims=True) + RMS_EPS)

def causal_depthwise_conv(x, w):
    width, seq = w.shape[0], x.shape[1]
    xp = jnp.pad(x, ((0, 0), (width - 1, 0), (0, 0)))
    y = w[0] * xp[:, :seq]
    for j in range(1, width):
        y = y + w[j] * xp[:, j:j + seq]
    return y

def rel_bucket(dist):
    max_exact = NUM_BUCKETS // 2
    d = jnp.maximum(dist, 1).astype(jnp.float32)
    large = max_exact + (jnp.log(d / max_exact) / math.log(REL_MAX_DIST / max_exact)
                         * (NUM_BUCKETS - max_exact)).astype(jnp.int32)
    large = jnp.minimum(large, NUM_BUCKETS - 1)
    return jnp.where(dist < max_exact, dist, large)

def gated_delta_rule(q, k, v, g, beta):
    bsz, seq, nh, dk = q.shape
    dv = v.shape[-1]
    c = GDN_CHUNK
    n = seq // c

    def chunk(t):
        return jnp.moveaxis(t.reshape((bsz, n, c, nh) + t.shape[3:]), 3, 1)

    qc, kc, vc, gc, bc = chunk(q), chunk(k), chunk(v), chunk(g), chunk(beta)
    gam = jnp.cumsum(gc, axis=-1)
    idx = jnp.arange(c)
    incl = idx[:, None] >= idx[None, :]
    strict = idx[:, None] > idx[None, :]
    decay = jnp.exp(jnp.where(incl, gam[..., :, None] - gam[..., None, :], -jnp.inf))
    kk = jnp.einsum('bhnid,bhnjd->bhnij', kc, kc)
    lower = jnp.eye(c, dtype=jnp.float32) + jnp.where(strict, bc[..., :, None] * kk * decay, 0.0)
    rhs = jnp.concatenate([vc * bc[..., None], kc * (bc * jnp.exp(gam))[..., None]], axis=-1)
    sol = lax.linalg.triangular_solve(lower, rhs, left_side=True, lower=True, unit_diagonal=True)
    u, w = sol[..., :dv], sol[..., dv:]
    qk = jnp.einsum('bhnid,bhnjd->bhnij', qc, kc) * decay
    q_dec = qc * jnp.exp(gam)[..., None]
    k_dec = kc * jnp.exp(gam[..., -1:] - gam)[..., None]
    g_last = jnp.exp(gam[..., -1])

    def step(state, inp):
        u_n, w_n, qk_n, qd_n, kd_n, gl_n = inp
        delta = u_n - jnp.einsum('bhck,bhkv->bhcv', w_n, state)
        o_n = jnp.einsum('bhck,bhkv->bhcv', qd_n, state) + jnp.einsum('bhij,bhjv->bhiv', qk_n, delta)
        state = gl_n[..., None, None] * state + jnp.einsum('bhck,bhcv->bhkv', kd_n, delta)
        return state, o_n

    xs = tuple(jnp.moveaxis(t, 2, 0) for t in (u, w, qk, q_dec, k_dec, g_last))
    state0 = jnp.zeros((bsz, nh, dk, dv), jnp.float32)
    _, o = lax.scan(step, state0, xs)
    return o.transpose(1, 0, 3, 2, 4).reshape(bsz, seq, nh, dv)

def dilated_branch(q, k, v, window, dilation, rel_bias):
    bsz, seq, nh, dh = q.shape
    span = window // dilation
    sub = seq // dilation
    nb = -(-sub // SWA_BLOCK)
    padded = nb * SWA_BLOCK

    def to_blocks(t):
        t = t.reshape(bsz, sub, dilation, nh, dh).transpose(0, 2, 1, 3, 4)
        t = jnp.pad(t, ((0, 0), (0, 0), (0, padded - sub), (0, 0), (0, 0)))
        return t.reshape(bsz, dilation, nb, SWA_BLOCK, nh, dh)

    def with_prev(t):
        prev = jnp.pad(t, ((0, 0), (0, 0), (1, 0), (0, 0), (0, 0), (0, 0)))[:, :, :-1]
        return jnp.concatenate([prev, t], axis=3)

    qb = to_blocks(q)
    kb, vb = with_prev(to_blocks(k)), with_prev(to_blocks(v))
    qi = jnp.arange(SWA_BLOCK)[:, None] + SWA_BLOCK
    kj = jnp.arange(2 * SWA_BLOCK)[None, :]
    rel = qi - kj
    key_sub = jnp.arange(nb)[:, None, None] * SWA_BLOCK + kj[None] - SWA_BLOCK
    mask = (rel >= 0) & (rel <= span) & (key_sub >= 0)
    bias = jnp.moveaxis(rel_bias[rel_bucket(jnp.maximum(rel, 0) * dilation)], -1, 0)
    s = jnp.einsum('bgnqhd,bgnkhd->bgnhqk', qb, kb).astype(jnp.float32) * dh ** -0.5
    s = s + bias.astype(jnp.float32)
    s = jnp.where(mask[None, None, :, None], s, -jnp.inf)
    m = jnp.max(s, axis=-1, keepdims=True)
    p = jnp.exp(s - m)
    l = jnp.sum(p, axis=-1, keepdims=True)
    o = jnp.einsum('bgnhqk,bgnkhd->bgnqhd', (p / l).astype(v.dtype), vb)
    lse = (m + jnp.log(l))[..., 0]
    o = o.reshape(bsz, dilation, padded, nh, dh)[:, :, :sub]
    o = o.transpose(0, 2, 1, 3, 4).reshape(bsz, seq, nh, dh)
    lse = lse.transpose(0, 1, 2, 4, 3).reshape(bsz, dilation, padded, nh)[:, :, :sub]
    lse = lse.transpose(0, 2, 1, 3).reshape(bsz, seq, nh)
    return o, lse

def dilated_attention(q, k, v, rel_bias):
    bsz, seq = q.shape[0], q.shape[1]
    outs, lses = [], []
    for g, (window, dilation) in enumerate(SWA_CONFIGS):
        o, lse = dilated_branch(q[:, :, g], k[:, :, g], v[:, :, g], window, dilation, rel_bias)
        outs.append(o)
        lses.append(lse)
    wts = jax.nn.softmax(jnp.stack(lses, 0), axis=0)
    o = jnp.einsum('gbsh,gbshd->bshd', wts, jnp.stack(outs, 0).astype(jnp.float32))
    return o.reshape(bsz, seq, SWA_OUT)

def even_mixer(x, rel_bias, w_in, conv_w, a_log, dt_bias, norm_w, w_out):
    bsz, seq, _ = x.shape
    f32 = jnp.float32
    q_a, k_a, v_a, z_a, b_a, a_a, q_b, k_b, v_b = jnp.split(x @ w_in, EVEN_SPLITS, axis=-1)
    qkv = jax.nn.silu(causal_depthwise_conv(jnp.concatenate([q_a, k_a, v_a], -1), conv_w)).astype(f32)
    q_a, k_a, v_a = jnp.split(qkv, (GDN_QK, 2 * GDN_QK), axis=-1)
    hk = (bsz, seq, GDN_HEADS, GDN_DK)
    q_a = l2_normalize(q_a.reshape(hk)) * GDN_DK ** -0.5
    k_a = l2_normalize(k_a.reshape(hk))
    v_a = v_a.reshape(bsz, seq, GDN_HEADS, GDN_DV)
    beta = jax.nn.sigmoid(b_a.astype(f32))
    g = -jnp.exp(a_log.astype(f32)) * jax.nn.softplus(a_a.astype(f32) + dt_bias.astype(f32))
    o_a = gated_delta_rule(q_a, k_a, v_a, g, beta)
    o_a = rms_norm_2(o_a, norm_w) * jax.nn.silu(z_a.astype(f32).reshape(bsz, seq, GDN_HEADS, GDN_DV))
    o_a = o_a.reshape(bsz, seq, GDN_V).astype(x.dtype)
    shp = (bsz, seq, SWA_GROUPS, SWA_HEADS, SWA_HEAD_DIM)
    o_b = dilated_attention(q_b.reshape(shp), k_b.reshape(shp), v_b.reshape(shp), rel_bias).astype(x.dtype)
    return jnp.concatenate([o_a, o_b], axis=-1) @ w_out

def diff_attention(q, k, v, lam, rel_bias):
    bsz, seq, nh, _, dh = q.shape
    nq = seq // Q_BLOCK
    qb = q.reshape(bsz, nq, Q_BLOCK, nh, 2, dh).transpose(1, 0, 3, 4, 2, 5)
    kt = k.transpose(0, 2, 3, 1, 4)
    vt = v.transpose(0, 2, 1, 3)
    k_pos = jnp.arange(seq)

    def block(args):
        q_blk, start = args
        dist = (start + jnp.arange(Q_BLOCK))[:, None] - k_pos[None, :]
        bias = jnp.moveaxis(rel_bias[rel_bucket(jnp.maximum(dist, 0))], -1, 0).astype(jnp.float32)
        s = jnp.einsum('bhcqd,bhckd->bhcqk', q_blk, kt).astype(jnp.float32) * dh ** -0.5
        s = jnp.where(dist >= 0, s + bias[None, :, None], -jnp.inf)
        p = jax.nn.softmax(s, axis=-1)
        attn = p[:, :, 0] - lam * p[:, :, 1]
        return jnp.einsum('bhqk,bhkv->bhqv', attn.astype(v.dtype), vt)

    o = lax.map(block, (qb, jnp.arange(nq) * Q_BLOCK))
    return o.transpose(1, 0, 3, 2, 4).reshape(bsz, seq, nh, 2 * dh)

def gla_chunked(q, k, v, log_a):
    bsz, seq, nh, dk = q.shape
    dv = v.shape[-1]
    c = GLA_CHUNK
    n = seq // c

    def chunk(t):
        return t.reshape(bsz, n, c, nh, t.shape[-1]).transpose(1, 0, 3, 2, 4)

    qc, kc, vc = chunk(q), chunk(k), chunk(v)
    bc = jnp.cumsum(chunk(log_a), axis=3)
    idx = jnp.arange(c)
    incl = (idx[:, None] >= idx[None, :])[:, :, None]

    def step(state, inp):
        q_n, k_n, v_n, b_n = inp
        dec = jnp.exp(jnp.where(incl, b_n[..., :, None, :] - b_n[..., None, :, :], -jnp.inf))
        attn = jnp.einsum('bhik,bhjk,bhijk->bhij', q_n, k_n, dec)
        o_n = jnp.einsum('bhik,bhkv->bhiv', q_n * jnp.exp(b_n), state) + jnp.einsum('bhij,bhjv->bhiv', attn, v_n)
        b_last = b_n[..., -1:, :]
        state = jnp.exp(b_last[..., 0, :])[..., None] * state + jnp.einsum(
            'bhck,bhcv->bhkv', k_n * jnp.exp(b_last - b_n), v_n)
        return state, o_n

    state0 = jnp.zeros((bsz, nh, dk, dv), jnp.float32)
    _, o = lax.scan(step, state0, (qc, kc, vc, bc))
    return o.transpose(1, 0, 3, 2, 4).reshape(bsz, seq, nh, dv)

def odd_mixer(x, rel_bias, w_in, lam_params, diff_norm_w, gla_w_gate, gla_b_gate, gla_norm_w, w_out, lam_init):
    bsz, seq, _ = x.shape
    f32 = jnp.float32
    q_c, k_c, v_c, q_d, k_d, v_d, r_d, g_d = jnp.split(x @ w_in, ODD_SPLITS, axis=-1)
    lp = lam_params.astype(f32)
    lam = jnp.exp(jnp.sum(lp[0] * lp[1])) - jnp.exp(jnp.sum(lp[2] * lp[3])) + lam_init
    shp = (bsz, seq, DIFF_HEADS, 2, DIFF_HEAD_DIM)
    o_c = diff_attention(q_c.reshape(shp), k_c.reshape(shp),
                         v_c.reshape(bsz, seq, DIFF_HEADS, 2 * DIFF_HEAD_DIM), lam, rel_bias)
    o_c = (rms_norm_2(o_c, diff_norm_w) * (1.0 - lam_init)).reshape(bsz, seq, DIFF_V).astype(x.dtype)
    log_a = jax.nn.log_sigmoid((g_d @ gla_w_gate + gla_b_gate).astype(f32)) / GLA_GATE_TAU
    hk = (bsz, seq, GLA_HEADS, GLA_DK)
    o_d = gla_chunked(q_d.astype(f32).reshape(hk) * GLA_DK ** -0.5, k_d.astype(f32).reshape(hk),
                      v_d.astype(f32).reshape(bsz, seq, GLA_HEADS, GLA_DV), log_a.reshape(hk))
    o_d = rms_norm_2(o_d, gla_norm_w) * jax.nn.silu(r_d.astype(f32).reshape(bsz, seq, GLA_HEADS, GLA_DV))
    o_d = o_d.reshape(bsz, seq, GLA_V).astype(x.dtype)
    return jnp.concatenate([o_c, o_d], axis=-1) @ w_out

def conv_ffn(x, w_up, conv_w, conv_b, w_down):
    h = causal_depthwise_conv(x @ w_up, conv_w) + conv_b
    gate, val = jnp.split(h, 2, axis=-1)
    return (jax.nn.silu(gate) * val) @ w_down

def second_inputs(seed: int = 0) -> dict:
    key = jax.random.key(seed)
    ks = jax.random.split(key, 24)
    f32 = jnp.float32

    def normal(k, shape, scale):
        return jax.random.normal(k, shape, f32) * scale

    dt = jnp.exp(jax.random.uniform(ks[5], (N_EVEN, GDN_HEADS), f32, math.log(1e-3), math.log(1e-1)))
    return {
        'x': normal(ks[0], (BATCH, SEQ, D_MODEL), 1.0),
        'rel_bias': normal(ks[1], (NUM_BUCKETS, REL_HEADS), 0.1),
        'w_in_even': normal(ks[2], (N_EVEN, D_MODEL, EVEN_IN), D_MODEL ** -0.5),
        'gdn_conv_w': normal(ks[3], (N_EVEN, GDN_CONV, 2 * GDN_QK + GDN_V), GDN_CONV ** -0.5),
        'gdn_a_log': jnp.log(jax.random.uniform(ks[4], (N_EVEN, GDN_HEADS), f32, 1.0, 16.0)),
        'gdn_dt_bias': dt + jnp.log(-jnp.expm1(-dt)),
        'gdn_norm_w': 1.0 + normal(ks[6], (N_EVEN, GDN_DV), 0.05),
        'w_out_even': normal(ks[7], (N_EVEN, EVEN_OUT, D_MODEL), EVEN_OUT ** -0.5 * DEEPNORM_BETA),
        'w_in_odd': normal(ks[8], (N_ODD, D_MODEL, ODD_IN), D_MODEL ** -0.5),
        'diff_lambda': normal(ks[9], (N_ODD, 4, DIFF_HEAD_DIM), 0.1),
        'diff_norm_w': 1.0 + normal(ks[10], (N_ODD, 2 * DIFF_HEAD_DIM), 0.05),
        'gla_w_gate': normal(ks[11], (N_ODD, GLA_GATE_RANK, GLA_QK), GLA_GATE_RANK ** -0.5),
        'gla_b_gate': normal(ks[12], (N_ODD, GLA_QK), 0.1),
        'gla_norm_w': 1.0 + normal(ks[13], (N_ODD, GLA_DV), 0.05),
        'w_out_odd': normal(ks[14], (N_ODD, ODD_OUT, D_MODEL), ODD_OUT ** -0.5 * DEEPNORM_BETA),
        'ffn_w_up': normal(ks[15], (DEPTH, D_MODEL, 2 * D_FF), D_MODEL ** -0.5),
        'ffn_conv_w': normal(ks[16], (DEPTH, FFN_CONV, 2 * D_FF), FFN_CONV ** -0.5),
        'ffn_conv_b': normal(ks[17], (DEPTH, 2 * D_FF), 0.02),
        'ffn_w_down': normal(ks[18], (DEPTH, D_FF, D_MODEL), D_FF ** -0.5 * DEEPNORM_BETA),
        'ln_g': 1.0 + normal(ks[19], (DEPTH, 2, D_MODEL), 0.05),
        'ln_b': normal(ks[20], (DEPTH, 2, D_MODEL), 0.02),
    }

def second_block(x, rel_bias, w_in_even, gdn_conv_w, gdn_a_log, gdn_dt_bias, gdn_norm_w, w_out_even,
              w_in_odd, diff_lambda, diff_norm_w, gla_w_gate, gla_b_gate, gla_norm_w, w_out_odd,
              ffn_w_up, ffn_conv_w, ffn_conv_b, ffn_w_down, ln_g, ln_b):
    h = x
    for layer in range(DEPTH):
        i = layer // 2
        if layer % 2 == 0:
            mix = even_mixer(h, rel_bias, w_in_even[i], gdn_conv_w[i], gdn_a_log[i], gdn_dt_bias[i],
                             gdn_norm_w[i], w_out_even[i])
        else:
            lam_init = 0.8 - 0.6 * math.exp(-0.3 * layer)
            mix = odd_mixer(h, rel_bias, w_in_odd[i], diff_lambda[i], diff_norm_w[i], gla_w_gate[i],
                            gla_b_gate[i], gla_norm_w[i], w_out_odd[i], lam_init)
        h = layer_norm(DEEPNORM_ALPHA * h + mix, ln_g[layer, 0], ln_b[layer, 0])
        ffn = conv_ffn(h, ffn_w_up[layer], ffn_conv_w[layer], ffn_conv_b[layer], ffn_w_down[layer])
        h = layer_norm(DEEPNORM_ALPHA * h + ffn, ln_g[layer, 1], ln_b[layer, 1])
    return h


def setup_inputs(seed=0):
    out = dict(first_inputs(seed))
    for name, value in second_inputs(seed + 1).items():
        if name != "x":
            out[name + "_2"] = value
    return out


def reference(
    x, c, w_ada, b_ada, norm_g, hg_w_in, hg_lb, hg_norm_g, hg_w_out, lru_w_in, lru_conv_w,
    lru_conv_b, lru_w_a, lru_b_a, lru_w_x, lru_b_x, lru_lam, lru_w_out, peer_w_q, peer_keys,
    peer_u, peer_v, final_g, rel_bias_2, w_in_even_2, gdn_conv_w_2, gdn_a_log_2, gdn_dt_bias_2,
    gdn_norm_w_2, w_out_even_2, w_in_odd_2, diff_lambda_2, diff_norm_w_2, gla_w_gate_2,
    gla_b_gate_2, gla_norm_w_2, w_out_odd_2, ffn_w_up_2, ffn_conv_w_2, ffn_conv_b_2,
    ffn_w_down_2, ln_g_2, ln_b_2,
):
    x = first_block(
        x, c, w_ada, b_ada, norm_g, hg_w_in, hg_lb, hg_norm_g, hg_w_out, lru_w_in, lru_conv_w,
        lru_conv_b, lru_w_a, lru_b_a, lru_w_x, lru_b_x, lru_lam, lru_w_out, peer_w_q, peer_keys,
        peer_u, peer_v, final_g,
    )
    return second_block(
        x, rel_bias_2, w_in_even_2, gdn_conv_w_2, gdn_a_log_2, gdn_dt_bias_2, gdn_norm_w_2,
        w_out_even_2, w_in_odd_2, diff_lambda_2, diff_norm_w_2, gla_w_gate_2, gla_b_gate_2,
        gla_norm_w_2, w_out_odd_2, ffn_w_up_2, ffn_conv_w_2, ffn_conv_b_2, ffn_w_down_2, ln_g_2,
        ln_b_2,
    )


_drawn_inputs = setup_inputs


def setup_inputs(seed=0):
    import zlib

    import numpy as np

    out = dict(_drawn_inputs(seed))
    spreads = {}
    factors = {'norm_g': 2.822,
     'hg_norm_g': 7.714,
     'lru_b_a': 8.0,
     'lru_b_x': 8.0,
     'rel_bias_2': 5.798,
     'gdn_norm_w_2': 5.396,
     'diff_lambda_2': 8.0,
     'diff_norm_w_2': 7.075,
     'gla_b_gate_2': 7.167,
     'gla_norm_w_2': 7.266,
     'ffn_conv_b_2': 6.584}
    for name, (base, spread) in spreads.items():
        noise = np.random.default_rng([zlib.crc32(name.encode()), seed]).standard_normal(out[name].shape)
        drawn = base * np.exp(spread * noise) if base else spread * noise
        out[name] = jnp.asarray(drawn.astype(out[name].dtype))
    for name, factor in factors.items():
        out[name] = (out[name] * factor).astype(out[name].dtype)
    return out
```

```python
import math
from contextlib import ExitStack

import numpy as np

import concourse.bass as bass
from concourse import mybir

F32 = mybir.dt.float32
U32 = mybir.dt.uint32
ALU = mybir.AluOpType
ACT = mybir.ActivationFunctionType
AX = mybir.AxisListType

P = 128
T = 256
TT = T // P
D = 1024
DC = D // P
RING = 8
TILE = 1024
HG_HEADS = 8
LRU_BLOCKS = 4
PEER_HEADS = 8
NKEYS = 128
TOPK = 16
GDN_HEADS = 6
SWA_GROUPS, SWA_HEADS, SWA_DH = 3, 4, 64
SWA_CONFIGS = ((128, 1), (512, 4), (2048, 16))
DIFF_HEADS = 4
GLA_HEADS, GLA_DK = 4, 64
GLA_TAU = 16.0
GATE_RANK = 16
D_FF = 2816
FC = D_FF // P
NUM_BUCKETS, REL_MAX = 32, 2048
LRU_C = 8.0
DEPTH = 2
ALPHA = (2 * DEPTH) ** 0.25
LAM_INIT = 0.8 - 0.6 * math.exp(-0.3)
PAIR_LEVELS = 7
DIAGONAL, CROSS = PAIR_LEVELS, PAIR_LEVELS + 1
SKEW = 512
NEG = -1e30

PARAMS = [
    ("c", DC), ("norm_g", 4 * DC), ("b_ada", 2 * 6 * DC), ("hg_lb", DC), ("hg_norm_g", DC),
    ("lru_conv_w", 4 * DC), ("lru_conv_b", DC), ("lru_b_a", 2 * DC), ("lru_b_x", 2 * DC),
    ("lru_lam", 2 * DC), ("final_g", DC), ("gdn_conv_w", 4 * 18), ("gdn_norm_w", 1),
    ("gdn_dt_bias", GDN_HEADS), ("gdn_a_log", GDN_HEADS), ("diff_norm_w", 1),
    ("gla_b_gate", 2), ("gla_norm_w", 1), ("ffn_conv_w", 2 * 3 * 2 * FC),
    ("ffn_conv_b", 2 * 2 * FC), ("ln_g", 4 * DC), ("ln_b", 4 * DC),
]
CONSTS = [
    ("ident", P), ("ones", P), ("mean_d", P), ("mean_head", P), ("iota", NKEYS), ("iota16", TOPK),
    ("tri", P), ("strict", P), ("pairs", PAIR_LEVELS * P), ("eps", 2), ("zero", P),
]
SMALL = [("w_ba", DC * 2 * GDN_HEADS), ("w_gd", DC * GATE_RANK), ("w_gate", 2 * P)]


def columns(table):
    at, out = 0, {}
    for name, n in table:
        out[name] = (at, n)
        at += n
    return out, at


STREAM = [
    ("ada0", 6 * DC), ("hg_in", 5 * DC), ("hg_out", DC), ("wq0", 2 * PEER_HEADS), ("keys0", 2),
    ("experts0", 2 * NKEYS),
    ("ada1", 6 * DC), ("lru_in", 2 * DC), ("lru_gates", 8), ("lru_out", DC),
    ("wq1", 2 * PEER_HEADS), ("keys1", 2), ("experts1", 2 * NKEYS),
    ("even_in", 42), ("even_out", DC), ("up0", 2 * FC), ("down0", FC),
    ("odd_in", 24), ("odd_out", DC), ("up1", 2 * FC), ("down1", FC),
]
STREAM_AT, STREAM_USED = columns(STREAM)
STREAM_TILES = -(-STREAM_USED // RING) * RING


class Tally:

    def __init__(self):
        self.count = {}

    def up(self, sem, by=1):
        self.count[id(sem)] = self.count.get(id(sem), 0) + by
        return self.count[id(sem)]

    def value(self, sem):
        return self.count.get(id(sem), 0)


def wide(ap, *shape):
    return ap.broadcast_to(list(shape))


def over(ap, n):
    return wide(ap.unsqueeze(1), ap.shape[0], n, ap.shape[1])


def build(nc, tiles, x_in, params_in, consts_in, small_in, masks_in, lam_in, bias_in, skew, out):
    pcol, n_params = columns(PARAMS)
    ccol, n_consts = columns(CONSTS)
    scol, n_small = columns(SMALL)

    ctx = ExitStack()
    with ctx:
        def sb(name, cols, dt=F32):
            return ctx.enter_context(nc.sbuf_tensor(name, [P, cols], dt))

        sems = {}

        def sem(name):
            if name not in sems:
                sems[name] = ctx.enter_context(nc.semaphore(name))
            return sems[name]

        X = sb("X", DC * T)
        H = sb("H", DC * T)
        ring = sb("ring", RING * TILE)
        BIG = sb("BIG", 128 * T)
        par = sb("par", n_params)
        con = sb("con", n_consts)
        mod = sb("mod", 2 * 6 * DC)
        coef = sb("coef", 112)
        slots = sb("slots", 3 * T)
        onehot_a = sb("onehot_a", 2 * 4 * P)
        onehot_b = sb("onehot_b", 2 * 4 * P)
        act_v = sb("act_v", 4 * T)
        inv = sb("inv", T)
        SM = sb("SM", n_small)
        stat = sb("stat", 16)
        PA = ctx.enter_context(nc.psum_tensor("PA", [P, 4 * 512], F32))
        PB = ctx.enter_context(nc.psum_tensor("PB", [P, 4 * 512], F32))

        def p(name, i=0, n=None):
            at, size = pcol[name]
            return par[:, at + i:at + i + (size if n is None else n)]

        def c(name, i=0, n=None):
            at, size = ccol[name]
            return con[:, at + i:at + i + (size if n is None else n)]

        def big(at, n):
            return BIG[:, at:at + n]

        def chunks(ap, t=T):
            return ap.rearrange("p (c t) -> p c t", t=t)

        ident = c("ident")
        TMP = big(120 * T, DC * T)

        loaded = [sem(f"tile_loaded_{i}") for i in range(RING)]
        tile_done = sem("tile_done")
        taken = sem("product_taken")

        PRODUCTS = [("hg_in", 5 * DC), ("hg_out", DC), ("wq0", 16), ("lru_in", 16), ("lru_out", DC),
                    ("wq1", 16), ("even_in", 42), ("even_out", DC), ("up0", 2 * FC),
                    ("odd_in", 24), ("odd_out", DC), ("up1", 2 * FC)]
        product_at, _ = columns(PRODUCTS)

        def product_slot(i):
            return PB[:, (i % 4) * 512:(i % 4) * 512 + T]


        HG = []
        for d in range(2):
            HG.append(dict(chunks=DC, heads=HG_HEADS, v_made=d == 1,
                           q=big((0, 40 * T)[d], DC * T), v=big((24 * T, 8 * T)[d], DC * T),
                           logit=big((8 * T, 16 * T)[d], DC * T), k=big(48 * T, DC * T),
                           b=big(56 * T, DC * T), e=big(64 * T, DC * T), kh=big(72 * T, DC * T),
                           qh=big(80 * T, DC * T), at=big(88 * T, DC * T), ax=big(96 * T, 4 * T),
                           vt=big(100 * T, DC * T)))
        HG_G = big(32 * T, DC * T)
        HG_MIX = big(108 * T, DC * T)
        LRU = dict(xc=big(0, 8 * T), y=big(8 * T, 8 * T),
                   gate=[big((16 + 8 * i) * T, 8 * T) for i in range(4)],
                   la=big(48 * T, 8 * T), a=big(56 * T, 8 * T), m=big(64 * T, 8 * T),
                   h0=big(72 * T, 8 * T), h1=big(80 * T, 8 * T))
        EVEN = dict(q=big(0, 6 * T), k=big(6 * T, 6 * T), v=big(12 * T, 6 * T), z=big(18 * T, 6 * T),
                    qb=big(24 * T, 6 * T), kb=big(30 * T, 6 * T), vb=big(36 * T, 6 * T),
                    sq=big(42 * T, 6 * T), vt=big(48 * T, 6 * T), dt=big(54 * T, 9 * T),
                    mt=big(63 * T, 6 * T), m01=big(69 * T, 3 * T), qk0=big(72 * T, 3 * T),
                    qk01=big(75 * T, 3 * T), qk1=big(78 * T, 3 * T), n=big(81 * T, 6 * T),
                    nt=big(87 * T, 6 * T), x=big(93 * T, 6 * T), y=big(99 * T, 6 * T),
                    c=big(105 * T, 6 * T), ct=big(111 * T, 6 * T), p1=big(42 * T, 6 * T),
                    p2=big(117 * T, 6 * T), d0=big(105 * T, 3 * T), r1=big(108 * T, 3 * T),
                    d1=big(111 * T, 3 * T), ba=big(123 * T, 24), g=big(123 * T + 24, 12),
                    beta=big(123 * T + 36, 12), nbeta=big(123 * T + 48, 12),
                    gam=big(123 * T + 60, 12), t0=big(123 * T + 72, 12), t1=big(123 * T + 84, 12),
                    ea=big(123 * T + 96, 6), low=big(124 * T, PAIR_LEVELS * P),
                    mix=big(81 * T, 8 * T), vbt=big(54 * T, 6 * T), bias=big(60 * T, 8 * T),
                    neg=big(68 * T, 6 * T), prob=big(74 * T, 3 * T), probt=big(77 * T, 3 * T))
        ODD = dict(qc=big(0, 4 * T), kc=big(4 * T, 4 * T), vc=big(8 * T, 4 * T), r=big(20 * T, 4 * T),
                   gd=big(42 * T, T), g1=big(43 * T, 2 * T), g2=big(45 * T, 2 * T),
                   sq=big(47 * T, 4 * T), vct=big(51 * T, 4 * T), bias=big(55 * T, 8 * T),
                   neg=big(63 * T, 2 * T), prob=big(65 * T, 2 * T), probt=big(67 * T, T),
                   lamv=big(69 * T, T), mix=big(70 * T, 8 * T))
        GLA = dict(chunks=2, heads=GLA_HEADS, v_made=False, q=big(12 * T, 2 * T), k=big(14 * T, 2 * T),
                   v=big(16 * T, 4 * T), b=big(24 * T, 2 * T), e=big(26 * T, 2 * T),
                   kh=big(28 * T, 2 * T), qh=big(30 * T, 2 * T), at=big(32 * T, 4 * T),
                   ax=big(36 * T, 2 * T), vt=big(38 * T, 4 * T))
        REL, ONEHOT, ROWS = big(0, 512), big(512, SKEW), big(1024, 4 * SKEW)
        MASK_LOW, MASK_SWA, MASK_CAUSAL, MASK_BUCKET = 0, 7 * P, 7 * P + 6 * T, 7 * P + 8 * T
        KEY_SCORES = [big((16 + 8 * t) * T, 8 * T) for t in range(TT)]
        SPARE, CAND, CAND_SPARE, PICK = (big((32 + 8 * i) * T, 8 * T) for i in range(4))
        VAL, IDX, IDX_F = (big((64 + i) * T, T) for i in range(3))
        CVAL, CPOS, HIGH, LOW, HIGH_F, LOW_F, GATE = (big(67 * T + i * P, P) for i in range(7))
        GSUM = big(71 * T, PEER_HEADS)

        def chosen(t, j):
            return big(72 * T + (t * 3 + j) * P, P)

        block = ctx.enter_context(nc.Block())

        @block.sync
        def _(sp):
            w = Tally()
            sp.dma_start(par[:, :], params_in).then_inc(sem("params_loaded"), 16)
            sp.dma_start(X[:, :], x_in).then_inc(sem("x_loaded"), 16)
            sp.dma_start(con[:, :], consts_in).then_inc(sem("consts_loaded"), 16)
            sp.dma_start(SM[:, :], small_in).then_inc(sem("small_loaded"), 16)

            def load(s, n):
                sp.dma_start(ring[:, s * TILE:(s + 1) * TILE], tiles[n]).then_inc(loaded[s], 16)

            for s in range(RING):
                load(s, s)
            with sp.Fori(1, STREAM_TILES // RING) as it:
                for s in range(RING):
                    sp.wait_ge(tile_done, it * RING + (s - RING + 1))
                    load(s, it * RING + s)
            sp.wait_ge(sem("result_ready"), w.up(sem("result_ready")))
            sp.dma_start(out, X[:, :]).then_inc(sem("result_stored"), 16)
            sp.wait_ge(sem("result_stored"), w.up(sem("result_stored"), 16))

        @block.tensor
        def _(pe):
            w = Tally()
            mm = nc.tensor.matmul

            def tile(n, it=0):
                pe.wait_ge(loaded[n % RING], (it + (n // RING + 1)) * 16)
                return ring[:, (n % RING) * TILE:(n % RING + 1) * TILE]

            def loop(n, body, peel=0):
                full = n // RING
                if full < 2 + (peel > 0):
                    for i in range(n):
                        body(i, 0)
                    return
                for i in range(RING * peel):
                    body(i, 0)
                with pe.Fori(peel, full) as it:
                    for i in range(RING):
                        body(i, it)
                for i in range(RING * full, n):
                    body(i, 0)

            def linear(name, src):
                r0, n = STREAM_AT[name]
                q0 = product_at[name][0]

                def body(i, it):
                    wt = tile(r0 + i, it)
                    if not isinstance(it, int) or q0 + i >= 4:
                        pe.wait_ge(taken, it * RING + (q0 + i - 3))
                    for k in range(DC):
                        ins = mm(product_slot(q0 + i), wt[:, k * P:(k + 1) * P],
                                 src[:, k * T:(k + 1) * T], start=k == 0, stop=k == DC - 1)
                    ins.then_inc(tile_done, 1)

                loop(n, body, peel=1 if q0 == 0 else 0)

            def all_taken(name):
                q0, n = product_at[name]
                pe.wait_ge(taken, q0 + n)

            def ada(layer):
                r0, n = STREAM_AT[f"ada{layer}"]

                def body(i, it):
                    wt = tile(r0 + i, it)
                    for k in range(DC):
                        ins = mm(PA[:, bass.ds(it * RING + i, 1)], wt[:, k * P:(k + 1) * P],
                                 coef[:, k:k + 1], start=k == 0, stop=k == DC - 1)
                    ins.then_inc(tile_done, 1)

                loop(n, body)

            def column_sums(squares, mat, dst):
                for k in range(DC):
                    ins = mm(dst, mat, squares[:, k * T:(k + 1) * T], start=k == 0, stop=k == DC - 1)
                return ins

            def rms():
                pe.wait_ge(sem("squares_ready"), w.up(sem("squares_ready")))
                column_sums(TMP, c("mean_d"), PA[:, 0:T]).then_inc(sem("mean_square_ready"), 1)

            def layer_norm():
                pe.wait_ge(sem("x_ready"), w.up(sem("x_ready")))
                column_sums(X[:, :], c("mean_d"), PA[:, 0:T]).then_inc(sem("mean_ready"), 1)
                rms()

            def head_sums(n, src, mat, dst):
                for h in range(n):
                    ins = mm(dst[:, h * T:(h + 1) * T], mat, src[:, h * T:(h + 1) * T],
                             start=True, stop=True)
                return ins

            def decay_attention(cfg):
                nh, kh, qh = cfg["heads"], cfg["kh"], cfg["qh"]
                per = nh // cfg["chunks"]
                rows = P // per

                def operand(buf, h, ch):
                    lo = (h % per) * rows
                    at = (h // per) * T + ch * P
                    return buf[lo:lo + rows, at:at + P]

                if cfg["v_made"]:
                    pe.wait_ge(sem("decay_v_ready"), w.up(sem("decay_v_ready")))
                for h in range(nh):
                    for ch in range(TT):
                        ins = nc.tensor.transpose(PA[:, (h * TT + ch) * P:(h * TT + ch + 1) * P],
                                                  cfg["v"][:, h * T + ch * P:h * T + (ch + 1) * P], ident)
                ins.then_inc(sem("decay_vt_psum"), 1)
                for lev in range(CROSS + 1):
                    dst = (PB, PA)[lev % 2]
                    if lev == 1:
                        pe.wait_ge(sem("decay_vt_ready"), w.up(sem("decay_vt_ready")))
                    if lev >= 2:
                        pe.wait_ge(sem("decay_masked"), w.up(sem("decay_masked")))
                    if lev != DIAGONAL:
                        pe.wait_ge(sem("decay_keys_ready"), w.up(sem("decay_keys_ready")))
                    k_, q_ = (cfg["k"], cfg["q"]) if lev == DIAGONAL else (kh, qh)
                    for h in range(nh):
                        for ch in range(TT if lev != CROSS else 1):
                            at = (h % per) * 1024 + (h // per * TT + ch if lev != CROSS else h // per) * P
                            ins = mm(dst[:, at:at + P], operand(k_, h, ch),
                                     operand(q_, h, 1 if lev == CROSS else ch), start=True, stop=True)
                    ins.then_inc(sem("decay_scores"), 1)
                pe.wait_ge(sem("decay_masked"), w.up(sem("decay_masked")))
                pe.wait_ge(sem("decay_masked"), w.up(sem("decay_masked")))
                vt, at_, ax = cfg["vt"], cfg["at"], cfg["ax"]
                for h in range(nh):
                    for ch in range(TT):
                        o = PA[:, (h * TT + ch) * P:(h * TT + ch + 1) * P]
                        v_own = vt[:, (h * TT + ch) * P:(h * TT + ch + 1) * P]
                        i = (h % per) * (nh // per) + h // per
                        a_own = at_[:, (i * TT + ch) * P:(i * TT + ch + 1) * P]
                        ins = mm(o, v_own, a_own, start=True, stop=ch == 0)
                        if ch == 1:
                            ins = mm(o, vt[:, h * TT * P:(h * TT + 1) * P], ax[:, i * P:(i + 1) * P],
                                     start=False, stop=True)
                ins.then_inc(sem("decay_out"), 1)

            def peer(layer):
                linear(f"wq{layer}", H)
                all_taken(f"wq{layer}")
                QT = big(0, 16 * T)
                r0, n = STREAM_AT[f"keys{layer}"]
                for i in range(n):
                    kt = tile(r0 + i)
                    for j in range(8):
                        hp = i * 8 + j
                        for t, dst in enumerate((PA, PB)):
                            ins = mm(dst[:, hp * NKEYS:(hp + 1) * NKEYS],
                                     QT[:, hp * T + t * P:hp * T + (t + 1) * P],
                                     kt[:, j * NKEYS:(j + 1) * NKEYS], start=True, stop=True)
                    ins.then_inc(tile_done, 1)
                for t in range(TT):
                    pe.wait_ge(sem("chosen_ready"), w.up(sem("chosen_ready")))
                    for j in range(3):
                        ins = nc.tensor.transpose(PA[:, (t * 3 + j) * P:(t * 3 + j + 1) * P],
                                                  chosen(t, j), ident)
                ins.then_inc(sem("slots_psum"), 1)
                pe.wait_ge(sem("slots_ready"), w.up(sem("slots_ready")))

                g0 = layer * 64

                def group(r, it):
                    pe.wait_ge(sem("onehots_ready"), it * 4 + (g0 + r + 1))
                    if not isinstance(it, int) or g0 + r >= 4:
                        pe.wait_ge(sem("gates_copied"), it * 4 + (g0 + r - 3))
                    for j in range(4):
                        at = ((r % 2) * 4 + j) * P
                        ins = mm(PA[:, (r * 4 + j) * P:(r * 4 + j + 1) * P],
                                 onehot_a[:, at:at + P], onehot_b[:, at:at + P], start=True, stop=True)
                    ins.then_inc(sem("gates_psum"), 1)

                for r in range(4):
                    group(r, 0)
                with pe.Fori(1, 16) as it:
                    for r in range(4):
                        group(r, it)

                pe.wait_ge(sem("gates_copied"), g0 + 64)
                for b in range(4):
                    mm(PA[:, b * 512:(b + 1) * 512], c("zero", 0, P), wide(c("zero", 0, 1), P, 512),
                       start=True, stop=False, skip_group_check=True)
                r0, n = STREAM_AT[f"experts{layer}"]
                w0 = layer * NKEYS

                def up(r, i, it):
                    ut = tile(r0 + i, it)
                    for k in range(DC):
                        ins = mm(PB[:, (r % 4) * 512:(r % 4) * 512 + T], ut[:, k * P:(k + 1) * P],
                                 H[:, k * T:(k + 1) * T], start=k == 0, stop=k == DC - 1)
                    ins.then_inc(tile_done, 1)

                def down(r, i, it, last=False):
                    vt = tile(r0 + i, it)
                    pe.wait_ge(sem("gated_ready"), it * 4 + (w0 + r + 1))
                    for m in range(DC):
                        ins = mm(PA[:, m * T:(m + 1) * T], vt[:, m * P:(m + 1) * P],
                                 act_v[:, (r % 4) * T:(r % 4 + 1) * T], start=False, stop=last,
                                 skip_group_check=True)
                    ins.then_inc(tile_done, 1)

                up(0, 0, 0)
                with pe.Fori(0, NKEYS // 4 - 1) as it:
                    for r in range(4):
                        up(r + 1, 1 + 2 * r, it)
                        down(r, 2 + 2 * r, it)
                j0 = NKEYS - 4
                for r in range(4):
                    if r < 3:
                        up(r + 1, 2 * j0 + 1 + 2 * r, 0)
                    down(j0 + r, 2 * j0 + 2 + 2 * r if r < 3 else n - 1, 0, r == 3)

            def conv_ffn(i):
                linear(f"up{i}", X)
                r0, n = STREAM_AT[f"down{i}"]
                pe.wait_ge(sem("ffn_hidden_ready"), w.up(sem("ffn_hidden_ready")))
                for k in range(n):
                    wt = tile(r0 + k)
                    for m in range(DC):
                        ins = mm(PA[:, m * T:(m + 1) * T], wt[:, m * P:(m + 1) * P],
                                 big(k * T, T), start=k == 0 and m % 2 == 0, stop=k == n - 1,
                                 skip_group_check=True)
                    ins.then_inc(tile_done, 1)

            def bias_rows():
                pe.wait_ge(sem("bias_loaded"), w.up(sem("bias_loaded"), 32))
                for h in range(4):
                    ins = mm(PA[:, h * SKEW:(h + 1) * SKEW], REL[0:32, h * P:(h + 1) * P],
                             ONEHOT[0:32, :], start=True, stop=True)
                ins.then_inc(sem("bias_rows_psum"), 1)

            def even_mixer():
                linear("even_in", X)
                e = EVEN
                all_taken("even_in")
                pe.wait_ge(sem("small_loaded"), w.up(sem("small_loaded"), 16))
                for t in range(TT):
                    for k in range(DC):
                        ins = mm(PB[:, t * 512:t * 512 + 12], X[:, k * T + t * P:k * T + (t + 1) * P],
                                 SM[:, scol["w_ba"][0] + k * 12:scol["w_ba"][0] + (k + 1) * 12],
                                 start=k == 0, stop=k == DC - 1)
                ins.then_inc(sem("ba_psum"), 1)
                for i in range(2):
                    pe.wait_ge(sem("qk_squares"), w.up(sem("qk_squares")))
                    head_sums(GDN_HEADS, e["sq"], c("ones"), PA).then_inc(sem("qk_lengths"), 1)
                pe.wait_ge(sem("qk_roots"), w.up(sem("qk_roots"), 2))
                for h in range(GDN_HEADS):
                    for t in range(TT):
                        ins = nc.tensor.transpose(PA[:, (h * TT + t) * P:(h * TT + t + 1) * P],
                                                  e["v"][:, h * T + t * P:h * T + (t + 1) * P], ident)
                ins.then_inc(sem("gdn_vt_psum"), 1)
                pe.wait_ge(sem("g_ready"), w.up(sem("g_ready")))
                for t in range(TT):
                    for u in range(t + 1):
                        ins = mm(PB[:, 1024 + t * 8:1024 + t * 8 + 6],
                                 c("ones") if u < t else c("tri"), e["g"][:, u * 6:(u + 1) * 6],
                                 start=u == 0, stop=u == t)
                ins.then_inc(sem("gam_col_psum"), 1)
                for h in range(GDN_HEADS):
                    if h >= 2:
                        pe.wait_ge(sem("decay_taken"), w.up(sem("decay_taken")))
                    dst = PB[:, (h % 2) * 512:(h % 2) * 512 + T]
                    for t in range(TT):
                        for u in range(t + 1):
                            ins = mm(dst[:, t * P:(t + 1) * P],
                                     wide(e["g"][:, u * 6 + h:u * 6 + h + 1], P, P),
                                     c("ones") if u < t else c("tri"), start=u == 0, stop=u == t)
                    ins.then_inc(sem("gam_row_psum"), 1)
                pe.wait_ge(sem("decay_taken"), w.up(sem("decay_taken")))
                pe.wait_ge(sem("decay_taken"), w.up(sem("decay_taken")))
                pe.wait_ge(sem("gdn_vt_ready"), w.up(sem("gdn_vt_ready")))
                pe.wait_ge(sem("qk_normed"), w.up(sem("qk_normed")))
                for i, (a, b) in enumerate((("k", "k"), ("k", "q"))):
                    for j, (s, t) in enumerate(((0, 0), (0, 1), (1, 1))):
                        n = i * 3 + j
                        dst = (PA, PB)[n % 2]
                        if n >= 2:
                            pe.wait_ge(sem("pair_taken"), w.up(sem("pair_taken")))
                        for h in range(GDN_HEADS):
                            ins = mm(dst[:, h * P:(h + 1) * P], e[a][:, h * T + s * P:h * T + (s + 1) * P],
                                     e[b][:, h * T + t * P:h * T + (t + 1) * P], start=True, stop=True)
                        ins.then_inc(sem("pair_psum"), 1)
                pe.wait_ge(sem("pair_taken"), w.up(sem("pair_taken")))
                pe.wait_ge(sem("pair_taken"), w.up(sem("pair_taken")))
                NM = GDN_HEADS * TT

                def at(i):
                    return slice(i * P, (i + 1) * P)

                for i in range(NM):
                    ins = nc.tensor.transpose(PA[:, at(i)], e["mt"][:, at(i)], ident)
                ins.then_inc(sem("m_psum"), 1)
                pe.wait_ge(sem("n_ready"), w.up(sem("n_ready")))
                for i in range(NM):
                    ins = nc.tensor.transpose(PB[:, at(i)], e["n"][:, at(i)], ident)
                ins.then_inc(sem("nt_psum"), 1)
                for lev in range(1, PAIR_LEVELS):
                    pe.wait_ge(sem("block_ready"), w.up(sem("block_ready")))
                    for i in range(NM):
                        ins = mm(PA[:, at(i)], e["ct"][:, at(i)], e["x"][:, at(i)], start=True, stop=True)
                    ins.then_inc(sem("inv_p1"), 1)
                    for i in range(NM):
                        ins = mm(PB[:, at(i)], e["c"][:, at(i)], e["y"][:, at(i)], start=True, stop=True)
                    ins.then_inc(sem("inv_p2"), 1)
                    pe.wait_ge(sem("inv_p1_ready"), w.up(sem("inv_p1_ready")))
                    for i in range(NM):
                        ins = mm(PA[:, at(i)], e["y"][:, at(i)], e["p1"][:, at(i)], start=True, stop=True)
                    ins.then_inc(sem("inv_xpx"), 1)
                    pe.wait_ge(sem("inv_p2_ready"), w.up(sem("inv_p2_ready")))
                    for i in range(NM):
                        ins = mm(PB[:, at(i)], e["x"][:, at(i)], e["p2"][:, at(i)], start=True, stop=True)
                    ins.then_inc(sem("inv_ypy"), 1)
                pe.wait_ge(sem("inverse_ready"), w.up(sem("inverse_ready")))
                for h in range(GDN_HEADS):
                    ins = mm(PA[:, at(h)], e["y"][:, at(h * 2)], e["vt"][:, at(h * 2)], start=True, stop=True)
                ins.then_inc(sem("delta0_psum"), 1)
                pe.wait_ge(sem("delta0_ready"), w.up(sem("delta0_ready")))
                for h in range(GDN_HEADS):
                    ins = mm(PB[:, at(h)], e["m01"][:, at(h)], e["d0"][:, at(h)], start=True, stop=True)
                ins.then_inc(sem("carry_psum"), 1)
                pe.wait_ge(sem("carry_ready"), w.up(sem("carry_ready")))
                for h in range(GDN_HEADS):
                    ins = mm(PA[:, at(h)], e["y"][:, at(h * 2 + 1)], e["r1"][:, at(h)], start=True, stop=True)
                ins.then_inc(sem("delta1_psum"), 1)
                pe.wait_ge(sem("delta1_ready"), w.up(sem("delta1_ready")))
                for h in range(GDN_HEADS):
                    for t in range(TT):
                        o = PB[:, (h * TT + t) * P:(h * TT + t + 1) * P]
                        if t == 0:
                            ins = mm(o, e["d0"][:, at(h)], e["qk0"][:, at(h)], start=True, stop=True)
                        else:
                            mm(o, e["d0"][:, at(h)], e["qk01"][:, at(h)], start=True, stop=False)
                            ins = mm(o, e["d1"][:, at(h)], e["qk1"][:, at(h)], start=False, stop=True)
                ins.then_inc(sem("gdn_out_psum"), 1)
                pe.wait_ge(sem("head_squares"), w.up(sem("head_squares")))
                head_sums(GDN_HEADS, e["sq"], c("mean_head"), PA).then_inc(sem("head_means"), 1)
                pe.wait_ge(sem("head_roots"), w.up(sem("head_roots")))
                for i in range(6):
                    for t in range(TT):
                        ins = nc.tensor.transpose(PA[:, (i * TT + t) * P:(i * TT + t + 1) * P],
                                                  e["vb"][:, i * T + t * P:i * T + (t + 1) * P], ident)
                ins.then_inc(sem("swa_vt_psum"), 1)
                pe.wait_ge(sem("swa_vt_ready"), w.up(sem("swa_vt_ready")))
                attend(SWA_GROUPS * TT * P, "swa")
                pe.wait_ge(sem("gdn_done"), w.up(sem("gdn_done")))
                linear("even_out", e["mix"])

            def attend(keys, kind):
                n = 0
                for h in range(4):
                    for t in range(TT):
                        S_, W_ = PA[:, 0:1024], PA[:, 1024:2048]
                        if n >= 1:
                            pe.wait_ge(sem(kind + "_scores_taken"), w.up(sem(kind + "_scores_taken")))
                        if kind == "swa":
                            e = EVEN
                            lo = (h % 2) * SWA_DH
                            for g in range(SWA_GROUPS):
                                at = (g * 2 + h // 2) * T
                                ins = mm(S_[:, g * T:(g + 1) * T],
                                         e["qb"][lo:lo + SWA_DH, at + t * P:at + (t + 1) * P],
                                         e["kb"][lo:lo + SWA_DH, at:at + T], start=True, stop=True)
                        else:
                            e = ODD
                            for i in range(2):
                                lo = i * 64
                                ins = mm(S_[:, i * 512:i * 512 + T],
                                         e["qc"][lo:lo + 64, h * T + t * P:h * T + (t + 1) * P],
                                         e["kc"][lo:lo + 64, h * T:(h + 1) * T], start=True, stop=True)
                        ins.then_inc(sem(kind + "_scores"), 1)
                        pe.wait_ge(sem(kind + "_weights"), w.up(sem(kind + "_weights")))
                        nk = keys // P
                        for i in range(nk):
                            ins = nc.tensor.transpose(W_[:, i * P:(i + 1) * P],
                                                      e["prob"][:, i * P:(i + 1) * P], ident)
                        ins.then_inc(sem(kind + "_wt_psum"), 1)
                        pe.wait_ge(sem(kind + "_wt_ready"), w.up(sem(kind + "_wt_ready")))
                        if kind == "swa":
                            lo = (h % 2) * SWA_DH
                            o = PB[lo:lo + SWA_DH, (n % 4) * 512:(n % 4) * 512 + P]
                            for i in range(nk):
                                g, kc = i // TT, i % TT
                                vt = ((g * 2 + h // 2) * TT + kc) * P + lo
                                ins = mm(o, e["vbt"][:, vt:vt + SWA_DH], e["probt"][:, i * P:(i + 1) * P],
                                         start=i == 0, stop=i == nk - 1)
                        else:
                            o = PB[:, (n % 4) * 512:(n % 4) * 512 + P]
                            for i in range(nk):
                                ins = mm(o, e["vct"][:, (h * TT + i) * P:(h * TT + i + 1) * P],
                                         e["probt"][:, i * P:(i + 1) * P], start=i == 0, stop=i == nk - 1)
                        ins.then_inc(sem(kind + "_out_psum"), 1)
                        n += 1
                pe.wait_ge(sem(kind + "_scores_taken"), w.up(sem(kind + "_scores_taken")))
                pe.wait_ge(sem(kind + "_done"), w.up(sem(kind + "_done")))

            def odd_mixer():
                e = ODD
                linear("odd_in", X)
                all_taken("odd_in")
                for k in range(DC):
                    ins = mm(PB[0:GATE_RANK, 0:T],
                             SM[:, scol["w_gd"][0] + k * 16:scol["w_gd"][0] + (k + 1) * 16],
                             X[:, k * T:(k + 1) * T], start=k == 0, stop=k == DC - 1)
                ins.then_inc(sem("gd_psum"), 1)
                pe.wait_ge(sem("gd_ready"), w.up(sem("gd_ready")))
                for i in range(2):
                    ins = mm(PB[:, 512 + i * 512:512 + i * 512 + T],
                             SM[0:GATE_RANK, scol["w_gate"][0] + i * P:scol["w_gate"][0] + (i + 1) * P],
                             e["gd"][0:GATE_RANK, :], start=True, stop=True)
                ins.then_inc(sem("gate_psum"), 1)
                pe.wait_ge(sem("gate_taken"), w.up(sem("gate_taken")))
                decay_attention(GLA)
                pe.wait_ge(sem("head_squares"), w.up(sem("head_squares")))
                head_sums(4, e["sq"], c("mean_head"), PA).then_inc(sem("head_means"), 1)
                pe.wait_ge(sem("head_roots"), w.up(sem("head_roots")))
                for h in range(DIFF_HEADS):
                    for t in range(TT):
                        ins = nc.tensor.transpose(PA[:, (h * TT + t) * P:(h * TT + t + 1) * P],
                                                  e["vc"][:, h * T + t * P:h * T + (t + 1) * P], ident)
                ins.then_inc(sem("diff_vt_psum"), 1)
                pe.wait_ge(sem("diff_vt_ready"), w.up(sem("diff_vt_ready")))
                attend(T, "diff")
                pe.wait_ge(sem("head_squares"), w.up(sem("head_squares")))
                head_sums(4, e["sq"], c("mean_head"), PA).then_inc(sem("head_means"), 1)
                pe.wait_ge(sem("head_roots"), w.up(sem("head_roots")))
                pe.wait_ge(sem("mix_ready"), w.up(sem("mix_ready")))
                linear("odd_out", e["mix"])

            pe.wait_ge(sem("consts_loaded"), w.up(sem("consts_loaded"), 16))
            pe.wait_ge(sem("cond_ready"), w.up(sem("cond_ready")))
            ada(0)
            pe.wait_ge(sem("mod_ready"), w.up(sem("mod_ready")))
            rms()
            pe.wait_ge(sem("h_ready"), w.up(sem("h_ready")))
            linear("hg_in", H)
            all_taken("hg_in")
            decay_attention(HG[0])
            pe.wait_ge(sem("decay_out_taken"), w.up(sem("decay_out_taken")))
            decay_attention(HG[1])
            pe.wait_ge(sem("head_squares"), w.up(sem("head_squares")))
            head_sums(HG_HEADS, TMP, c("mean_head"), PA).then_inc(sem("head_means"), 1)
            pe.wait_ge(sem("head_roots"), w.up(sem("head_roots")))
            pe.wait_ge(sem("mix_ready"), w.up(sem("mix_ready")))
            linear("hg_out", HG_MIX)
            pe.wait_ge(sem("x_ready"), w.up(sem("x_ready")))
            rms()
            pe.wait_ge(sem("h_ready"), w.up(sem("h_ready")))
            peer(0)
            pe.wait_ge(sem("x_ready"), w.up(sem("x_ready")))
            ada(1)
            pe.wait_ge(sem("mod_ready"), w.up(sem("mod_ready")))
            rms()
            pe.wait_ge(sem("h_ready"), w.up(sem("h_ready")))
            linear("lru_in", H)
            all_taken("lru_in")
            r0, n = STREAM_AT["lru_gates"]
            for i in range(n):
                wt = tile(r0 + i)
                if i >= 2:
                    pe.wait_ge(sem("lru_gate_taken"), w.up(sem("lru_gate_taken")))
                for j in range(4):
                    m = (i % 2) * 4 + j
                    for k in range(2):
                        ins = mm(PA[:, (i % 2) * 1024 + j * T:(i % 2) * 1024 + (j + 1) * T],
                                 wt[:, (j * 2 + k) * P:(j * 2 + k + 1) * P],
                                 LRU["xc"][:, (2 * (m // 2) + k) * T:(2 * (m // 2) + k + 1) * T],
                                 start=k == 0, stop=k == 1)
                ins.then_inc(tile_done, 1)
            pe.wait_ge(sem("lru_gate_taken"), w.up(sem("lru_gate_taken")))
            pe.wait_ge(sem("lru_gate_taken"), w.up(sem("lru_gate_taken")))
            pe.wait_ge(sem("mix_ready"), w.up(sem("mix_ready")))
            linear("lru_out", LRU["h0"])
            pe.wait_ge(sem("x_ready"), w.up(sem("x_ready")))
            rms()
            pe.wait_ge(sem("h_ready"), w.up(sem("h_ready")))
            peer(1)
            pe.wait_ge(sem("x_ready"), w.up(sem("x_ready")))
            rms()
            pe.wait_ge(sem("x_normed"), w.up(sem("x_normed")))
            bias_rows()
            pe.wait_ge(sem("bias_rows_taken"), w.up(sem("bias_rows_taken")))
            even_mixer()
            layer_norm()
            pe.wait_ge(sem("x_normed"), w.up(sem("x_normed")))
            conv_ffn(0)
            layer_norm()
            pe.wait_ge(sem("x_normed"), w.up(sem("x_normed")))
            odd_mixer()
            layer_norm()
            pe.wait_ge(sem("x_normed"), w.up(sem("x_normed")))
            conv_ffn(1)
            layer_norm()

        @block.scalar
        def _(act):
            w = Tally()
            fn = nc.scalar.activation

            def all_taken(name):
                q0, n = product_at[name]
                act.wait_ge(taken, q0 + n)

            def evacuate(name, dst, func=ACT.Identity, first=0, last=None):
                q0, n = product_at[name]
                r0 = STREAM_AT[name][0]
                last = n if last is None else last
                if q0 + first > 0:
                    act.wait_ge(taken, q0 + first)

                def body(i, it):
                    act.wait_ge(tile_done, it * 8 + (r0 + i + 1))
                    fn(dst[:, bass.ds(it * (8 * T) + (i - first) * T, T)], product_slot(q0 + i),
                       func).then_inc(taken, 1)

                full = (last - first) // 8
                if full >= 2:
                    with act.Fori(0, full) as it:
                        for i in range(8):
                            body(first + i, it)
                else:
                    full = 0
                for i in range(first + 8 * full, last):
                    body(i, 0)

            def squares(src, dst, name):
                fn(dst, src, ACT.Square).then_inc(sem(name), 1)

            def root(layer_norm=False):
                act.wait_ge(sem("mean_square_ready"), w.up(sem("mean_square_ready")))
                fn(inv[:, :], PA[:, 0:T], ACT.Sqrt,
                   bias=c("eps", 1 if layer_norm else 0, 1)).then_inc(sem("root_ready"), 1)

            def rms():
                squares(X[:, :], TMP, "squares_ready")
                root()

            def layer_norm():
                act.wait_ge(sem("centered"), w.up(sem("centered")))
                squares(X[:, :], TMP, "squares_ready")
                root(True)

            def head_norm(o, sq, n):
                act.wait_ge(sem("heads_ready"), w.up(sem("heads_ready")))
                squares(o, sq, "head_squares")
                act.wait_ge(sem("head_means"), w.up(sem("head_means")))
                fn(sq, PA[:, 0:n * T], ACT.Sqrt, bias=c("eps", 0, 1)).then_inc(sem("head_roots"), 1)

            def decay_attention(cfg):
                n = cfg["heads"] * T
                act.wait_ge(sem("decay_vt_psum"), w.up(sem("decay_vt_psum")))
                fn(cfg["vt"], PA[:, 0:n], ACT.Identity).then_inc(sem("decay_vt_ready"), 1)
                for lev in range(CROSS + 1):
                    if lev == DIAGONAL:
                        continue
                    act.wait_ge(sem("decay_diff"), w.up(sem("decay_diff")))
                    fn(cfg["e"], cfg["e"], ACT.Abs).then_inc(sem("act_step"), 1)
                    act.wait_ge(sem("act_step"), w.up(sem("act_step")))
                    fn(cfg["e"], cfg["e"], ACT.Exp, scale=-1.0).then_inc(sem("decay_exp"), 1)

            def peer(layer):
                evacuate(f"wq{layer}", big(0, 16 * T))
                r0, n = STREAM_AT[f"keys{layer}"]
                act.wait_ge(tile_done, r0 + n)
                for t, src in enumerate((PA, PB)):
                    fn(KEY_SCORES[t], src[:, :], ACT.Identity).then_inc(sem("key_scores"), 1)
                for t in range(TT):
                    act.wait_ge(sem("gate_diff"), w.up(sem("gate_diff")))
                    fn(GATE, GATE, ACT.Exp).then_inc(sem("gate_exp"), 1)
                act.wait_ge(sem("slots_psum"), w.up(sem("slots_psum")))
                fn(slots[:, :].rearrange("p (j t c) -> p t j c", j=3, t=TT),
                   PA[:, 0:6 * P].rearrange("p (t j c) -> p t j c", j=3, t=TT),
                   ACT.Identity).then_inc(sem("slots_ready"), 1)
                g0 = layer * 64
                gates = chunks(BIG[:, :])

                def group(r, it):
                    act.wait_ge(sem("gates_psum"), it * 4 + (g0 + r + 1))
                    fn(gates[:, :, bass.ds(it * 16 + r * 4, 4)],
                       PA[:, r * 512:(r + 1) * 512].rearrange("p (t j) -> p j t", t=4),
                       ACT.Identity).then_inc(sem("gates_copied"), 1)

                with act.Fori(0, 16) as it:
                    for r in range(4):
                        group(r, it)
                r0, n = STREAM_AT[f"experts{layer}"]

                def gelu(r, i, it):
                    act.wait_ge(tile_done, it * 8 + (r0 + i + 1))
                    fn(act_v[:, r * T:(r + 1) * T], PB[:, r * 512:r * 512 + T],
                       ACT.Gelu_apprx_tanh).then_inc(sem("gelu_ready"), 1)

                for r in range(4):
                    gelu(r, max(0, 2 * r - 1), 0)
                with act.Fori(1, NKEYS // 4) as it:
                    for r in range(4):
                        gelu(r, 2 * r - 1, it)

            def conv_ffn(i):
                q0, n = product_at[f"up{i}"]
                act.wait_ge(taken, q0 + FC)
                fn(big(0, FC * T), big(0, FC * T), ACT.Silu).then_inc(sem("gate_silu"), 1)

            def attend(kind, e, dst_chunk):
                groups = 3 if kind == "swa" else 2
                for h in range(4):
                    for t in range(TT):
                        act.wait_ge(sem(kind + "_max"), w.up(sem(kind + "_max")))
                        if kind == "swa":
                            fn(e["prob"], e["prob"], ACT.Exp, bias=stat[:, 0:1],
                               accum_out=stat[:, 2:3]).then_inc(sem("swa_exp"), 1)
                        else:
                            for i in range(2):
                                fn(e["prob"][:, i * T:(i + 1) * T], e["prob"][:, i * T:(i + 1) * T],
                                   ACT.Exp, bias=stat[:, i:i + 1],
                                   accum_out=stat[:, 2 + i:3 + i]).then_inc(sem("diff_exp"), 1)
                        act.wait_ge(sem(kind + "_wt_psum"), w.up(sem(kind + "_wt_psum")))
                        nk = TT * (3 if kind == "swa" else 1)
                        fn(e["probt"], PA[:, 1024:1024 + nk * P],
                           ACT.Identity).then_inc(sem(kind + "_wt_ready"), 1)
                        act.wait_ge(sem(kind + "_out_psum"), w.up(sem(kind + "_out_psum")))
                        n = h * TT + t
                        if kind == "swa":
                            rows = slice((h % 2) * SWA_DH, (h % 2 + 1) * SWA_DH)
                            at = (6 + h // 2) * T + t * P
                        else:
                            rows, at = slice(0, P), h * T + t * P
                        ins = fn(e["mix"][rows, at:at + P], PB[rows, (n % 4) * 512:(n % 4) * 512 + P],
                                 ACT.Identity)
                        if n < 7:
                            ins.then_inc(sem("act_step"), 1)
                            act.wait_ge(sem("act_step"), w.up(sem("act_step")))
                ins.then_inc(sem(kind + "_done"), 1)

            def even_mixer():
                e = EVEN
                evacuate("even_in", big(18 * T, 24 * T), first=18)
                qkv = big(0, 18 * T)
                act.wait_ge(taken, product_at["even_in"][0] + 42)
                fn(qkv, qkv, ACT.Silu).then_inc(sem("qkv_silu"), 1)
                act.wait_ge(sem("qkv_silu"), w.up(sem("qkv_silu")))
                squares(e["q"], e["sq"], "qk_squares")
                act.wait_ge(sem("qk_lengths"), w.up(sem("qk_lengths")))
                fn(e["x"], PA[:, 0:6 * T], ACT.Sqrt, bias=c("eps", 0, 1)).then_inc(sem("qk_roots"), 1)
                act.wait_ge(sem("qk_roots"), w.up(sem("qk_roots")))
                squares(e["k"], e["sq"], "qk_squares")
                act.wait_ge(sem("qk_lengths"), w.up(sem("qk_lengths")))
                fn(e["y"], PA[:, 0:6 * T], ACT.Sqrt, bias=c("eps", 0, 1)).then_inc(sem("qk_roots"), 1)
                w.up(sem("qk_roots"))
                fn(e["z"], e["z"], ACT.Silu).then_inc(sem("gate_silu"), 1)
                act.wait_ge(sem("ba_ready"), w.up(sem("ba_ready")))
                b_ = e["ba"].rearrange("p (t n) -> p t n", t=2)
                fn(e["beta"].rearrange("p (t n) -> p t n", t=2), b_[:, :, 0:6], ACT.Sigmoid)\
                    .then_inc(sem("beta_ready"), 1)
                fn(e["ea"], p("gdn_a_log", 0, 6), ACT.Exp).then_inc(sem("a_ready"), 1)
                fn(e["t1"], e["t0"], ACT.Abs).then_inc(sem("act_step"), 1)
                act.wait_ge(sem("act_step"), w.up(sem("act_step")))
                fn(e["t1"], e["t1"], ACT.Exp, scale=-1.0).then_inc(sem("act_step"), 1)
                act.wait_ge(sem("act_step"), w.up(sem("act_step")))
                fn(e["t1"], e["t1"], ACT.Ln, bias=c("ones", 0, 1)).then_inc(sem("softplus_ln"), 1)
                act.wait_ge(sem("gdn_vt_psum"), w.up(sem("gdn_vt_psum")))
                act.wait_ge(sem("beta_ready"), w.up(sem("beta_ready")))
                for h in range(GDN_HEADS):
                    for t in range(TT):
                        i = h * TT + t
                        ins = fn(e["vt"][:, i * P:(i + 1) * P], PA[:, i * P:(i + 1) * P], ACT.Identity,
                                 scale=e["beta"][:, t * 6 + h:t * 6 + h + 1])
                ins.then_inc(sem("gdn_vt_ready"), 1)
                for h in range(GDN_HEADS):
                    act.wait_ge(sem("decay_diff_h"), w.up(sem("decay_diff_h")))
                    fn(e["dt"][:, h * 384:(h + 1) * 384], e["dt"][:, h * 384:(h + 1) * 384],
                       ACT.Exp).then_inc(sem("gdn_decay"), 1)
                act.wait_ge(sem("m_psum"), w.up(sem("m_psum")))
                for i in range(12):
                    h, t = i // 2, i % 2
                    ins = fn(e["n"][:, i * P:(i + 1) * P], PA[:, i * P:(i + 1) * P], ACT.Identity,
                             scale=e["beta"][:, t * 6 + h:t * 6 + h + 1])
                ins.then_inc(sem("n_ready"), 1)
                act.wait_ge(sem("nt_psum"), w.up(sem("nt_psum")))
                fn(e["nt"], PB[:, 0:12 * P], ACT.Identity).then_inc(sem("nt_ready"), 1)
                for lev in range(1, PAIR_LEVELS):
                    act.wait_ge(sem("inv_p1"), w.up(sem("inv_p1")))
                    fn(e["p1"], PA[:, 0:12 * P], ACT.Identity).then_inc(sem("inv_p1_ready"), 1)
                    act.wait_ge(sem("inv_p2"), w.up(sem("inv_p2")))
                    fn(e["p2"], PB[:, 0:12 * P], ACT.Identity).then_inc(sem("inv_p2_ready"), 1)
                act.wait_ge(sem("delta0_psum"), w.up(sem("delta0_psum")))
                fn(e["d0"], PA[:, 0:6 * P], ACT.Identity).then_inc(sem("delta0_ready"), 1)
                act.wait_ge(sem("delta1_psum"), w.up(sem("delta1_psum")))
                fn(e["d1"], PA[:, 0:6 * P], ACT.Identity).then_inc(sem("delta1_ready"), 1)
                act.wait_ge(sem("gdn_out_psum"), w.up(sem("gdn_out_psum")))
                fn(e["mix"][:, 0:6 * T], PB[:, 0:6 * T], ACT.Identity).then_inc(sem("heads_ready"), 1)
                head_norm(e["mix"][:, 0:6 * T], e["sq"], 6)
                act.wait_ge(sem("swa_vt_psum"), w.up(sem("swa_vt_psum")))
                fn(e["vbt"], PA[:, 0:12 * P], ACT.Identity).then_inc(sem("swa_vt_ready"), 1)
                attend("swa", e, 6)

            def odd_mixer():
                e = ODD
                evacuate("odd_in", big(0, 24 * T))
                act.wait_ge(sem("gd_psum"), w.up(sem("gd_psum")))
                fn(e["gd"][0:GATE_RANK, :], PB[0:GATE_RANK, 0:T], ACT.Identity).then_inc(sem("gd_ready"), 1)
                act.wait_ge(taken, product_at["odd_in"][0] + 24)
                fn(e["r"], e["r"], ACT.Silu).then_inc(sem("gate_silu"), 1)
                act.wait_ge(sem("gate_taken"), w.up(sem("gate_taken")))
                fn(e["g2"], e["g1"], ACT.Abs).then_inc(sem("act_step"), 1)
                act.wait_ge(sem("act_step"), w.up(sem("act_step")))
                fn(e["g2"], e["g2"], ACT.Exp, scale=-1.0).then_inc(sem("act_step"), 1)
                act.wait_ge(sem("act_step"), w.up(sem("act_step")))
                fn(e["g2"], e["g2"], ACT.Ln, bias=c("ones", 0, 1)).then_inc(sem("softplus_ln"), 1)
                decay_attention(GLA)
                head_norm(e["mix"][:, 4 * T:8 * T], e["sq"], 4)
                act.wait_ge(sem("diff_vt_psum"), w.up(sem("diff_vt_psum")))
                fn(e["vct"], PA[:, 0:8 * P], ACT.Identity).then_inc(sem("diff_vt_ready"), 1)
                act.wait_ge(sem("lam_sums"), w.up(sem("lam_sums")))
                fn(stat[:, 8:10], stat[:, 6:8], ACT.Exp).then_inc(sem("lam_exp"), 1)
                attend("diff", e, 0)
                act.wait_ge(sem("diff_done"), 1)
                squares(e["mix"][:, 0:4 * T], e["sq"], "head_squares")
                act.wait_ge(sem("head_means"), w.up(sem("head_means")))
                fn(e["sq"], PA[:, 0:4 * T], ACT.Sqrt, bias=c("eps", 0, 1)).then_inc(sem("head_roots"), 1)

            act.wait_ge(sem("params_loaded"), w.up(sem("params_loaded"), 16))
            act.wait_ge(sem("consts_loaded"), w.up(sem("consts_loaded"), 16))
            fn(coef[:, 0:DC], p("c", 0, DC), ACT.Silu).then_inc(sem("cond_ready"), 1)
            act.wait_ge(sem("lb_shifted"), w.up(sem("lb_shifted")))
            fn(coef[:, 40:48], coef[:, 40:48], ACT.Exp).then_inc(sem("lb_exp"), 1)
            act.wait_ge(sem("x_loaded"), w.up(sem("x_loaded"), 16))
            rms()
            evacuate("hg_in", big(0, 40 * T))
            all_taken("hg_in")
            fn(HG_G, HG_G, ACT.Silu).then_inc(sem("gate_silu"), 1)
            for d in range(2):
                cfg = HG[d]
                if d == 1:
                    act.wait_ge(sem("decay_out_taken"), w.up(sem("decay_out_taken")))
                logit = cfg["logit"] if d == 0 else chunks(cfg["logit"])[:, :, ::-1]
                fn(cfg["e"] if d == 0 else chunks(cfg["e"]), logit, ACT.Sigmoid)\
                    .then_inc(sem("gate_sigmoid"), 1)
                act.wait_ge(sem("gate_clamped"), w.up(sem("gate_clamped")))
                fn(cfg["e"], cfg["e"], ACT.Ln).then_inc(sem("log_gate"), 1)
                decay_attention(cfg)
            head_norm(HG_MIX, TMP, HG_HEADS)
            act.wait_ge(sem("x_ready"), w.up(sem("x_ready")))
            rms()
            peer(0)
            act.wait_ge(sem("x_ready"), w.up(sem("x_ready")))
            rms()
            evacuate("lru_in", LRU["y"], ACT.Gelu_apprx_tanh, first=8)
            act.wait_ge(sem("lam_negated"), w.up(sem("lam_negated")))
            fn(coef[:, 80:96], coef[:, 64:80], ACT.Abs).then_inc(sem("act_step"), 1)
            act.wait_ge(sem("act_step"), w.up(sem("act_step")))
            fn(coef[:, 80:96], coef[:, 80:96], ACT.Exp, scale=-1.0).then_inc(sem("act_step"), 1)
            act.wait_ge(sem("act_step"), w.up(sem("act_step")))
            fn(coef[:, 80:96], coef[:, 80:96], ACT.Ln, bias=c("ones", 0, 1)).then_inc(sem("softplus_ln"), 1)
            r0, n = STREAM_AT["lru_gates"]
            for i in range(n):
                d, kind, half = i // 4, (i // 2) % 2, i % 2
                act.wait_ge(tile_done, r0 + i + 1)
                for j in range(4):
                    m = half * 4 + j
                    ins = fn(LRU["gate"][d * 2 + kind][:, m * T:(m + 1) * T],
                             PA[:, half * 1024 + j * T:half * 1024 + (j + 1) * T], ACT.Sigmoid,
                             bias=p(("lru_b_a", "lru_b_x")[kind], d * DC + m, 1))
                ins.then_inc(sem("lru_gate_taken"), 1)
            for d in range(2):
                act.wait_ge(sem("log_a"), w.up(sem("log_a")))
                fn(LRU["a"], LRU["la"], ACT.Exp).then_inc(sem("lru_a"), 1)
                fn(LRU["m"], LRU["la"], ACT.Tanh, scale=-1.0).then_inc(sem("lru_tanh"), 1)
                act.wait_ge(sem("mult_square"), w.up(sem("mult_square")))
                fn(LRU["m"], LRU["m"], ACT.Sqrt).then_inc(sem("lru_mult"), 1)
            act.wait_ge(sem("x_ready"), w.up(sem("x_ready")))
            rms()
            peer(1)
            act.wait_ge(sem("x_ready"), w.up(sem("x_ready")))
            rms()
            act.wait_ge(sem("bias_rows_psum"), w.up(sem("bias_rows_psum")))
            fn(ROWS, PA[:, :], ACT.Identity).then_inc(sem("bias_rows_taken"), 1)
            act.wait_ge(sem("bias_rows_stored"), w.up(sem("bias_rows_stored"), 16))
            even_mixer()
            act.wait_ge(sem("x_ready"), w.up(sem("x_ready")))
            layer_norm()
            conv_ffn(0)
            act.wait_ge(sem("x_ready"), w.up(sem("x_ready")))
            layer_norm()
            odd_mixer()
            act.wait_ge(sem("x_ready"), w.up(sem("x_ready")))
            layer_norm()
            conv_ffn(1)
            act.wait_ge(sem("x_ready"), w.up(sem("x_ready")))
            layer_norm()

        @block.vector
        def _(dve):
            w = Tally()
            v = nc.vector
            tt, ts, stt = v.tensor_tensor, v.tensor_scalar, v.scalar_tensor_tensor

            def all_taken(name):
                q0, n = product_at[name]
                dve.wait_ge(taken, q0 + n)

            def loop(n, body):
                full = n // 8
                if full >= 2:
                    with dve.Fori(0, full) as it:
                        for i in range(8):
                            body(i, it)
                else:
                    full = 0
                for i in range(8 * full, n):
                    body(i, 0)

            def convolve(name, n, dst, weight, taps, shifts, bias):
                q0, r0 = product_at[name][0], STREAM_AT[name][0]
                s0, per = w.value(sem("conv_step")), len(shifts) - 1
                if q0 > 0:
                    dve.wait_ge(taken, q0)
                order = [taps.index(0)] + [i for i in range(len(taps)) if taps[i] != 0]

                def body(i, it):
                    dve.wait_ge(tile_done, it * 8 + (r0 + i + 1))
                    ps = product_slot(q0 + i)
                    for q, tap in enumerate(order):
                        sh = taps[tap]
                        wc = weight(tap)[:, bass.ds(it * 8 + i, 1)]
                        out_ = dst[:, bass.ds(it * (8 * T) + (i * T + max(0, -sh)), T - abs(sh))]
                        src = ps[:, max(0, sh):T - max(0, -sh)]
                        if q:
                            dve.wait_ge(sem("conv_step"), it * (8 * per) + (s0 + i * per + q))
                            ins = stt(out_, src, wc, out_, ALU.mult, ALU.add)
                        elif bias is None:
                            ins = ts(out_, src, wc, None, ALU.mult)
                        else:
                            ins = ts(out_, src, wc, bias[:, bass.ds(it * 8 + i, 1)], ALU.mult, ALU.add)
                        ins.then_inc(sem("conv_step") if q < per else taken, 1)

                loop(n, body)
                w.up(sem("conv_step"), n * per)

            def add_product(name, gate=None):
                q0, n = product_at[name]
                r0 = STREAM_AT[name][0]
                dve.wait_ge(taken, q0)
                for m in range(n):
                    dve.wait_ge(tile_done, r0 + m + 1)
                    add_chunk(m, product_slot(q0 + m), gate).then_inc(taken, 1)
                dve.wait_ge(taken, q0 + n)
                v.tensor_copy(stat[:, 15:16], X[:, 0:1]).then_inc(sem("x_ready"), 1)

            def add_chunk(m, src, gate):
                xm = X[:, m * T:(m + 1) * T]
                if gate is None:
                    return stt(xm, xm, ALPHA, src, ALU.mult, ALU.add)
                return stt(xm, src, gate[:, m:m + 1], xm, ALU.mult, ALU.add)

            def add_sums(stream, gate=None):
                r0, n = STREAM_AT[stream]
                dve.wait_ge(tile_done, r0 + n)
                for m in range(DC):
                    ins = add_chunk(m, PA[:, m * T:(m + 1) * T], gate)
                ins.then_inc(sem("x_ready"), 1)

            def modulation(layer, sub, part):
                at = (layer * 6 + sub * 3 + part) * DC
                return mod[:, at:at + DC]

            def gains(layer, sub):
                at = 8 + (layer * 2 + sub) * DC
                return coef[:, at:at + DC]

            def modulate(layer):
                r0, n = STREAM_AT[f"ada{layer}"]
                dve.wait_ge(tile_done, r0 + n)
                tt(mod[:, layer * 48:layer * 48 + 48], PA[:, 0:48],
                   p("b_ada", layer * 48, 48), ALU.add).then_inc(sem("dve_step"), 1)
                dve.wait_ge(sem("dve_step"), w.up(sem("dve_step")))
                for sub in range(2):
                    ins = stt(gains(layer, sub), modulation(layer, sub, 1), 1.0,
                              p("norm_g", (layer * 2 + sub) * DC, DC), ALU.add, ALU.mult)
                ins.then_inc(sem("dve_step"), 1)
                dve.wait_ge(sem("dve_step"), w.up(sem("dve_step")))
                v.tensor_copy(stat[:, 14:15], mod[:, 0:1]).then_inc(sem("mod_ready"), 1)

            def normalize(dst, gain, shift, name):
                dve.wait_ge(sem("root_ready"), w.up(sem("root_ready")))
                v.reciprocal(inv[:, :], inv[:, :]).then_inc(sem("dve_step"), 1)
                dve.wait_ge(sem("dve_step"), w.up(sem("dve_step")))
                tt(chunks(dst), chunks(X[:, :]), over(inv[:, :], DC), ALU.mult).then_inc(sem("dve_step"), 1)
                dve.wait_ge(sem("dve_step"), w.up(sem("dve_step")))
                for k in range(DC):
                    dk = dst[:, k * T:(k + 1) * T]
                    if shift is None:
                        ins = ts(dk, dk, gain[:, k:k + 1], None, ALU.mult)
                    else:
                        ins = ts(dk, dk, gain[:, k:k + 1], shift[:, k:k + 1], ALU.mult, ALU.add)
                if name == "x_normed":
                    ins.then_inc(sem("dve_step"), 1)
                    dve.wait_ge(sem("dve_step"), w.up(sem("dve_step")))
                    ins = v.tensor_copy(stat[:, 13:14], X[:, 0:1])
                ins.then_inc(sem(name), 1)

            def layer_norm(i):
                dve.wait_ge(sem("mean_ready"), w.up(sem("mean_ready")))
                tt(chunks(X[:, :]), chunks(X[:, :]), over(PA[:, 0:T], DC), ALU.subtract)\
                    .then_inc(sem("centered"), 1)
                dve.wait_ge(sem("centered"), w.up(sem("centered")))
                normalize(X[:, :], p("ln_g", i * DC, DC), p("ln_b", i * DC, DC), "x_normed")

            def head_norm(o, sq, n, gain, gate):
                dve.wait_ge(sem("head_roots"), w.up(sem("head_roots")))
                v.reciprocal(sq, sq).then_inc(sem("dve_step"), 1)
                dve.wait_ge(sem("dve_step"), w.up(sem("dve_step")))
                tt(o, o, sq, ALU.mult).then_inc(sem("dve_step"), 1)
                dve.wait_ge(sem("dve_step"), w.up(sem("dve_step")))
                if gate is not None:
                    dve.wait_ge(sem("gate_silu"), w.up(sem("gate_silu")))
                for h in range(n):
                    oh = o[:, h * T:(h + 1) * T]
                    if gate is None:
                        ins = ts(oh, oh, gain(h), 1.0 - LAM_INIT, ALU.mult, ALU.mult)
                    else:
                        ins = stt(oh, oh, gain(h), gate[:, h * T:(h + 1) * T], ALU.mult, ALU.mult)
                return ins

            def cumulate(cfg):
                for i in range(cfg["chunks"]):
                    ins = v.tensor_tensor_scan(cfg["b"][:, i * T:(i + 1) * T], wide(c("ones", 0, 1), P, T),
                                               cfg["e"][:, i * T:(i + 1) * T], 0.0, ALU.mult, ALU.add)
                ins.then_inc(sem("dve_step"), 1)
                dve.wait_ge(sem("dve_step"), w.up(sem("dve_step")))

            def decay_attention(cfg):
                b, e, k_, q_, kh, qh = (cfg[x] for x in ("b", "e", "k", "q", "kh", "qh"))
                per = cfg["heads"] // cfg["chunks"]
                nm = cfg["chunks"] * TT

                def by_rows(x, n):
                    return x.rearrange("p (r n c) -> p r n c", r=per, n=n)

                def diff(lev):
                    size = 2 << lev if lev < DIAGONAL else T
                    bv, ev = (x.rearrange("p (n l) -> p n l", l=size) for x in (b, e))
                    ref = bv[:, :, size // 2 - 1:size // 2]
                    tt(ev, bv, wide(ref, P, b.shape[1] // size, size), ALU.subtract)\
                        .then_inc(sem("decay_diff"), 1)

                v.memset(cfg["at"], 0.0).then_inc(sem("dve_step"), 1)
                dve.wait_ge(sem("dve_step"), w.up(sem("dve_step")))
                diff(0)
                for lev in range(CROSS + 1):
                    if lev != DIAGONAL:
                        dve.wait_ge(sem("decay_exp"), w.up(sem("decay_exp")))
                        tt(kh, k_, e, ALU.mult)
                        tt(qh, q_, e, ALU.mult).then_inc(sem("decay_keys_ready"), 1)
                        dve.wait_ge(sem("decay_keys_ready"), w.up(sem("decay_keys_ready")))
                        nxt = CROSS if lev == DIAGONAL - 1 else lev + 1
                        if lev < DIAGONAL:
                            diff(nxt)
                    dve.wait_ge(sem("decay_scores"), w.up(sem("decay_scores")))
                    src = (PB, PA)[lev % 2]
                    if lev == CROSS:
                        n = cfg["chunks"]
                        got = by_rows(src[:, :], 2048 // per // P)[:, :, 0:n, :]
                        v.tensor_copy(by_rows(cfg["ax"], n), got).then_inc(sem("decay_masked"), 1)
                    else:
                        mask = ident if lev == DIAGONAL else c("pairs", lev * P, P)
                        got = by_rows(src[:, :], 2048 // per // P)[:, :, 0:nm, :]
                        v.copy_predicated(by_rows(cfg["at"], nm),
                                          wide(mask.unsqueeze(1).unsqueeze(1), P, per, nm, P).bitcast(U32),
                                          got).then_inc(sem("decay_masked"), 1)
                    dve.wait_ge(sem("decay_masked"), w.up(sem("decay_masked")))
                dve.wait_ge(sem("decay_out"), w.up(sem("decay_out")))

            def top16(scores, spare, n, width, val, idx):
                def row(a, i):
                    return a[:, i * width:(i + 1) * width]
                for half in range(2):
                    src = spare if half else scores
                    for i in range(n):
                        ins = v.max(val[:, i * 16 + half * 8:i * 16 + half * 8 + 8], row(src, i))
                    ins.then_inc(sem("dve_step"), 1)
                    dve.wait_ge(sem("dve_step"), w.up(sem("dve_step")))
                    for i in range(n):
                        at = slice(i * 16 + half * 8, i * 16 + half * 8 + 8)
                        ins = v.max_index(idx[:, at], val[:, at], row(src, i))
                        if not half:
                            ins = v.match_replace(row(spare, i), val[:, at], row(src, i), -3e38)
                    ins.then_inc(sem("dve_step"), 1)
                    dve.wait_ge(sem("dve_step"), w.up(sem("dve_step")))

            def peer(layer):
                nh, hk = PEER_HEADS, PEER_HEADS * TOPK
                idx, cpos, high, low = (x.bitcast(U32) for x in (IDX, CPOS, HIGH, LOW))
                dve.wait_ge(sem("key_scores"), w.up(sem("key_scores"), TT))
                for t in range(TT):
                    top16(KEY_SCORES[t], SPARE, 2 * nh, NKEYS, VAL, idx)
                    v.tensor_copy(IDX_F, idx).then_inc(sem("dve_step"), 1)
                    dve.wait_ge(sem("dve_step"), w.up(sem("dve_step")))
                    s = VAL.rearrange("p (h s a) -> p h s a", s=2, a=TOPK)
                    tt(CAND.rearrange("p (h a b) -> p h a b", a=TOPK, b=TOPK),
                       wide(s[:, :, 0, :].unsqueeze(3), P, nh, TOPK, TOPK),
                       wide(s[:, :, 1, :].unsqueeze(2), P, nh, TOPK, TOPK), ALU.add).then_inc(sem("dve_step"), 1)
                    dve.wait_ge(sem("dve_step"), w.up(sem("dve_step")))
                    top16(CAND, CAND_SPARE, nh, TOPK * TOPK, CVAL, cpos)
                    v.tensor_scalar(high, cpos, 4, None, ALU.logical_shift_right)
                    v.tensor_scalar(low, cpos, 15, None, ALU.bitwise_and).then_inc(sem("dve_step"), 1)
                    dve.wait_ge(sem("dve_step"), w.up(sem("dve_step")))
                    v.tensor_copy(HIGH_F, high)
                    v.tensor_copy(LOW_F, low).then_inc(sem("dve_step"), 1)
                    dve.wait_ge(sem("dve_step"), w.up(sem("dve_step")))
                    ids = IDX_F.rearrange("p (h s a) -> p h s a", s=2, a=TOPK)
                    for side, rank in enumerate((HIGH_F, LOW_F)):
                        pick = PICK.rearrange("p (n a) -> p n a", a=TOPK)
                        tt(pick, wide(rank.unsqueeze(2), P, hk, TOPK), over(c("iota16"), hk),
                           ALU.is_equal).then_inc(sem("dve_step"), 1)
                        dve.wait_ge(sem("dve_step"), w.up(sem("dve_step")))
                        pick4 = PICK.rearrange("p (h k a) -> p h k a", k=TOPK, a=TOPK)
                        tt(pick4, pick4, wide(ids[:, :, side, :].unsqueeze(2), P, nh, TOPK, TOPK),
                           ALU.mult).then_inc(sem("dve_step"), 1)
                        dve.wait_ge(sem("dve_step"), w.up(sem("dve_step")))
                        v.tensor_reduce(chosen(t, side), pick, AX.X, ALU.add).then_inc(sem("dve_step"), 1)
                        dve.wait_ge(sem("dve_step"), w.up(sem("dve_step")))
                    cv = CVAL.rearrange("p (h k) -> p h k", k=TOPK)
                    gt = GATE.rearrange("p (h k) -> p h k", k=TOPK)
                    tt(gt, cv, wide(cv[:, :, 0:1], P, nh, TOPK), ALU.subtract).then_inc(sem("gate_diff"), 1)
                    dve.wait_ge(sem("gate_exp"), w.up(sem("gate_exp")))
                    v.tensor_reduce(GSUM, gt, AX.X, ALU.add).then_inc(sem("dve_step"), 1)
                    dve.wait_ge(sem("dve_step"), w.up(sem("dve_step")))
                    v.reciprocal(GSUM, GSUM).then_inc(sem("dve_step"), 1)
                    dve.wait_ge(sem("dve_step"), w.up(sem("dve_step")))
                    tt(chosen(t, 2).rearrange("p (h k) -> p h k", k=TOPK), gt,
                       wide(GSUM.unsqueeze(2), P, nh, TOPK), ALU.mult).then_inc(sem("chosen_ready"), 1)
                dve.wait_ge(sem("slots_ready"), w.up(sem("slots_ready")))
                g0 = layer * 64

                def group(r, it):
                    if not isinstance(it, int) or g0 + r >= 2:
                        dve.wait_ge(sem("gates_psum"), it * 4 + (g0 + r - 1))
                    for j in range(4):
                        at = ((r % 2) * 4 + j) * P
                        tok = it * 16 + (r * 4 + j)
                        ts(onehot_a[:, at:at + P], c("iota"), slots[:, bass.ds(tok, 1)],
                           slots[:, bass.ds(tok + 2 * T, 1)], ALU.is_equal, ALU.mult)
                        ins = ts(onehot_b[:, at:at + P], c("iota"), slots[:, bass.ds(tok + T, 1)],
                                 None, ALU.is_equal)
                    ins.then_inc(sem("onehots_ready"), 1)

                for r in range(4):
                    group(r, 0)
                with dve.Fori(1, 16) as it:
                    for r in range(4):
                        group(r, it)
                w0 = layer * NKEYS

                def gated(r, it):
                    dve.wait_ge(sem("gelu_ready"), it * 4 + (w0 + r + 1))
                    a = act_v[:, r * T:(r + 1) * T]
                    tt(a, a, BIG[:, bass.ds(it * (4 * T) + r * T, T)], ALU.mult)\
                        .then_inc(sem("gated_ready"), 1)

                with dve.Fori(0, NKEYS // 4) as it:
                    for r in range(4):
                        gated(r, it)
                add_sums(f"experts{layer}", modulation(layer, 1, 2))

            def conv_ffn(i):
                wt = [p("ffn_conv_w", i * 132 + tap * 44, 44) for tap in range(3)]
                convolve(f"up{i}", 2 * FC, BIG[:, :], lambda tap: wt[tap], [-2, -1, 0], [0] * 3,
                         p("ffn_conv_b", i * 44, 44))
                all_taken(f"up{i}")
                dve.wait_ge(sem("gate_silu"), w.up(sem("gate_silu")))
                tt(big(0, FC * T), big(0, FC * T), big(FC * T, FC * T), ALU.mult)\
                    .then_inc(sem("ffn_hidden_ready"), 1)
                add_sums(f"down{i}")

            def attend(kind, e):
                groups = 3 if kind == "swa" else 2
                pr = chunks(e["prob"])
                for h in range(4):
                    for t in range(TT):
                        dve.wait_ge(sem(kind + "_scores"), w.up(sem(kind + "_scores")))
                        bias = over(e["bias"][:, (t * 4 + h) * T:(t * 4 + h + 1) * T], groups)
                        src = chunks(PA[:, 0:3 * T]) if kind == "swa" else chunks(PA[:, 0:1024], 512)[:, :, 0:T]
                        stt(pr, src, SWA_DH ** -0.5, bias, ALU.mult, ALU.add)\
                            .then_inc(sem(kind + "_scores_taken"), 1)
                        dve.wait_ge(sem(kind + "_scores_taken"), w.up(sem(kind + "_scores_taken")))
                        if kind == "swa":
                            tt(e["prob"], e["prob"], e["neg"][:, t * 3 * T:(t + 1) * 3 * T], ALU.add).then_inc(sem("dve_step"), 1)
                            dve.wait_ge(sem("dve_step"), w.up(sem("dve_step")))
                            v.reduce_max(stat[:, 0:1], e["prob"], AX.X).then_inc(sem("dve_step"), 1)
                            dve.wait_ge(sem("dve_step"), w.up(sem("dve_step")))
                            n = 1
                        else:
                            tt(pr, pr, over(e["neg"][:, t * T:(t + 1) * T], 2), ALU.add).then_inc(sem("dve_step"), 1)
                            dve.wait_ge(sem("dve_step"), w.up(sem("dve_step")))
                            v.reduce_max(stat[:, 0:2], pr, AX.X).then_inc(sem("dve_step"), 1)
                            dve.wait_ge(sem("dve_step"), w.up(sem("dve_step")))
                            n = 2
                        ts(stat[:, 0:n], stat[:, 0:n], -1.0, None, ALU.mult).then_inc(sem(kind + "_max"), 1)
                        dve.wait_ge(sem(kind + "_exp"), w.up(sem(kind + "_exp"), n))
                        v.reciprocal(stat[:, 2:2 + n], stat[:, 2:2 + n]).then_inc(sem("dve_step"), 1)
                        dve.wait_ge(sem("dve_step"), w.up(sem("dve_step")))
                        if kind == "swa":
                            ts(e["prob"], e["prob"], stat[:, 2:3], None, ALU.mult)\
                                .then_inc(sem("swa_weights"), 1)
                        else:
                            tt(stat[:, 3:4], stat[:, 3:4], stat[:, 4:5], ALU.mult).then_inc(sem("dve_step"), 1)
                            dve.wait_ge(sem("dve_step"), w.up(sem("dve_step")))
                            ts(pr[:, 0, :], pr[:, 0, :], stat[:, 2:3], None, ALU.mult).then_inc(sem("dve_step"), 1)
                            dve.wait_ge(sem("dve_step"), w.up(sem("dve_step")))
                            stt(pr[:, 0, :], pr[:, 1, :], stat[:, 3:4], pr[:, 0, :], ALU.mult, ALU.add)\
                                .then_inc(sem("diff_weights"), 1)

            def even_mixer():
                e = EVEN
                dve.wait_ge(sem("bias_rows_stored"), w.up(sem("bias_rows_stored"), 16))
                convolve("even_in", 18, BIG[:, :],
                         lambda tap: p("gdn_conv_w", tap * 18, 18), [-3, -2, -1, 0], [0] * 4, None)
                dve.wait_ge(sem("ba_psum"), w.up(sem("ba_psum")))
                for t in range(TT):
                    ins = v.tensor_copy(e["ba"][:, t * 12:(t + 1) * 12], PB[:, t * 512:t * 512 + 12])
                ins.then_inc(sem("dve_step"), 1)
                dve.wait_ge(sem("dve_step"), w.up(sem("dve_step")))
                ba = e["ba"].rearrange("p (t n) -> p t n", t=2)
                tt(e["t0"].rearrange("p (t n) -> p t n", t=2), ba[:, :, 6:12],
                   over(p("gdn_dt_bias", 0, 6), TT), ALU.add).then_inc(sem("ba_ready"), 1)
                dve.wait_ge(sem("ba_ready"), w.up(sem("ba_ready")))
                for i, (x, y) in enumerate((("q", "x"), ("k", "y"))):
                    dve.wait_ge(sem("qk_roots"), w.up(sem("qk_roots")))
                    v.reciprocal(e[y], e[y]).then_inc(sem("dve_step"), 1)
                    dve.wait_ge(sem("dve_step"), w.up(sem("dve_step")))
                    if i == 0:
                        ins = stt(e["q"], e["q"], float(P) ** -0.5, e[y], ALU.mult, ALU.mult)
                        ins.then_inc(sem("dve_step"), 1)
                        dve.wait_ge(sem("dve_step"), w.up(sem("dve_step")))
                    else:
                        tt(e["k"], e["k"], e[y], ALU.mult).then_inc(sem("qk_normed"), 1)
                        dve.wait_ge(sem("qk_normed"), w.up(sem("qk_normed")))
                dve.wait_ge(sem("softplus_ln"), w.up(sem("softplus_ln")))
                stt(e["t0"], e["t0"], 0.0, e["t1"], ALU.max, ALU.add).then_inc(sem("dve_step"), 1)
                dve.wait_ge(sem("dve_step"), w.up(sem("dve_step")))
                dve.wait_ge(sem("a_ready"), w.up(sem("a_ready")))
                g2 = e["g"].rearrange("p (t n) -> p t n", t=2)
                stt(g2, e["t0"].rearrange("p (t n) -> p t n", t=2), -1.0, over(e["ea"], 2),
                    ALU.mult, ALU.mult).then_inc(sem("dve_step"), 1)
                dve.wait_ge(sem("dve_step"), w.up(sem("dve_step")))
                dve.wait_ge(sem("beta_ready"), w.up(sem("beta_ready")))
                ts(e["nbeta"], e["beta"], -1.0, None, ALU.mult).then_inc(sem("g_ready"), 1)
                dve.wait_ge(sem("g_ready"), w.up(sem("g_ready")))
                dve.wait_ge(sem("gam_col_psum"), w.up(sem("gam_col_psum")))
                for t in range(TT):
                    ins = v.tensor_copy(e["gam"][:, t * 6:t * 6 + 6], PB[:, 1024 + t * 8:1024 + t * 8 + 6])
                ins.then_inc(sem("dve_step"), 1)
                dve.wait_ge(sem("dve_step"), w.up(sem("dve_step")))
                for h in range(GDN_HEADS):
                    dve.wait_ge(sem("gam_row_psum"), w.up(sem("gam_row_psum")))
                    src, dt = PB[:, (h % 2) * 512:(h % 2) * 512 + T], e["dt"][:, h * 384:(h + 1) * 384]
                    ts(dt[:, 0:T], src, e["gam"][:, h:h + 1], 0.0, ALU.subtract, ALU.min)
                    ts(dt[:, T:T + P], src[:, P:T], e["gam"][:, 6 + h:7 + h], 0.0, ALU.subtract, ALU.min)\
                        .then_inc(sem("decay_taken"), 1)
                    dve.wait_ge(sem("decay_taken"), w.up(sem("decay_taken")))
                    v.tensor_copy(stat[:, 12:13], dt[:, 0:1]).then_inc(sem("decay_diff_h"), 1)
                dve.wait_ge(sem("gdn_decay"), w.up(sem("gdn_decay"), GDN_HEADS))
                dts = e["dt"].rearrange("p (h c) -> p h c", h=GDN_HEADS)
                up_incl = over(c("tri"), GDN_HEADS)
                mt = e["mt"].rearrange("p (h t c) -> p h t c", t=TT, c=P)
                for i in range(2):
                    for j in range(3):
                        n = i * 3 + j
                        dve.wait_ge(sem("pair_psum"), w.up(sem("pair_psum")))
                        src = chunks((PA, PB)[n % 2][:, 0:6 * P], P)
                        dcy = dts[:, :, j * P:(j + 1) * P]
                        if i == 0:
                            dst = chunks(e["m01"], P) if j == 1 else mt[:, :, 0 if j == 0 else 1, :]
                        else:
                            dst = chunks((e["qk0"], e["qk01"], e["qk1"])[j], P)
                        ins = tt(dst, src, dcy, ALU.mult)
                        if j != 1:
                            ins.then_inc(sem("dve_step"), 1)
                            dve.wait_ge(sem("dve_step"), w.up(sem("dve_step")))
                            ins = tt(dst, dst, up_incl, ALU.mult)
                            if i == 0:
                                ins.then_inc(sem("dve_step"), 1)
                                dve.wait_ge(sem("dve_step"), w.up(sem("dve_step")))
                                ins = tt(dst, dst, over(c("strict"), GDN_HEADS), ALU.mult)
                        ins.then_inc(sem("pair_taken"), 1)
                dve.wait_ge(sem("pair_taken"), w.up(sem("pair_taken"), 6))
                n3, nt3, x3, y3, c3, ct3 = (chunks(e[k], P) for k in ("n", "nt", "x", "y", "c", "ct"))
                dve.wait_ge(sem("low_masks_loaded"), w.up(sem("low_masks_loaded"), 16))
                dve.wait_ge(sem("n_ready"), w.up(sem("n_ready")))
                dve.wait_ge(sem("nt_ready"), w.up(sem("nt_ready")))

                def blocks(lev):
                    tt(c3, n3, over(e["low"][:, lev * P:(lev + 1) * P], 12), ALU.mult)
                    return tt(ct3, nt3, over(c("pairs", lev * P, P), 12), ALU.mult)

                blocks(0).then_inc(sem("dve_step"), 1)
                dve.wait_ge(sem("dve_step"), w.up(sem("dve_step")))
                tt(x3, over(ident, 12), c3, ALU.subtract)
                tt(y3, over(ident, 12), ct3, ALU.subtract).then_inc(sem("dve_step"), 1)
                dve.wait_ge(sem("dve_step"), w.up(sem("dve_step")))
                for lev in range(1, PAIR_LEVELS):
                    blocks(lev).then_inc(sem("block_ready"), 1)
                    dve.wait_ge(sem("block_ready"), w.up(sem("block_ready")))
                    dve.wait_ge(sem("inv_xpx"), w.up(sem("inv_xpx")))
                    dve.wait_ge(sem("inv_ypy"), w.up(sem("inv_ypy")))
                    tt(e["x"], e["x"], PA[:, 0:12 * P], ALU.subtract)
                    ins = tt(e["y"], e["y"], PB[:, 0:12 * P], ALU.subtract)
                    if lev < PAIR_LEVELS - 1:
                        ins.then_inc(sem("dve_step"), 1)
                        dve.wait_ge(sem("dve_step"), w.up(sem("dve_step")))
                ins.then_inc(sem("inverse_ready"), 1)
                dve.wait_ge(sem("carry_psum"), w.up(sem("carry_psum")))
                vt = e["vt"].rearrange("p (h t c) -> p h t c", t=TT, c=P)
                for h in range(GDN_HEADS):
                    ins = stt(e["r1"][:, h * P:(h + 1) * P], PB[:, h * P:(h + 1) * P],
                              e["nbeta"][:, 6 + h:7 + h], vt[:, h, 1, :], ALU.mult, ALU.add)
                ins.then_inc(sem("carry_ready"), 1)
                head_norm(e["mix"][:, 0:6 * T], e["sq"], 6, lambda h: p("gdn_norm_w"), e["z"])\
                    .then_inc(sem("gdn_done"), 1)
                dve.wait_ge(sem("attention_tables_loaded"), w.up(sem("attention_tables_loaded"), 48))
                attend("swa", e)
                dve.wait_ge(sem("swa_done"), w.up(sem("swa_done")))
                add_product("even_out")

            def odd_mixer():
                e = ODD
                dve.wait_ge(sem("gate_psum"), w.up(sem("gate_psum")))
                for i in range(2):
                    ins = ts(e["g1"][:, i * T:(i + 1) * T], PB[:, 512 + i * 512:512 + i * 512 + T],
                             p("gla_b_gate", i, 1), None, ALU.add)
                ins.then_inc(sem("gate_taken"), 1)
                dve.wait_ge(sem("gate_taken"), w.up(sem("gate_taken")))
                all_taken("odd_in")
                dve.wait_ge(sem("softplus_ln"), w.up(sem("softplus_ln")))
                stt(e["g1"], e["g1"], 0.0, e["g2"], ALU.min, ALU.subtract).then_inc(sem("dve_step"), 1)
                dve.wait_ge(sem("dve_step"), w.up(sem("dve_step")))
                ts(GLA["e"], e["g1"], 1.0 / GLA_TAU, None, ALU.mult)
                ts(GLA["q"], GLA["q"], GLA_DK ** -0.5, None, ALU.mult).then_inc(sem("dve_step"), 1)
                dve.wait_ge(sem("dve_step"), w.up(sem("dve_step")))
                cumulate(GLA)
                decay_attention(GLA)
                o = e["mix"][:, 4 * T:8 * T]
                v.tensor_copy(o, PA[:, 0:4 * T]).then_inc(sem("heads_ready"), 1)
                dve.wait_ge(sem("heads_ready"), w.up(sem("heads_ready")))
                head_norm(o, e["sq"], 4, lambda h: p("gla_norm_w"), e["r"]).then_inc(sem("dve_step"), 1)
                dve.wait_ge(sem("dve_step"), w.up(sem("dve_step")))
                dve.wait_ge(sem("attention_tables_loaded"), w.up(sem("attention_tables_loaded"), 64))
                lv = e["lamv"].rearrange("p (a b c) -> p a b c", a=2, b=2)
                tt(lv[:, :, 0, :], lv[:, :, 0, :], lv[:, :, 1, :], ALU.mult).then_inc(sem("dve_step"), 1)
                dve.wait_ge(sem("dve_step"), w.up(sem("dve_step")))
                v.tensor_reduce(stat[:, 6:8], lv[:, :, 0, :], AX.X, ALU.add).then_inc(sem("lam_sums"), 1)
                dve.wait_ge(sem("lam_exp"), w.up(sem("lam_exp")))
                tt(stat[:, 4:5], stat[:, 9:10], stat[:, 8:9], ALU.subtract).then_inc(sem("dve_step"), 1)
                dve.wait_ge(sem("dve_step"), w.up(sem("dve_step")))
                ts(stat[:, 4:5], stat[:, 4:5], -LAM_INIT, None, ALU.add).then_inc(sem("dve_step"), 1)
                dve.wait_ge(sem("dve_step"), w.up(sem("dve_step")))
                attend("diff", e)
                head_norm(e["mix"][:, 0:4 * T], e["sq"], 4, lambda h: p("diff_norm_w"), None).then_inc(sem("dve_step"), 1)
                dve.wait_ge(sem("dve_step"), w.up(sem("dve_step")))
                v.tensor_copy(stat[:, 11:12], e["mix"][:, 0:1]).then_inc(sem("mix_ready"), 1)
                add_product("odd_out")

            dve.wait_ge(sem("params_loaded"), w.up(sem("params_loaded"), 16))
            dve.wait_ge(sem("consts_loaded"), w.up(sem("consts_loaded"), 16))
            lb, om = coef[:, 40:48], coef[:, 48:56]
            tt(lb, p("hg_lb"), p("hg_lb"), ALU.subtract).then_inc(sem("lb_shifted"), 1)
            dve.wait_ge(sem("lb_exp"), w.up(sem("lb_exp")))
            v.reciprocal(om, lb).then_inc(sem("dve_step"), 1)
            dve.wait_ge(sem("dve_step"), w.up(sem("dve_step")))
            tt(lb, lb, om, ALU.mult).then_inc(sem("dve_step"), 1)
            dve.wait_ge(sem("dve_step"), w.up(sem("dve_step")))
            tt(lb, lb, lb, ALU.subtract).then_inc(sem("dve_step"), 1)
            dve.wait_ge(sem("dve_step"), w.up(sem("dve_step")))
            ts(om, lb, -1.0, 1.0, ALU.mult, ALU.add).then_inc(sem("dve_step"), 1)
            dve.wait_ge(sem("dve_step"), w.up(sem("dve_step")))
            modulate(0)
            dve.wait_ge(sem("x_loaded"), w.up(sem("x_loaded"), 16))
            normalize(H[:, :], gains(0, 0), modulation(0, 0, 0), "h_ready")
            all_taken("hg_in")
            for d in range(2):
                cfg = HG[d]
                if d == 1:
                    v.tensor_copy(chunks(cfg["q"]), chunks(HG[0]["q"])[:, :, ::-1])
                dve.wait_ge(sem("gate_sigmoid"), w.up(sem("gate_sigmoid")))
                if d == 1:
                    v.tensor_copy(chunks(cfg["v"]), chunks(HG[0]["v"])[:, :, ::-1])\
                        .then_inc(sem("decay_v_ready"), 1)
                for m in range(DC):
                    s_ = slice(m * T, (m + 1) * T)
                    ins = ts(cfg["k"][:, s_], cfg["e"][:, s_], om[:, m:m + 1], lb[:, m:m + 1],
                             ALU.mult, ALU.add)
                ins.then_inc(sem("dve_step"), 1)
                dve.wait_ge(sem("dve_step"), w.up(sem("dve_step")))
                ts(cfg["e"], cfg["k"], 2.0 ** -63, None, ALU.max).then_inc(sem("gate_clamped"), 1)
                ts(cfg["k"], cfg["k"], -1.0, 1.0, ALU.mult, ALU.add)
                dve.wait_ge(sem("log_gate"), w.up(sem("log_gate")))
                cumulate(cfg)
                decay_attention(cfg)
                if d == 0:
                    v.tensor_copy(HG_MIX, PA[:, :]).then_inc(sem("decay_out_taken"), 1)
                    dve.wait_ge(sem("decay_out_taken"), w.up(sem("decay_out_taken")))
                else:
                    tt(chunks(HG_MIX), chunks(HG_MIX), chunks(PA[:, :])[:, :, ::-1], ALU.add)\
                        .then_inc(sem("heads_ready"), 1)
                    dve.wait_ge(sem("heads_ready"), w.up(sem("heads_ready")))
            head_norm(HG_MIX, TMP, HG_HEADS, lambda h: p("hg_norm_g", h, 1), HG_G)\
                .then_inc(sem("mix_ready"), 1)
            add_product("hg_out", modulation(0, 0, 2))
            normalize(H[:, :], gains(0, 1), modulation(0, 1, 0), "h_ready")
            peer(0)
            modulate(1)
            normalize(H[:, :], gains(1, 0), modulation(1, 0, 0), "h_ready")
            nlam, ln1, rate = coef[:, 64:80], coef[:, 80:96], coef[:, 96:112]
            ts(nlam, p("lru_lam"), -1.0, None, ALU.mult).then_inc(sem("lam_negated"), 1)
            convolve("lru_in", DC, LRU["xc"], lambda tap: p("lru_conv_w", tap * DC, DC),
                     [-2, -1, 0, 1], [0] * 4, p("lru_conv_b"))
            dve.wait_ge(sem("lam_negated"), w.up(sem("lam_negated")))
            dve.wait_ge(sem("softplus_ln"), w.up(sem("softplus_ln")))
            stt(rate, nlam, 0.0, ln1, ALU.max, ALU.add).then_inc(sem("dve_step"), 1)
            dve.wait_ge(sem("dve_step"), w.up(sem("dve_step")))
            ts(rate, rate, -LRU_C, None, ALU.mult).then_inc(sem("dve_step"), 1)
            dve.wait_ge(sem("dve_step"), w.up(sem("dve_step")))
            dve.wait_ge(sem("lru_gate_taken"), w.up(sem("lru_gate_taken"), 8))
            all_taken("lru_in")
            for d in range(2):
                la, a, m_, h_ = LRU["la"], LRU["a"], LRU["m"], (LRU["h0"], LRU["h1"])[d]
                for m in range(DC):
                    s_ = slice(m * T, (m + 1) * T)
                    ins = ts(la[:, s_], LRU["gate"][2 * d][:, s_], rate[:, d * DC + m:d * DC + m + 1],
                             None, ALU.mult)
                ins.then_inc(sem("log_a"), 1)
                dve.wait_ge(sem("lru_a"), w.up(sem("lru_a")))
                dve.wait_ge(sem("lru_tanh"), w.up(sem("lru_tanh")))
                tt(la, a, a, ALU.mult).then_inc(sem("dve_step"), 1)
                dve.wait_ge(sem("dve_step"), w.up(sem("dve_step")))
                stt(m_, la, 1.0, m_, ALU.add, ALU.mult).then_inc(sem("mult_square"), 1)
                dve.wait_ge(sem("mult_square"), w.up(sem("mult_square")))
                tt(la, LRU["gate"][2 * d + 1], LRU["xc"], ALU.mult).then_inc(sem("dve_step"), 1)
                dve.wait_ge(sem("dve_step"), w.up(sem("dve_step")))
                dve.wait_ge(sem("lru_mult"), w.up(sem("lru_mult")))
                tt(m_, m_, la, ALU.mult).then_inc(sem("dve_step"), 1)
                dve.wait_ge(sem("dve_step"), w.up(sem("dve_step")))
                for m in range(DC):
                    s_ = slice(m * T, (m + 1) * T)
                    a1, u1, h1 = a[:, s_], m_[:, s_], h_[:, s_]
                    if d:
                        a1, u1, h1 = a1[:, ::-1], u1[:, ::-1], h1[:, ::-1]
                    ins = v.tensor_tensor_scan(h1, a1, u1, 0.0, ALU.mult, ALU.add)
                ins.then_inc(sem("dve_step"), 1)
                dve.wait_ge(sem("dve_step"), w.up(sem("dve_step")))
            tt(LRU["h0"], LRU["h0"], LRU["h1"], ALU.add).then_inc(sem("dve_step"), 1)
            dve.wait_ge(sem("dve_step"), w.up(sem("dve_step")))
            tt(LRU["h0"], LRU["h0"], LRU["y"], ALU.mult).then_inc(sem("mix_ready"), 1)
            add_product("lru_out", modulation(1, 0, 2))
            normalize(H[:, :], gains(1, 1), modulation(1, 1, 0), "h_ready")
            peer(1)
            dve.wait_ge(sem("x_ready"), w.up(sem("x_ready"), 4))
            normalize(X[:, :], p("final_g"), None, "x_normed")
            dve.wait_ge(sem("x_normed"), w.up(sem("x_normed")))
            even_mixer()
            layer_norm(0)
            dve.wait_ge(sem("x_normed"), w.up(sem("x_normed")))
            conv_ffn(0)
            layer_norm(1)
            dve.wait_ge(sem("x_normed"), w.up(sem("x_normed")))
            odd_mixer()
            layer_norm(2)
            dve.wait_ge(sem("x_normed"), w.up(sem("x_normed")))
            conv_ffn(1)
            layer_norm(3)
            dve.wait_ge(sem("x_normed"), w.up(sem("x_normed")))
            v.tensor_copy(stat[:, 12:13], X[:, 0:1]).then_inc(sem("result_ready"), 1)

        @block.gpsimd
        def _(pool):
            w = Tally()

            def attention_bias(dst, n_tiles=TT):
                for t in range(n_tiles):
                    src = bass.AP(skew.tensor, 255 - P * t, [[4 * SKEW - 1, P], [SKEW, 4], [1, T]])
                    pool.dma_start(dst[:, t * 4 * T:(t + 1) * 4 * T].rearrange("p (h k) -> p h k", h=4),
                                   src).then_inc(sem("attention_tables_loaded"), 16)

            e = EVEN
            pool.wait_ge(sem("x_normed"), w.up(sem("x_normed")))
            pool.dma_start(REL, bias_in).then_inc(sem("bias_loaded"), 16)
            pool.dma_start(ONEHOT, masks_in[:, MASK_BUCKET:MASK_BUCKET + SKEW])\
                .then_inc(sem("bias_loaded"), 16)
            pool.dma_start(e["low"], masks_in[:, MASK_LOW:MASK_LOW + PAIR_LEVELS * P])\
                .then_inc(sem("low_masks_loaded"), 16)
            pool.wait_ge(sem("bias_rows_taken"), w.up(sem("bias_rows_taken")))
            pool.dma_start(skew, ROWS).then_inc(sem("bias_rows_stored"), 16)
            pool.wait_ge(sem("bias_rows_stored"), w.up(sem("bias_rows_stored"), 16))
            pool.wait_ge(sem("gdn_out_psum"), w.up(sem("gdn_out_psum")))
            attention_bias(e["bias"])
            pool.dma_start(e["neg"], masks_in[:, MASK_SWA:MASK_SWA + 6 * T])\
                .then_inc(sem("attention_tables_loaded"), 16)
            pool.wait_ge(sem("x_normed"), w.up(sem("x_normed"), 2))
            e = ODD
            attention_bias(e["bias"])
            pool.dma_start(e["neg"], masks_in[:, MASK_CAUSAL:MASK_CAUSAL + 2 * T])\
                .then_inc(sem("attention_tables_loaded"), 16)
            pool.dma_start(e["lamv"], lam_in).then_inc(sem("attention_tables_loaded"), 16)


def constants():
    i = np.arange(P)
    s, t = i[:, None], i[None, :]
    eye = np.eye(P)
    ones = np.ones((P, P))
    pairs = [((s >> (l + 1)) == (t >> (l + 1))) & (((s >> l) & 1) == 0) & (((t >> l) & 1) == 1)
             for l in range(PAIR_LEVELS)]
    parts = {
        "ident": eye, "ones": ones, "mean_d": ones / D, "mean_head": ones / P,
        "iota": np.tile(i, (P, 1)), "iota16": np.tile(np.arange(TOPK), (P, 1)),
        "tri": s <= t, "strict": s < t, "pairs": np.concatenate(pairs, 1),
        "eps": np.tile([1e-6, 1e-5], (P, 1)), "zero": np.zeros((P, P)),
    }
    consts = np.concatenate([np.asarray(parts[n], np.float32) for n, _ in CONSTS], 1)
    q, k = np.arange(T)[:, None], np.arange(T)[None, :]
    dist = q - k
    swa = np.zeros((TT, P, SWA_GROUPS, T), np.float32)
    for g, (window, dil) in enumerate(SWA_CONFIGS):
        ok = (dist >= 0) & (dist % dil == 0) & (dist // dil <= window // dil)
        swa[:, :, g] = np.where(ok, 0.0, NEG).reshape(TT, P, T)
    causal = np.where(dist >= 0, 0.0, NEG).reshape(TT, P, T)
    dd = np.maximum(255 - np.arange(SKEW), 0)
    exact = NUM_BUCKETS // 2
    f = np.float32
    large = exact + (np.log(np.maximum(dd, 1).astype(f) / f(exact)) / f(math.log(REL_MAX / exact))
                     * f(NUM_BUCKETS - exact)).astype(np.int32)
    bucket = np.where(dd < exact, dd, np.minimum(large, NUM_BUCKETS - 1))
    onehot = np.zeros((P, SKEW), np.float32)
    onehot[bucket, np.arange(SKEW)] = 1
    low = np.concatenate([m.T for m in pairs], 1)
    masks = np.concatenate([low, swa.transpose(1, 0, 2, 3).reshape(P, -1),
                            causal.transpose(1, 0, 2).reshape(P, -1), onehot], 1)
    return consts, np.ascontiguousarray(masks, np.float32)


def tiles_of(w):
    k, m = w.shape
    return w.reshape(k // P, P, m // P, P).transpose(2, 1, 0, 3).reshape(m // P, P, -1)


def column_chunks(v):
    return v.reshape(-1, P).T


def lay_out(a):
    a = {k: np.asarray(v) for k, v in a.items()}
    f = np.float32
    tiles = np.zeros((STREAM_TILES, P, TILE), f)

    def put(name, arr):
        at, n = STREAM_AT[name]
        tiles[at:at + n] = arr

    for l in range(2):
        put(f"ada{l}", tiles_of(a["w_ada"][l]))
        put(f"wq{l}", tiles_of(a["peer_w_q"][l]))
        put(f"keys{l}", a["peer_keys"][l].reshape(2, 8, NKEYS, P).transpose(0, 3, 1, 2).reshape(2, P, TILE))
        at, n = STREAM_AT[f"experts{l}"]
        up = a["peer_u"][l].reshape(NKEYS, NKEYS, DC, P).transpose(1, 3, 2, 0)
        down = a["peer_v"][l].reshape(NKEYS, NKEYS, D).transpose(1, 0, 2)
        tiles[at] = up[0].reshape(P, TILE)
        tiles[at + 1:at + n - 2:2] = up[1:].reshape(NKEYS - 1, P, TILE)
        tiles[at + 2:at + n - 1:2] = down[:-1]
        tiles[at + n - 1] = down[-1]
        put(f"up{l}", tiles_of(a["ffn_w_up_2"][l]))
        put(f"down{l}", a["ffn_w_down_2"][l].reshape(FC, P, D))
    put("hg_in", tiles_of(a["hg_w_in"][0]))
    put("hg_out", tiles_of(a["hg_w_out"][0]))
    put("lru_in", tiles_of(a["lru_w_in"][0]))
    put("lru_out", tiles_of(a["lru_w_out"][0]))
    g = np.stack([a["lru_w_a"][0], a["lru_w_x"][0]], 1)
    g = g.reshape(2, 2, 2, 2, 2, P, 2, P)
    put("lru_gates", g.transpose(0, 1, 2, 5, 3, 6, 4, 7).reshape(8, P, TILE))
    we, wo = a["w_in_even_2"][0], a["w_in_odd_2"][0]
    nba = 4 * GDN_HEADS * P
    put("even_in", tiles_of(np.concatenate([we[:, :nba], we[:, nba + 12:]], 1)))
    put("even_out", tiles_of(a["w_out_even_2"][0]))
    put("odd_in", tiles_of(wo[:, :24 * P]))
    put("odd_out", tiles_of(a["w_out_odd_2"][0]))

    vec = {
        "c": a["c"], "norm_g": a["norm_g"], "b_ada": a["b_ada"], "hg_lb": a["hg_lb"],
        "hg_norm_g": a["hg_norm_g"], "lru_conv_w": a["lru_conv_w"], "lru_conv_b": a["lru_conv_b"],
        "lru_b_a": a["lru_b_a"], "lru_b_x": a["lru_b_x"], "lru_lam": a["lru_lam"],
        "final_g": a["final_g"], "gdn_conv_w": a["gdn_conv_w_2"], "gdn_norm_w": a["gdn_norm_w_2"],
        "diff_norm_w": a["diff_norm_w_2"], "gla_b_gate": a["gla_b_gate_2"],
        "gla_norm_w": a["gla_norm_w_2"], "ffn_conv_w": a["ffn_conv_w_2"],
        "ffn_conv_b": a["ffn_conv_b_2"], "ln_g": a["ln_g_2"], "ln_b": a["ln_b_2"],
    }
    cols = {n: column_chunks(x) for n, x in vec.items()}
    for n in ("gdn_dt_bias", "gdn_a_log"):
        cols[n] = np.repeat(a[n + "_2"].reshape(1, GDN_HEADS), P, 0)
    for n, size in PARAMS:
        assert cols[n].shape == (P, size), (n, cols[n].shape)
    params = np.concatenate([cols[n] for n, _ in PARAMS], 1)

    def by_rows(w):
        return w.reshape(DC, P, -1).transpose(1, 0, 2).reshape(P, -1)

    gate = np.zeros((P, 2 * P), f)
    gate[:GATE_RANK] = a["gla_w_gate_2"][0]
    small = np.concatenate([by_rows(we[:, nba:nba + 12]), by_rows(wo[:, 24 * P:]), gate], 1)
    bias = np.zeros((P, 4, P), f)
    bias[:NUM_BUCKETS] = a["rel_bias_2"][:, :, None]
    consts, masks = constants()
    x = a["x"][0].reshape(T, DC, P).transpose(2, 1, 0).reshape(P, -1)
    lam = np.repeat(a["diff_lambda_2"][0].reshape(1, -1), P, 0)
    return {"tiles": tiles, "x": x, "params": params, "consts": consts, "small": small, "masks": masks,
            "lam": lam, "bias": bias.reshape(P, -1)}


ORDER = ["tiles", "x", "params", "consts", "small", "masks", "lam", "bias"]


def kernel(**inputs):
    import concourse.bacc as _bacc
    from concourse.bass_utils import run_bass_kernel_spmd as _run

    nc = _bacc.Bacc("TRN2", target_bir_lowering=False, num_devices=1)
    arrays = {n: np.ascontiguousarray(v) for n, v in lay_out(inputs).items()}
    args = [nc.dram_tensor(n, arrays[n].shape, F32, kind="ExternalInput").ap() for n in ORDER]
    skew = nc.dram_tensor("skew", (P, 4 * SKEW), F32, kind="Internal").ap()
    out = nc.dram_tensor("out", (P, DC * T), F32, kind="ExternalOutput").ap()
    build(nc, *args, skew, out)
    r = _run(nc, [arrays], core_ids=[0])
    got = r.results[0]["out"]
    return np.ascontiguousarray(got.reshape(P, DC, T).transpose(2, 1, 0).reshape(1, T, D))
```

```python
import math
from contextlib import ExitStack

import numpy as np

import concourse.bass as bass
from concourse import mybir

F32 = mybir.dt.float32
F32R = mybir.dt.float32r
U32 = mybir.dt.uint32
ALU = mybir.AluOpType
ACT = mybir.ActivationFunctionType
AX = mybir.AxisListType

P = 128
T = 256
TT = T // P
D = 1024
DC = D // P
RING = 4
UNROLL = 8
HALF = 512
TILE = 1024
HG_HEADS = 8
LRU_BLOCKS = 4
PEER_HEADS = 8
NKEYS = 128
TOPK = 16
EARLY = 52
MAIN = NKEYS - EARLY
GDN_HEADS = 6
SWA_GROUPS, SWA_HEADS, SWA_DH = 3, 4, 64
SWA_CONFIGS = ((128, 1), (512, 4), (2048, 16))
DIFF_HEADS = 4
GLA_HEADS, GLA_DK = 4, 64
GLA_TAU = 16.0
GATE_RANK = 16
D_FF = 2816
FC = D_FF // P
NUM_BUCKETS, REL_MAX = 32, 2048
LRU_C = 8.0
DEPTH = 2
ALPHA = (2 * DEPTH) ** 0.25
LAM_INIT = 0.8 - 0.6 * math.exp(-0.3)
PAIR_LEVELS = 7
DIAGONAL, CROSS = PAIR_LEVELS, PAIR_LEVELS + 1
SKEW = 512
NEG = -1e30

PARAMS = [
    ("c", DC), ("norm_g", 4 * DC), ("b_ada", 2 * 6 * DC), ("hg_lb", DC), ("hg_norm_g", DC),
    ("lru_conv_w", 4 * DC), ("lru_conv_b", DC), ("lru_b_a", 2 * DC), ("lru_b_x", 2 * DC),
    ("lru_lam", 2 * DC), ("final_g", DC), ("gdn_conv_w", 4 * 18), ("gdn_norm_w", 1),
    ("gdn_dt_bias", GDN_HEADS), ("gdn_a_log", GDN_HEADS), ("diff_norm_w", 1),
    ("gla_b_gate", 2), ("gla_norm_w", 1), ("ffn_conv_w", 2 * 3 * 2 * FC),
    ("ffn_conv_b", 2 * 2 * FC), ("ln_g", 4 * DC), ("ln_b", 4 * DC),
]
CONSTS = [
    ("ident", P), ("ones", P), ("mean_d", P), ("mean_head", P), ("iota", NKEYS), ("iota16", TOPK),
    ("tri", P), ("strict", P), ("pairs", PAIR_LEVELS * P), ("eps", 2), ("zero", P),
]
SMALL = [("w_ba", DC * 2 * GDN_HEADS), ("w_gd", DC * GATE_RANK), ("w_gate", 2 * P)]


def columns(table):
    at, out = 0, {}
    for name, n in table:
        out[name] = (at, n)
        at += n
    return out, at


STREAM = [
    ("hg_in", 5 * DC), ("hg_out", DC), ("wq0", 2 * PEER_HEADS), ("keys0", 2),
    ("early0", EARLY), ("experts0", 2 * MAIN), ("late0", EARLY),
    ("lru_in", 2 * DC), ("lru_gates", 8), ("lru_out", DC),
    ("wq1", 2 * PEER_HEADS), ("keys1", 2),
    ("early1", EARLY), ("experts1", 2 * MAIN), ("late1", EARLY),
    ("even_in", 42), ("even_out", DC), ("up0", 2 * FC), ("down0", FC),
    ("odd_in", 24), ("odd_out", DC), ("up1", 2 * FC), ("down1", FC),
]
STREAM_AT, STREAM_USED = columns(STREAM)
SPLIT_TILES = 2 * MAIN + EARLY


def split_at(layer, k):
    return 2 * (layer * SPLIT_TILES + k)


def down_at(j):
    return 3 + 2 * j if j < MAIN - 2 else MAIN + j


class Tally:

    def __init__(self):
        self.count = {}

    def up(self, sem, by=1):
        self.count[id(sem)] = self.count.get(id(sem), 0) + by
        return self.count[id(sem)]

    def value(self, sem):
        return self.count.get(id(sem), 0)


def wide(ap, *shape):
    return ap.broadcast_to(list(shape))


def over(ap, n):
    return wide(ap.unsqueeze(1), ap.shape[0], n, ap.shape[1])


def build(nc, tiles, ada_in, x_in, params_in, consts_in, small_in, masks_in, lam_in, bias_in, skew, out):
    pcol, n_params = columns(PARAMS)
    ccol, n_consts = columns(CONSTS)
    scol, n_small = columns(SMALL)

    ctx = ExitStack()
    with ctx:
        def sb(name, cols, dt=F32):
            return ctx.enter_context(nc.sbuf_tensor(name, [P, cols], dt))

        sems = {}

        def sem(name):
            if name not in sems:
                sems[name] = ctx.enter_context(nc.semaphore(name))
            return sems[name]

        def overlaid(name, cols, *others):
            with nc.sbuf_tensor(name, [P, cols], F32) as whole:
                pass
            parts = [sb(n, size, F32R) for n, size in others]
            if cols > sum(size for _, size in others):
                sb(name + "_rest", cols - sum(size for _, size in others))
            return whole, *parts

        X = sb("X", DC * T)
        H, w_high = overlaid("H", DC * T, ("w_high", 2 * TILE))
        h_high = sb("h_high", DC * T, F32R)
        h_low = sb("h_low", DC * T, F32R)
        ring = sb("ring", RING * TILE)
        BIG = sb("BIG", 128 * T)
        par = sb("par", n_params)
        con = sb("con", n_consts)
        mod = sb("mod", 2 * 6 * DC)
        coef = sb("coef", 112)
        slots, a_low = overlaid("slots", 3 * T, ("a_low", 2 * T))
        onehots, w_low = overlaid("onehots", 2 * 2 * 4 * P, ("w_low", 2 * TILE))
        onehot_a, onehot_b = onehots[:, 0:2 * 4 * P], onehots[:, 2 * 4 * P:]
        act_v = sb("act_v", 2 * T)
        a_high = sb("a_high", 2 * T, F32R)
        inv = sb("inv", T)
        SM = sb("SM", n_small)
        stat = sb("stat", 16)
        PA = ctx.enter_context(nc.psum_tensor("PA", [P, 4 * 512], F32))
        PB = ctx.enter_context(nc.psum_tensor("PB", [P, 4 * 512], F32))

        def p(name, i=0, n=None):
            at, size = pcol[name]
            return par[:, at + i:at + i + (size if n is None else n)]

        def c(name, i=0, n=None):
            at, size = ccol[name]
            return con[:, at + i:at + i + (size if n is None else n)]

        def big(at, n):
            return BIG[:, at:at + n]

        def chunks(ap, t=T):
            return ap.rearrange("p (c t) -> p c t", t=t)

        ident = c("ident")
        TMP = big(120 * T, DC * T)

        def tile_half(ap, k, b):
            return ap[:, (k % 2) * TILE + b * HALF:(k % 2) * TILE + (b + 1) * HALF]

        def pair(ap, j):
            return ap[:, (j % 2) * T:(j % 2 + 1) * T]

        loaded = [sem(f"tile_loaded_{i}") for i in range(RING)]
        tile_done = sem("tile_done")
        ada_loaded = [sem(f"ada_loaded_{i}") for i in range(DC)]
        taken = sem("product_taken")

        PRODUCTS = [("hg_in", 5 * DC), ("hg_out", DC), ("wq0", 16), ("lru_in", 16), ("lru_out", DC),
                    ("wq1", 16), ("even_in", 42), ("even_out", DC), ("up0", 2 * FC),
                    ("odd_in", 24), ("odd_out", DC), ("up1", 2 * FC)]
        product_at, _ = columns(PRODUCTS)

        def product_slot(i):
            return PB[:, (i % 4) * 512:(i % 4) * 512 + T]


        HG = []
        for d in range(2):
            HG.append(dict(chunks=DC, heads=HG_HEADS, v_made=d == 1,
                           q=big((0, 40 * T)[d], DC * T), v=big((24 * T, 8 * T)[d], DC * T),
                           logit=big((8 * T, 16 * T)[d], DC * T), k=big(48 * T, DC * T),
                           b=big(56 * T, DC * T), e=big(64 * T, DC * T), kh=big(72 * T, DC * T),
                           qh=big(80 * T, DC * T), at=big(88 * T, DC * T), ax=big(96 * T, 4 * T),
                           vt=big(100 * T, DC * T)))
        ADA_RING, ADA_SUMS = big(40 * T, DC * TILE), big(72 * T, 12 * D)
        HG_G = big(32 * T, DC * T)
        HG_MIX = big(108 * T, DC * T)
        LRU = dict(xc=big(0, 8 * T), y=big(8 * T, 8 * T),
                   gate=[big((16 + 8 * i) * T, 8 * T) for i in range(4)],
                   la=big(48 * T, 8 * T), a=big(56 * T, 8 * T), m=big(64 * T, 8 * T),
                   h0=big(72 * T, 8 * T), h1=big(80 * T, 8 * T))
        EVEN = dict(q=big(0, 6 * T), k=big(6 * T, 6 * T), v=big(12 * T, 6 * T), z=big(18 * T, 6 * T),
                    qb=big(24 * T, 6 * T), kb=big(30 * T, 6 * T), vb=big(36 * T, 6 * T),
                    sq=big(42 * T, 6 * T), vt=big(48 * T, 6 * T), dt=big(54 * T, 9 * T),
                    mt=big(63 * T, 6 * T), m01=big(69 * T, 3 * T), qk0=big(72 * T, 3 * T),
                    qk01=big(75 * T, 3 * T), qk1=big(78 * T, 3 * T), n=big(81 * T, 6 * T),
                    nt=big(87 * T, 6 * T), x=big(93 * T, 6 * T), y=big(99 * T, 6 * T),
                    c=big(105 * T, 6 * T), ct=big(111 * T, 6 * T), p1=big(42 * T, 6 * T),
                    p2=big(117 * T, 6 * T), d0=big(105 * T, 3 * T), r1=big(108 * T, 3 * T),
                    d1=big(111 * T, 3 * T), ba=big(123 * T, 24), g=big(123 * T + 24, 12),
                    beta=big(123 * T + 36, 12), nbeta=big(123 * T + 48, 12),
                    gam=big(123 * T + 60, 12), t0=big(123 * T + 72, 12), t1=big(123 * T + 84, 12),
                    ea=big(123 * T + 96, 6), low=big(124 * T, PAIR_LEVELS * P),
                    mix=big(81 * T, 8 * T), vbt=big(54 * T, 6 * T), bias=big(60 * T, 8 * T),
                    neg=big(68 * T, 6 * T), prob=big(74 * T, 3 * T), probt=big(77 * T, 3 * T))
        ODD = dict(qc=big(0, 4 * T), kc=big(4 * T, 4 * T), vc=big(8 * T, 4 * T), r=big(20 * T, 4 * T),
                   gd=big(42 * T, T), g1=big(43 * T, 2 * T), g2=big(45 * T, 2 * T),
                   sq=big(47 * T, 4 * T), vct=big(51 * T, 4 * T), bias=big(55 * T, 8 * T),
                   neg=big(63 * T, 2 * T), prob=big(65 * T, 2 * T), probt=big(67 * T, T),
                   lamv=big(69 * T, T), mix=big(70 * T, 8 * T))
        GLA = dict(chunks=2, heads=GLA_HEADS, v_made=False, q=big(12 * T, 2 * T), k=big(14 * T, 2 * T),
                   v=big(16 * T, 4 * T), b=big(24 * T, 2 * T), e=big(26 * T, 2 * T),
                   kh=big(28 * T, 2 * T), qh=big(30 * T, 2 * T), at=big(32 * T, 4 * T),
                   ax=big(36 * T, 2 * T), vt=big(38 * T, 4 * T))
        REL, ONEHOT, ROWS = big(0, 512), big(512, SKEW), big(1024, 4 * SKEW)
        MASK_LOW, MASK_SWA, MASK_CAUSAL, MASK_BUCKET = 0, 7 * P, 7 * P + 6 * T, 7 * P + 8 * T
        KEY_SCORES = [big((16 + 8 * t) * T, 8 * T) for t in range(TT)]
        SPARE, CAND, CAND_SPARE, PICK = (big((32 + 8 * i) * T, 8 * T) for i in range(4))
        VAL, IDX, IDX_F = (big((64 + i) * T, T) for i in range(3))
        CVAL, CPOS, HIGH, LOW, HIGH_F, LOW_F, GATE = (big(67 * T + i * P, P) for i in range(7))
        GSUM = big(71 * T, PEER_HEADS)

        def chosen(t, j):
            return big(72 * T + (t * 3 + j) * P, P)

        block = ctx.enter_context(nc.Block())

        @block.sync
        def _(sp):
            w = Tally()
            sp.dma_start(par[:, :], params_in).then_inc(sem("params_loaded"), 16)
            sp.dma_start(X[:, :], x_in).then_inc(sem("x_loaded"), 16)
            sp.dma_start(con[:, :], consts_in).then_inc(sem("consts_loaded"), 16)
            sp.dma_start(SM[:, :], small_in).then_inc(sem("small_loaded"), 16)

            def load(s, n):
                sp.dma_start(ring[:, s * TILE:(s + 1) * TILE], tiles[n]).then_inc(loaded[s], 16)

            for s in range(RING):
                load(s, s)

            def reload(n, it, layer=None):
                if layer is None:
                    sp.wait_ge(tile_done, it * RING + (n + 1))
                else:
                    k = n - STREAM_AT[f"experts{layer}"][0]
                    sp.wait_ge(sem("low_ready"), it * (2 * RING) + split_at(layer, k + 1))
                load(n % RING, it * RING + (n + RING))

            starts = [(0, None)]
            for l in range(2):
                starts += [(STREAM_AT[f"experts{l}"][0], l), (sum(STREAM_AT[f"late{l}"]), None)]
            for (n0, layer), (n1, _) in zip(starts, starts[1:] + [(STREAM_USED, None)]):
                n1 = min(n1, STREAM_USED - RING)
                if n0 < n1:
                    full = (n1 - n0) // RING
                    with sp.Fori(0, full) as it:
                        for s in range(RING):
                            reload(n0 + s, it, layer)
                    for n in range(n0 + RING * full, n1):
                        reload(n, 0, layer)
            sp.wait_ge(sem("result_ready"), w.up(sem("result_ready")))
            sp.dma_start(out, X[:, :]).then_inc(sem("result_stored"), 16)
            sp.wait_ge(sem("result_stored"), w.up(sem("result_stored"), 16))

        @block.tensor
        def _(pe):
            w = Tally()
            mm = nc.tensor.matmul

            def tile(n, it=0):
                pe.wait_ge(loaded[n % RING], it * (16 * UNROLL // RING) + (n // RING + 1) * 16)
                return ring[:, (n % RING) * TILE:(n % RING + 1) * TILE]

            def loop(n, body, peel=0):
                full = n // UNROLL
                if full < 2 + (peel > 0):
                    for i in range(n):
                        body(i, 0)
                    return
                for i in range(UNROLL * peel):
                    body(i, 0)
                with pe.Fori(peel, full) as it:
                    for i in range(UNROLL):
                        body(i, it)
                for i in range(UNROLL * full, n):
                    body(i, 0)

            def linear(name, src):
                r0, n = STREAM_AT[name]
                q0 = product_at[name][0]

                def body(i, it):
                    wt = tile(r0 + i, it)
                    if not isinstance(it, int) or q0 + i >= 4:
                        pe.wait_ge(taken, it * UNROLL + (q0 + i - 3))
                    for k in range(DC):
                        ins = mm(product_slot(q0 + i), wt[:, k * P:(k + 1) * P],
                                 src[:, k * T:(k + 1) * T], start=k == 0, stop=k == DC - 1)
                    ins.then_inc(tile_done, 1)

                loop(n, body, peel=1 if q0 == 0 else 0)

            def all_taken(name):
                q0, n = product_at[name]
                pe.wait_ge(taken, q0 + n)

            def ada(first, last):
                pe.wait_ge(sem("ada_sums_ready"), last)
                for m in range(first * DC, last * DC):
                    ins = mm(PA[:, m:m + 1], ADA_SUMS[:, m * P:(m + 1) * P], c("ones", 0, 1),
                             start=True, stop=True)
                ins.then_inc(sem("ada_psum"), 1)

            def column_sums(squares, mat, dst):
                for k in range(DC):
                    ins = mm(dst, mat, squares[:, k * T:(k + 1) * T], start=k == 0, stop=k == DC - 1)
                return ins

            def rms():
                pe.wait_ge(sem("squares_ready"), w.up(sem("squares_ready")))
                column_sums(TMP, c("mean_d"), PA[:, 0:T]).then_inc(sem("mean_square_ready"), 1)

            def layer_norm():
                pe.wait_ge(sem("x_ready"), w.up(sem("x_ready")))
                column_sums(X[:, :], c("mean_d"), PA[:, 0:T]).then_inc(sem("mean_ready"), 1)
                rms()

            def head_sums(n, src, mat, dst):
                for h in range(n):
                    ins = mm(dst[:, h * T:(h + 1) * T], mat, src[:, h * T:(h + 1) * T],
                             start=True, stop=True)
                return ins

            def decay_attention(cfg):
                nh, kh, qh = cfg["heads"], cfg["kh"], cfg["qh"]
                per = nh // cfg["chunks"]
                rows = P // per

                def operand(buf, h, ch):
                    lo = (h % per) * rows
                    at = (h // per) * T + ch * P
                    return buf[lo:lo + rows, at:at + P]

                if cfg["v_made"]:
                    pe.wait_ge(sem("decay_v_ready"), w.up(sem("decay_v_ready")))
                for h in range(nh):
                    for ch in range(TT):
                        ins = nc.tensor.transpose(PA[:, (h * TT + ch) * P:(h * TT + ch + 1) * P],
                                                  cfg["v"][:, h * T + ch * P:h * T + (ch + 1) * P], ident)
                ins.then_inc(sem("decay_vt_psum"), 1)
                for lev in range(CROSS + 1):
                    dst = (PB, PA)[lev % 2]
                    if lev == 1:
                        pe.wait_ge(sem("decay_vt_ready"), w.up(sem("decay_vt_ready")))
                    if lev >= 2:
                        pe.wait_ge(sem("decay_masked"), w.up(sem("decay_masked")))
                    if lev != DIAGONAL:
                        pe.wait_ge(sem("decay_keys_ready"), w.up(sem("decay_keys_ready")))
                    k_, q_ = (cfg["k"], cfg["q"]) if lev == DIAGONAL else (kh, qh)
                    for h in range(nh):
                        for ch in range(TT if lev != CROSS else 1):
                            at = (h % per) * 1024 + (h // per * TT + ch if lev != CROSS else h // per) * P
                            ins = mm(dst[:, at:at + P], operand(k_, h, ch),
                                     operand(q_, h, 1 if lev == CROSS else ch), start=True, stop=True)
                    ins.then_inc(sem("decay_scores"), 1)
                pe.wait_ge(sem("decay_masked"), w.up(sem("decay_masked")))
                pe.wait_ge(sem("decay_masked"), w.up(sem("decay_masked")))
                vt, at_, ax = cfg["vt"], cfg["at"], cfg["ax"]
                for h in range(nh):
                    for ch in range(TT):
                        o = PA[:, (h * TT + ch) * P:(h * TT + ch + 1) * P]
                        v_own = vt[:, (h * TT + ch) * P:(h * TT + ch + 1) * P]
                        i = (h % per) * (nh // per) + h // per
                        a_own = at_[:, (i * TT + ch) * P:(i * TT + ch + 1) * P]
                        ins = mm(o, v_own, a_own, start=True, stop=ch == 0)
                        if ch == 1:
                            ins = mm(o, vt[:, h * TT * P:(h * TT + 1) * P], ax[:, i * P:(i + 1) * P],
                                     start=False, stop=True)
                ins.then_inc(sem("decay_out"), 1)

            def peer(layer):
                linear(f"wq{layer}", H)
                all_taken(f"wq{layer}")
                QT = big(0, 16 * T)
                r0, n = STREAM_AT[f"keys{layer}"]
                for i in range(n):
                    kt = tile(r0 + i)
                    for j in range(8):
                        hp = i * 8 + j
                        for t, dst in enumerate((PA, PB)):
                            ins = mm(dst[:, hp * NKEYS:(hp + 1) * NKEYS],
                                     QT[:, hp * T + t * P:hp * T + (t + 1) * P],
                                     kt[:, j * NKEYS:(j + 1) * NKEYS], start=True, stop=True)
                    ins.then_inc(tile_done, 1)
                pe.wait_ge(sem("key_scores"), TT * (layer + 1))
                r0, n = STREAM_AT[f"early{layer}"]
                e0 = layer * EARLY

                def early(i, it):
                    ut = tile(r0 + i, it)
                    if not isinstance(it, int) or e0 + i >= 4:
                        pe.wait_ge(sem("early_gelu"), it * UNROLL + (e0 + i - 3))
                    for k in range(DC):
                        ins = mm(PB[:, (i % 4) * 512:(i % 4) * 512 + T], ut[:, k * P:(k + 1) * P],
                                 H[:, k * T:(k + 1) * T], start=k == 0, stop=k == DC - 1)
                    ins.then_inc(tile_done, 1)

                loop(n, early, peel=1)
                for t in range(TT):
                    pe.wait_ge(sem("chosen_ready"), w.up(sem("chosen_ready")))
                    for j in range(3):
                        ins = nc.tensor.transpose(PA[:, (t * 3 + j) * P:(t * 3 + j + 1) * P],
                                                  chosen(t, j), ident)
                ins.then_inc(sem("slots_psum"), 1)
                pe.wait_ge(sem("slots_ready"), w.up(sem("slots_ready")))

                g0 = layer * 64

                def group(r, it):
                    pe.wait_ge(sem("onehots_ready"), it * 4 + (g0 + r + 1))
                    if not isinstance(it, int) or g0 + r >= 4:
                        pe.wait_ge(sem("gates_folded"), it * 4 + (g0 + r - 3))
                    for j in range(4):
                        at = ((r % 2) * 4 + j) * P
                        ins = mm(PA[:, (r * 4 + j) * P:(r * 4 + j + 1) * P],
                                 onehot_a[:, at:at + P], onehot_b[:, at:at + P], start=True, stop=True)
                    ins.then_inc(sem("gates_psum"), 1)

                for r in range(4):
                    group(r, 0)
                with pe.Fori(1, 16) as it:
                    for r in range(4):
                        group(r, it)

                pe.wait_ge(sem("gates_folded"), g0 + 64)
                for b in range(4):
                    mm(PA[:, b * 512:(b + 1) * 512], c("zero", 0, P), wide(c("zero", 0, 1), P, 512),
                       start=True, stop=False, skip_group_check=True)
                pe.wait_ge(sem("h_split"), w.up(sem("h_split")))

                def passes(dst, k, b, at, high, low, start, stop):
                    lhs_h = tile_half(w_high, k, b)[:, at * P:(at + 1) * P]
                    lhs_l = tile_half(w_low, k, b)[:, at * P:(at + 1) * P]
                    mm(dst, lhs_l, high, start=start, stop=False, skip_group_check=True)
                    mm(dst, lhs_h, low, start=False, stop=False, skip_group_check=True)
                    return mm(dst, lhs_h, high, start=False, stop=stop, skip_group_check=True)

                def up(j, k, it=0):
                    for b in range(2):
                        pe.wait_ge(sem("low_ready"), it * 16 + (split_at(layer, k) + b + 1))
                        for q in range(4):
                            m = 4 * b + q
                            ins = passes(PB[:, (j % 4) * 512:(j % 4) * 512 + T], k, b, q,
                                         h_high[:, m * T:(m + 1) * T], h_low[:, m * T:(m + 1) * T],
                                         m == 0, m == DC - 1)
                        ins.then_inc((sem("mid_tile"), tile_done)[b], 1)

                def down(j, k, it=0, step=16):
                    pe.wait_ge(sem("gated_ready"), it * 4 + (layer * NKEYS + j + 1))
                    for b in range(2):
                        pe.wait_ge(sem("low_ready"), it * step + (split_at(layer, k) + b + 1))
                        for q in range(4):
                            m = 4 * b + q
                            ins = passes(PA[:, m * T:(m + 1) * T], k, b, q, pair(a_high, j),
                                         pair(a_low, j), False, j == NKEYS - 1)
                        ins.then_inc((sem("mid_tile"), tile_done)[b], 1)

                up(0, 0)
                up(1, 1)
                steps = (MAIN - 2) // 4
                with pe.Fori(0, steps) as it:
                    for j in range(4):
                        up(j + 2, 2 + 2 * j, it)
                        down(j, down_at(j), it)
                for j in range(4 * steps, MAIN - 2):
                    up(j + 2, 2 + 2 * j)
                    down(j, down_at(j))
                down(MAIN - 2, down_at(MAIN - 2))
                down(MAIN - 1, down_at(MAIN - 1))
                steps = EARLY // 4
                with pe.Fori(0, steps - 1) as it:
                    for j in range(MAIN, MAIN + 4):
                        down(j, down_at(j), it, 8)
                for j in range(NKEYS - 4, NKEYS):
                    down(j, down_at(j))
            def conv_ffn(i):
                linear(f"up{i}", X)
                r0, n = STREAM_AT[f"down{i}"]
                pe.wait_ge(sem("ffn_hidden_ready"), w.up(sem("ffn_hidden_ready")))
                for k in range(n):
                    wt = tile(r0 + k)
                    for m in range(DC):
                        ins = mm(PA[:, m * T:(m + 1) * T], wt[:, m * P:(m + 1) * P],
                                 big(k * T, T), start=k == 0 and m % 2 == 0, stop=k == n - 1,
                                 skip_group_check=True)
                    ins.then_inc(tile_done, 1)

            def bias_rows():
                pe.wait_ge(sem("bias_loaded"), w.up(sem("bias_loaded"), 32))
                for h in range(4):
                    ins = mm(PA[:, h * SKEW:(h + 1) * SKEW], REL[0:32, h * P:(h + 1) * P],
                             ONEHOT[0:32, :], start=True, stop=True)
                ins.then_inc(sem("bias_rows_psum"), 1)

            def even_mixer():
                linear("even_in", X)
                e = EVEN
                all_taken("even_in")
                pe.wait_ge(sem("small_loaded"), w.up(sem("small_loaded"), 16))
                for t in range(TT):
                    for k in range(DC):
                        ins = mm(PB[:, t * 512:t * 512 + 12], X[:, k * T + t * P:k * T + (t + 1) * P],
                                 SM[:, scol["w_ba"][0] + k * 12:scol["w_ba"][0] + (k + 1) * 12],
                                 start=k == 0, stop=k == DC - 1)
                ins.then_inc(sem("ba_psum"), 1)
                for i in range(2):
                    pe.wait_ge(sem("qk_squares"), w.up(sem("qk_squares")))
                    head_sums(GDN_HEADS, e["sq"], c("ones"), PA).then_inc(sem("qk_lengths"), 1)
                pe.wait_ge(sem("qk_roots"), w.up(sem("qk_roots"), 2))
                for h in range(GDN_HEADS):
                    for t in range(TT):
                        ins = nc.tensor.transpose(PA[:, (h * TT + t) * P:(h * TT + t + 1) * P],
                                                  e["v"][:, h * T + t * P:h * T + (t + 1) * P], ident)
                ins.then_inc(sem("gdn_vt_psum"), 1)
                pe.wait_ge(sem("g_ready"), w.up(sem("g_ready")))
                for t in range(TT):
                    for u in range(t + 1):
                        ins = mm(PB[:, 1024 + t * 8:1024 + t * 8 + 6],
                                 c("ones") if u < t else c("tri"), e["g"][:, u * 6:(u + 1) * 6],
                                 start=u == 0, stop=u == t)
                ins.then_inc(sem("gam_col_psum"), 1)
                for h in range(GDN_HEADS):
                    if h >= 2:
                        pe.wait_ge(sem("decay_taken"), w.up(sem("decay_taken")))
                    dst = PB[:, (h % 2) * 512:(h % 2) * 512 + T]
                    for t in range(TT):
                        for u in range(t + 1):
                            ins = mm(dst[:, t * P:(t + 1) * P],
                                     wide(e["g"][:, u * 6 + h:u * 6 + h + 1], P, P),
                                     c("ones") if u < t else c("tri"), start=u == 0, stop=u == t)
                    ins.then_inc(sem("gam_row_psum"), 1)
                pe.wait_ge(sem("decay_taken"), w.up(sem("decay_taken")))
                pe.wait_ge(sem("decay_taken"), w.up(sem("decay_taken")))
                pe.wait_ge(sem("gdn_vt_ready"), w.up(sem("gdn_vt_ready")))
                pe.wait_ge(sem("qk_normed"), w.up(sem("qk_normed")))
                for i, (a, b) in enumerate((("k", "k"), ("k", "q"))):
                    for j, (s, t) in enumerate(((0, 0), (0, 1), (1, 1))):
                        n = i * 3 + j
                        dst = (PA, PB)[n % 2]
                        if n >= 2:
                            pe.wait_ge(sem("pair_taken"), w.up(sem("pair_taken")))
                        for h in range(GDN_HEADS):
                            ins = mm(dst[:, h * P:(h + 1) * P], e[a][:, h * T + s * P:h * T + (s + 1) * P],
                                     e[b][:, h * T + t * P:h * T + (t + 1) * P], start=True, stop=True)
                        ins.then_inc(sem("pair_psum"), 1)
                pe.wait_ge(sem("pair_taken"), w.up(sem("pair_taken")))
                pe.wait_ge(sem("pair_taken"), w.up(sem("pair_taken")))
                NM = GDN_HEADS * TT

                def at(i):
                    return slice(i * P, (i + 1) * P)

                for i in range(NM):
                    ins = nc.tensor.transpose(PA[:, at(i)], e["mt"][:, at(i)], ident)
                ins.then_inc(sem("m_psum"), 1)
                pe.wait_ge(sem("n_ready"), w.up(sem("n_ready")))
                for i in range(NM):
                    ins = nc.tensor.transpose(PB[:, at(i)], e["n"][:, at(i)], ident)
                ins.then_inc(sem("nt_psum"), 1)
                for lev in range(1, PAIR_LEVELS):
                    pe.wait_ge(sem("block_ready"), w.up(sem("block_ready")))
                    for i in range(NM):
                        ins = mm(PA[:, at(i)], e["ct"][:, at(i)], e["x"][:, at(i)], start=True, stop=True)
                    ins.then_inc(sem("inv_p1"), 1)
                    for i in range(NM):
                        ins = mm(PB[:, at(i)], e["c"][:, at(i)], e["y"][:, at(i)], start=True, stop=True)
                    ins.then_inc(sem("inv_p2"), 1)
                    pe.wait_ge(sem("inv_p1_ready"), w.up(sem("inv_p1_ready")))
                    for i in range(NM):
                        ins = mm(PA[:, at(i)], e["y"][:, at(i)], e["p1"][:, at(i)], start=True, stop=True)
                    ins.then_inc(sem("inv_xpx"), 1)
                    pe.wait_ge(sem("inv_p2_ready"), w.up(sem("inv_p2_ready")))
                    for i in range(NM):
                        ins = mm(PB[:, at(i)], e["x"][:, at(i)], e["p2"][:, at(i)], start=True, stop=True)
                    ins.then_inc(sem("inv_ypy"), 1)
                pe.wait_ge(sem("inverse_ready"), w.up(sem("inverse_ready")))
                for h in range(GDN_HEADS):
                    ins = mm(PA[:, at(h)], e["y"][:, at(h * 2)], e["vt"][:, at(h * 2)], start=True, stop=True)
                ins.then_inc(sem("delta0_psum"), 1)
                pe.wait_ge(sem("delta0_ready"), w.up(sem("delta0_ready")))
                for h in range(GDN_HEADS):
                    ins = mm(PB[:, at(h)], e["m01"][:, at(h)], e["d0"][:, at(h)], start=True, stop=True)
                ins.then_inc(sem("carry_psum"), 1)
                pe.wait_ge(sem("carry_ready"), w.up(sem("carry_ready")))
                for h in range(GDN_HEADS):
                    ins = mm(PA[:, at(h)], e["y"][:, at(h * 2 + 1)], e["r1"][:, at(h)], start=True, stop=True)
                ins.then_inc(sem("delta1_psum"), 1)
                pe.wait_ge(sem("delta1_ready"), w.up(sem("delta1_ready")))
                for h in range(GDN_HEADS):
                    for t in range(TT):
                        o = PB[:, (h * TT + t) * P:(h * TT + t + 1) * P]
                        if t == 0:
                            ins = mm(o, e["d0"][:, at(h)], e["qk0"][:, at(h)], start=True, stop=True)
                        else:
                            mm(o, e["d0"][:, at(h)], e["qk01"][:, at(h)], start=True, stop=False)
                            ins = mm(o, e["d1"][:, at(h)], e["qk1"][:, at(h)], start=False, stop=True)
                ins.then_inc(sem("gdn_out_psum"), 1)
                pe.wait_ge(sem("head_squares"), w.up(sem("head_squares")))
                head_sums(GDN_HEADS, e["sq"], c("mean_head"), PA).then_inc(sem("head_means"), 1)
                pe.wait_ge(sem("head_roots"), w.up(sem("head_roots")))
                for i in range(6):
                    for t in range(TT):
                        ins = nc.tensor.transpose(PA[:, (i * TT + t) * P:(i * TT + t + 1) * P],
                                                  e["vb"][:, i * T + t * P:i * T + (t + 1) * P], ident)
                ins.then_inc(sem("swa_vt_psum"), 1)
                pe.wait_ge(sem("swa_vt_ready"), w.up(sem("swa_vt_ready")))
                attend(SWA_GROUPS * TT * P, "swa")
                pe.wait_ge(sem("gdn_done"), w.up(sem("gdn_done")))
                linear("even_out", e["mix"])

            def attend(keys, kind):
                n = 0
                for h in range(4):
                    for t in range(TT):
                        S_, W_ = PA[:, 0:1024], PA[:, 1024:2048]
                        if n >= 1:
                            pe.wait_ge(sem("attention_scores_taken"), w.up(sem("attention_scores_taken")))
                        if kind == "swa":
                            e = EVEN
                            lo = (h % 2) * SWA_DH
                            for g in range(SWA_GROUPS):
                                at = (g * 2 + h // 2) * T
                                ins = mm(S_[:, g * T:(g + 1) * T],
                                         e["qb"][lo:lo + SWA_DH, at + t * P:at + (t + 1) * P],
                                         e["kb"][lo:lo + SWA_DH, at:at + T], start=True, stop=True)
                        else:
                            e = ODD
                            for i in range(2):
                                lo = i * 64
                                ins = mm(S_[:, i * 512:i * 512 + T],
                                         e["qc"][lo:lo + 64, h * T + t * P:h * T + (t + 1) * P],
                                         e["kc"][lo:lo + 64, h * T:(h + 1) * T], start=True, stop=True)
                        ins.then_inc(sem("attention_scores"), 1)
                        pe.wait_ge(sem("attention_weights"), w.up(sem("attention_weights")))
                        nk = keys // P
                        for i in range(nk):
                            ins = nc.tensor.transpose(W_[:, i * P:(i + 1) * P],
                                                      e["prob"][:, i * P:(i + 1) * P], ident)
                        ins.then_inc(sem("attention_wt_psum"), 1)
                        pe.wait_ge(sem("attention_wt_ready"), w.up(sem("attention_wt_ready")))
                        if kind == "swa":
                            lo = (h % 2) * SWA_DH
                            o = PB[lo:lo + SWA_DH, (n % 4) * 512:(n % 4) * 512 + P]
                            for i in range(nk):
                                g, kc = i // TT, i % TT
                                vt = ((g * 2 + h // 2) * TT + kc) * P + lo
                                ins = mm(o, e["vbt"][:, vt:vt + SWA_DH], e["probt"][:, i * P:(i + 1) * P],
                                         start=i == 0, stop=i == nk - 1)
                        else:
                            o = PB[:, (n % 4) * 512:(n % 4) * 512 + P]
                            for i in range(nk):
                                ins = mm(o, e["vct"][:, (h * TT + i) * P:(h * TT + i + 1) * P],
                                         e["probt"][:, i * P:(i + 1) * P], start=i == 0, stop=i == nk - 1)
                        ins.then_inc(sem("attention_out_psum"), 1)
                        n += 1
                pe.wait_ge(sem("attention_scores_taken"), w.up(sem("attention_scores_taken")))
                pe.wait_ge(sem("attention_done"), w.up(sem("attention_done")))

            def odd_mixer():
                e = ODD
                linear("odd_in", X)
                all_taken("odd_in")
                for k in range(DC):
                    ins = mm(PB[0:GATE_RANK, 0:T],
                             SM[:, scol["w_gd"][0] + k * 16:scol["w_gd"][0] + (k + 1) * 16],
                             X[:, k * T:(k + 1) * T], start=k == 0, stop=k == DC - 1)
                ins.then_inc(sem("gd_psum"), 1)
                pe.wait_ge(sem("gd_ready"), w.up(sem("gd_ready")))
                for i in range(2):
                    ins = mm(PB[:, 512 + i * 512:512 + i * 512 + T],
                             SM[0:GATE_RANK, scol["w_gate"][0] + i * P:scol["w_gate"][0] + (i + 1) * P],
                             e["gd"][0:GATE_RANK, :], start=True, stop=True)
                ins.then_inc(sem("gate_psum"), 1)
                pe.wait_ge(sem("gate_taken"), w.up(sem("gate_taken")))
                decay_attention(GLA)
                pe.wait_ge(sem("head_squares"), w.up(sem("head_squares")))
                head_sums(4, e["sq"], c("mean_head"), PA).then_inc(sem("head_means"), 1)
                pe.wait_ge(sem("head_roots"), w.up(sem("head_roots")))
                for h in range(DIFF_HEADS):
                    for t in range(TT):
                        ins = nc.tensor.transpose(PA[:, (h * TT + t) * P:(h * TT + t + 1) * P],
                                                  e["vc"][:, h * T + t * P:h * T + (t + 1) * P], ident)
                ins.then_inc(sem("diff_vt_psum"), 1)
                pe.wait_ge(sem("diff_vt_ready"), w.up(sem("diff_vt_ready")))
                attend(T, "diff")
                pe.wait_ge(sem("head_squares"), w.up(sem("head_squares")))
                head_sums(4, e["sq"], c("mean_head"), PA).then_inc(sem("head_means"), 1)
                pe.wait_ge(sem("head_roots"), w.up(sem("head_roots")))
                pe.wait_ge(sem("mix_ready"), w.up(sem("mix_ready")))
                linear("odd_out", e["mix"])

            pe.wait_ge(sem("consts_loaded"), w.up(sem("consts_loaded"), 16))
            ada(0, 2)
            pe.wait_ge(sem("mod_ready"), w.up(sem("mod_ready")))
            rms()
            pe.wait_ge(sem("h_ready"), w.up(sem("h_ready")))
            linear("hg_in", H)
            ada(2, 12)
            all_taken("hg_in")
            pe.wait_ge(sem("mod_ready"), w.up(sem("mod_ready")))
            decay_attention(HG[0])
            pe.wait_ge(sem("decay_out_taken"), w.up(sem("decay_out_taken")))
            decay_attention(HG[1])
            pe.wait_ge(sem("head_squares"), w.up(sem("head_squares")))
            head_sums(HG_HEADS, TMP, c("mean_head"), PA).then_inc(sem("head_means"), 1)
            pe.wait_ge(sem("head_roots"), w.up(sem("head_roots")))
            pe.wait_ge(sem("mix_ready"), w.up(sem("mix_ready")))
            linear("hg_out", HG_MIX)
            pe.wait_ge(sem("x_ready"), w.up(sem("x_ready")))
            rms()
            pe.wait_ge(sem("h_ready"), w.up(sem("h_ready")))
            peer(0)
            pe.wait_ge(sem("x_ready"), w.up(sem("x_ready")))
            rms()
            pe.wait_ge(sem("h_ready"), w.up(sem("h_ready")))
            linear("lru_in", H)
            all_taken("lru_in")
            r0, n = STREAM_AT["lru_gates"]
            for i in range(n):
                wt = tile(r0 + i)
                if i >= 2:
                    pe.wait_ge(sem("lru_gate_taken"), w.up(sem("lru_gate_taken")))
                for j in range(4):
                    m = (i % 2) * 4 + j
                    for k in range(2):
                        ins = mm(PA[:, (i % 2) * 1024 + j * T:(i % 2) * 1024 + (j + 1) * T],
                                 wt[:, (j * 2 + k) * P:(j * 2 + k + 1) * P],
                                 LRU["xc"][:, (2 * (m // 2) + k) * T:(2 * (m // 2) + k + 1) * T],
                                 start=k == 0, stop=k == 1)
                ins.then_inc(tile_done, 1)
            pe.wait_ge(sem("lru_gate_taken"), w.up(sem("lru_gate_taken")))
            pe.wait_ge(sem("lru_gate_taken"), w.up(sem("lru_gate_taken")))
            pe.wait_ge(sem("mix_ready"), w.up(sem("mix_ready")))
            linear("lru_out", LRU["h0"])
            pe.wait_ge(sem("x_ready"), w.up(sem("x_ready")))
            rms()
            pe.wait_ge(sem("h_ready"), w.up(sem("h_ready")))
            peer(1)
            pe.wait_ge(sem("x_ready"), w.up(sem("x_ready")))
            rms()
            pe.wait_ge(sem("x_normed"), w.up(sem("x_normed")))
            bias_rows()
            pe.wait_ge(sem("bias_rows_taken"), w.up(sem("bias_rows_taken")))
            even_mixer()
            layer_norm()
            pe.wait_ge(sem("x_normed"), w.up(sem("x_normed")))
            conv_ffn(0)
            layer_norm()
            pe.wait_ge(sem("x_normed"), w.up(sem("x_normed")))
            odd_mixer()
            layer_norm()
            pe.wait_ge(sem("x_normed"), w.up(sem("x_normed")))
            conv_ffn(1)
            layer_norm()

        @block.scalar
        def _(act):
            w = Tally()
            fn = nc.scalar.activation

            def all_taken(name):
                q0, n = product_at[name]
                act.wait_ge(taken, q0 + n)

            def evacuate(name, dst, func=ACT.Identity, first=0, last=None):
                q0, n = product_at[name]
                r0 = STREAM_AT[name][0]
                last = n if last is None else last
                if q0 + first > 0:
                    act.wait_ge(taken, q0 + first)

                def body(i, it):
                    act.wait_ge(tile_done, it * 8 + (r0 + i + 1))
                    fn(dst[:, bass.ds(it * (8 * T) + (i - first) * T, T)], product_slot(q0 + i),
                       func).then_inc(taken, 1)

                full = (last - first) // 8
                if full >= 2:
                    with act.Fori(0, full) as it:
                        for i in range(8):
                            body(first + i, it)
                else:
                    full = 0
                for i in range(first + 8 * full, last):
                    body(i, 0)

            def squares(src, dst, name):
                fn(dst, src, ACT.Square).then_inc(sem(name), 1)

            def root(layer_norm=False):
                act.wait_ge(sem("mean_square_ready"), w.up(sem("mean_square_ready")))
                fn(inv[:, :], PA[:, 0:T], ACT.Sqrt,
                   bias=c("eps", 1 if layer_norm else 0, 1)).then_inc(sem("root_ready"), 1)

            def rms():
                squares(X[:, :], TMP, "squares_ready")
                root()

            def layer_norm():
                act.wait_ge(sem("centered"), w.up(sem("centered")))
                squares(X[:, :], TMP, "squares_ready")
                root(True)

            def head_norm(o, sq, n):
                act.wait_ge(sem("heads_ready"), w.up(sem("heads_ready")))
                squares(o, sq, "head_squares")
                act.wait_ge(sem("head_means"), w.up(sem("head_means")))
                fn(sq, PA[:, 0:n * T], ACT.Sqrt, bias=c("eps", 0, 1)).then_inc(sem("head_roots"), 1)

            def decay_attention(cfg):
                n = cfg["heads"] * T
                act.wait_ge(sem("decay_vt_psum"), w.up(sem("decay_vt_psum")))
                fn(cfg["vt"], PA[:, 0:n], ACT.Identity).then_inc(sem("decay_vt_ready"), 1)
                for lev in range(CROSS + 1):
                    if lev == DIAGONAL:
                        continue
                    act.wait_ge(sem("decay_diff"), w.up(sem("decay_diff")))
                    fn(cfg["e"], cfg["e"], ACT.Abs).then_inc(sem("act_step"), 1)
                    act.wait_ge(sem("act_step"), w.up(sem("act_step")))
                    fn(cfg["e"], cfg["e"], ACT.Exp, scale=-1.0).then_inc(sem("decay_exp"), 1)

            def peer(layer):
                evacuate(f"wq{layer}", big(0, 16 * T))
                r0, n = STREAM_AT[f"keys{layer}"]
                act.wait_ge(tile_done, r0 + n)
                for t, src in enumerate((PA, PB)):
                    fn(KEY_SCORES[t], src[:, :], ACT.Identity).then_inc(sem("key_scores"), 1)
                fn(h_high[:, :], H[:, :], ACT.Identity).then_inc(sem("h_high"), 1)
                r0, n = STREAM_AT[f"early{layer}"]

                def early(first, last):
                    def body(i, it):
                        act.wait_ge(tile_done, it * 8 + (r0 + i + 1))
                        fn(BIG[:, bass.ds(it * (8 * T) + (MAIN + i) * T, T)],
                           PB[:, (i % 4) * 512:(i % 4) * 512 + T],
                           ACT.Gelu_apprx_tanh).then_inc(sem("early_gelu"), 1)

                    full = (last - first) // 8
                    with act.Fori(0, full) as it:
                        for i in range(8):
                            body(first + i, it)
                    for i in range(first + 8 * full, last):
                        body(i, 0)

                for t, (first, last) in enumerate(((0, 24), (24, 40))):
                    early(first, last)
                    act.wait_ge(sem("gate_diff"), w.up(sem("gate_diff")))
                    fn(GATE, GATE, ACT.Exp).then_inc(sem("gate_exp"), 1)
                early(40, n)
                act.wait_ge(sem("slots_psum"), w.up(sem("slots_psum")))
                fn(slots[:, :].rearrange("p (j t c) -> p t j c", j=3, t=TT),
                   PA[:, 0:6 * P].rearrange("p (t j c) -> p t j c", j=3, t=TT),
                   ACT.Identity).then_inc(sem("slots_ready"), 1)
                g0 = layer * 64
                gates = chunks(BIG[:, :])

                def group(r, it):
                    act.wait_ge(sem("gates_psum"), it * 4 + (g0 + r + 1))
                    fn(gates[:, 0:MAIN, bass.ds(it * 16 + r * 4, 4)],
                       PA[:, r * 512:(r + 1) * 512].rearrange("p (t j) -> p j t", t=4)[:, 0:MAIN, :],
                       ACT.Identity).then_inc(sem("gates_copied"), 1)

                with act.Fori(0, 16) as it:
                    for r in range(4):
                        group(r, it)
                r0, n = STREAM_AT[f"experts{layer}"]
                act.wait_ge(sem("h_split"), w.up(sem("h_split")))
                act.wait_ge(tile_done, r0)

                def high(k, it=0, step=8):
                    n = r0 + k
                    act.wait_ge(loaded[n % RING], it * (16 * step // RING) + (n // RING + 1) * 16)
                    for b in range(2):
                        if k >= 2 and b == 0:
                            act.wait_ge(sem("mid_tile"), it * step + (layer * SPLIT_TILES + k - 1))
                        if k >= 2 and b == 1:
                            act.wait_ge(tile_done, it * step + (r0 + k - 1))
                        at = (n % RING) * TILE + b * HALF
                        fn(tile_half(w_high, k, b), ring[:, at:at + HALF],
                           ACT.Identity).then_inc(sem("high_ready"), 1)

                def gelu(j, k, it=0):
                    act.wait_ge(tile_done, it * 8 + (r0 + k + 1))
                    if j >= 2:
                        act.wait_ge(sem("gated_ready"), it * 4 + (layer * NKEYS + j - 1))
                    fn(pair(act_v, j), PB[:, (j % 4) * 512:(j % 4) * 512 + T],
                       ACT.Gelu_apprx_tanh).then_inc(sem("gelu_ready"), 1)

                def column(j, it=0):
                    high(2 * j, it)
                    gelu(j, 2 * j - 2, it)
                    high(2 * j + 1, it)

                high(0)
                high(1)
                high(2)
                gelu(0, 0)
                high(3)
                gelu(1, 1)
                steps = (MAIN - 2) // 4
                with act.Fori(0, steps) as it:
                    for j in range(2, 6):
                        column(j, it)
                for j in range(4 * steps + 2, MAIN):
                    column(j)
                steps = EARLY // 4
                with act.Fori(0, steps) as it:
                    for k in range(2 * MAIN, 2 * MAIN + 4):
                        high(k, it, 4)

            def conv_ffn(i):
                q0, n = product_at[f"up{i}"]
                act.wait_ge(taken, q0 + FC)
                fn(big(0, FC * T), big(0, FC * T), ACT.Silu).then_inc(sem("gate_silu"), 1)

            def attend(kind, e, dst_chunk):
                groups = 3 if kind == "swa" else 2
                for h in range(4):
                    for t in range(TT):
                        act.wait_ge(sem("attention_max"), w.up(sem("attention_max")))
                        if kind == "swa":
                            fn(e["prob"], e["prob"], ACT.Exp, bias=stat[:, 0:1],
                               accum_out=stat[:, 2:3]).then_inc(sem("attention_exp"), 1)
                        else:
                            for i in range(2):
                                fn(e["prob"][:, i * T:(i + 1) * T], e["prob"][:, i * T:(i + 1) * T],
                                   ACT.Exp, bias=stat[:, i:i + 1],
                                   accum_out=stat[:, 2 + i:3 + i]).then_inc(sem("attention_exp"), 1)
                        act.wait_ge(sem("attention_wt_psum"), w.up(sem("attention_wt_psum")))
                        nk = TT * (3 if kind == "swa" else 1)
                        fn(e["probt"], PA[:, 1024:1024 + nk * P],
                           ACT.Identity).then_inc(sem("attention_wt_ready"), 1)
                        act.wait_ge(sem("attention_out_psum"), w.up(sem("attention_out_psum")))
                        n = h * TT + t
                        if kind == "swa":
                            rows = slice((h % 2) * SWA_DH, (h % 2 + 1) * SWA_DH)
                            at = (6 + h // 2) * T + t * P
                        else:
                            rows, at = slice(0, P), h * T + t * P
                        ins = fn(e["mix"][rows, at:at + P], PB[rows, (n % 4) * 512:(n % 4) * 512 + P],
                                 ACT.Identity)
                        if n < 7:
                            ins.then_inc(sem("act_step"), 1)
                            act.wait_ge(sem("act_step"), w.up(sem("act_step")))
                ins.then_inc(sem("attention_done"), 1)

            def even_mixer():
                e = EVEN
                evacuate("even_in", big(18 * T, 24 * T), first=18)
                qkv = big(0, 18 * T)
                act.wait_ge(taken, product_at["even_in"][0] + 42)
                fn(qkv, qkv, ACT.Silu).then_inc(sem("qkv_silu"), 1)
                act.wait_ge(sem("qkv_silu"), w.up(sem("qkv_silu")))
                squares(e["q"], e["sq"], "qk_squares")
                act.wait_ge(sem("qk_lengths"), w.up(sem("qk_lengths")))
                fn(e["x"], PA[:, 0:6 * T], ACT.Sqrt, bias=c("eps", 0, 1)).then_inc(sem("qk_roots"), 1)
                act.wait_ge(sem("qk_roots"), w.up(sem("qk_roots")))
                squares(e["k"], e["sq"], "qk_squares")
                act.wait_ge(sem("qk_lengths"), w.up(sem("qk_lengths")))
                fn(e["y"], PA[:, 0:6 * T], ACT.Sqrt, bias=c("eps", 0, 1)).then_inc(sem("qk_roots"), 1)
                w.up(sem("qk_roots"))
                fn(e["z"], e["z"], ACT.Silu).then_inc(sem("gate_silu"), 1)
                act.wait_ge(sem("ba_ready"), w.up(sem("ba_ready")))
                b_ = e["ba"].rearrange("p (t n) -> p t n", t=2)
                fn(e["beta"].rearrange("p (t n) -> p t n", t=2), b_[:, :, 0:6], ACT.Sigmoid)\
                    .then_inc(sem("beta_ready"), 1)
                fn(e["ea"], p("gdn_a_log", 0, 6), ACT.Exp).then_inc(sem("a_ready"), 1)
                fn(e["t1"], e["t0"], ACT.Abs).then_inc(sem("act_step"), 1)
                act.wait_ge(sem("act_step"), w.up(sem("act_step")))
                fn(e["t1"], e["t1"], ACT.Exp, scale=-1.0).then_inc(sem("act_step"), 1)
                act.wait_ge(sem("act_step"), w.up(sem("act_step")))
                fn(e["t1"], e["t1"], ACT.Ln, bias=c("ones", 0, 1)).then_inc(sem("softplus_ln"), 1)
                act.wait_ge(sem("gdn_vt_psum"), w.up(sem("gdn_vt_psum")))
                act.wait_ge(sem("beta_ready"), w.up(sem("beta_ready")))
                for h in range(GDN_HEADS):
                    for t in range(TT):
                        i = h * TT + t
                        ins = fn(e["vt"][:, i * P:(i + 1) * P], PA[:, i * P:(i + 1) * P], ACT.Identity,
                                 scale=e["beta"][:, t * 6 + h:t * 6 + h + 1])
                ins.then_inc(sem("gdn_vt_ready"), 1)
                for h in range(GDN_HEADS):
                    act.wait_ge(sem("decay_diff_h"), w.up(sem("decay_diff_h")))
                    fn(e["dt"][:, h * 384:(h + 1) * 384], e["dt"][:, h * 384:(h + 1) * 384],
                       ACT.Exp).then_inc(sem("gdn_decay"), 1)
                act.wait_ge(sem("m_psum"), w.up(sem("m_psum")))
                for i in range(12):
                    h, t = i // 2, i % 2
                    ins = fn(e["n"][:, i * P:(i + 1) * P], PA[:, i * P:(i + 1) * P], ACT.Identity,
                             scale=e["beta"][:, t * 6 + h:t * 6 + h + 1])
                ins.then_inc(sem("n_ready"), 1)
                act.wait_ge(sem("nt_psum"), w.up(sem("nt_psum")))
                fn(e["nt"], PB[:, 0:12 * P], ACT.Identity).then_inc(sem("nt_ready"), 1)
                for lev in range(1, PAIR_LEVELS):
                    act.wait_ge(sem("inv_p1"), w.up(sem("inv_p1")))
                    fn(e["p1"], PA[:, 0:12 * P], ACT.Identity).then_inc(sem("inv_p1_ready"), 1)
                    act.wait_ge(sem("inv_p2"), w.up(sem("inv_p2")))
                    fn(e["p2"], PB[:, 0:12 * P], ACT.Identity).then_inc(sem("inv_p2_ready"), 1)
                act.wait_ge(sem("delta0_psum"), w.up(sem("delta0_psum")))
                fn(e["d0"], PA[:, 0:6 * P], ACT.Identity).then_inc(sem("delta0_ready"), 1)
                act.wait_ge(sem("delta1_psum"), w.up(sem("delta1_psum")))
                fn(e["d1"], PA[:, 0:6 * P], ACT.Identity).then_inc(sem("delta1_ready"), 1)
                act.wait_ge(sem("gdn_out_psum"), w.up(sem("gdn_out_psum")))
                fn(e["mix"][:, 0:6 * T], PB[:, 0:6 * T], ACT.Identity).then_inc(sem("heads_ready"), 1)
                head_norm(e["mix"][:, 0:6 * T], e["sq"], 6)
                act.wait_ge(sem("swa_vt_psum"), w.up(sem("swa_vt_psum")))
                fn(e["vbt"], PA[:, 0:12 * P], ACT.Identity).then_inc(sem("swa_vt_ready"), 1)
                attend("swa", e, 6)

            def odd_mixer():
                e = ODD
                evacuate("odd_in", big(0, 24 * T))
                act.wait_ge(sem("gd_psum"), w.up(sem("gd_psum")))
                fn(e["gd"][0:GATE_RANK, :], PB[0:GATE_RANK, 0:T], ACT.Identity).then_inc(sem("gd_ready"), 1)
                act.wait_ge(taken, product_at["odd_in"][0] + 24)
                fn(e["r"], e["r"], ACT.Silu).then_inc(sem("gate_silu"), 1)
                act.wait_ge(sem("gate_taken"), w.up(sem("gate_taken")))
                fn(e["g2"], e["g1"], ACT.Abs).then_inc(sem("act_step"), 1)
                act.wait_ge(sem("act_step"), w.up(sem("act_step")))
                fn(e["g2"], e["g2"], ACT.Exp, scale=-1.0).then_inc(sem("act_step"), 1)
                act.wait_ge(sem("act_step"), w.up(sem("act_step")))
                fn(e["g2"], e["g2"], ACT.Ln, bias=c("ones", 0, 1)).then_inc(sem("softplus_ln"), 1)
                decay_attention(GLA)
                head_norm(e["mix"][:, 4 * T:8 * T], e["sq"], 4)
                act.wait_ge(sem("diff_vt_psum"), w.up(sem("diff_vt_psum")))
                fn(e["vct"], PA[:, 0:8 * P], ACT.Identity).then_inc(sem("diff_vt_ready"), 1)
                act.wait_ge(sem("lam_sums"), w.up(sem("lam_sums")))
                fn(stat[:, 8:10], stat[:, 6:8], ACT.Exp).then_inc(sem("lam_exp"), 1)
                attend("diff", e, 0)
                act.wait_ge(sem("attention_done"), 2)
                squares(e["mix"][:, 0:4 * T], e["sq"], "head_squares")
                act.wait_ge(sem("head_means"), w.up(sem("head_means")))
                fn(e["sq"], PA[:, 0:4 * T], ACT.Sqrt, bias=c("eps", 0, 1)).then_inc(sem("head_roots"), 1)

            act.wait_ge(sem("params_loaded"), w.up(sem("params_loaded"), 16))
            act.wait_ge(sem("consts_loaded"), w.up(sem("consts_loaded"), 16))
            fn(coef[:, 0:DC], p("c", 0, DC), ACT.Silu).then_inc(sem("cond_ready"), 1)
            act.wait_ge(sem("lb_shifted"), w.up(sem("lb_shifted")))
            fn(coef[:, 40:48], coef[:, 40:48], ACT.Exp).then_inc(sem("lb_exp"), 1)
            act.wait_ge(sem("x_loaded"), w.up(sem("x_loaded"), 16))
            rms()
            evacuate("hg_in", big(0, 40 * T))
            all_taken("hg_in")
            fn(HG_G, HG_G, ACT.Silu).then_inc(sem("gate_silu"), 1)
            act.wait_ge(sem("ada_used"), 12 * DC)
            for d in range(2):
                cfg = HG[d]
                if d == 1:
                    act.wait_ge(sem("decay_out_taken"), w.up(sem("decay_out_taken")))
                logit = cfg["logit"] if d == 0 else chunks(cfg["logit"])[:, :, ::-1]
                fn(cfg["e"] if d == 0 else chunks(cfg["e"]), logit, ACT.Sigmoid)\
                    .then_inc(sem("gate_sigmoid"), 1)
                act.wait_ge(sem("gate_clamped"), w.up(sem("gate_clamped")))
                fn(cfg["e"], cfg["e"], ACT.Ln).then_inc(sem("log_gate"), 1)
                decay_attention(cfg)
            head_norm(HG_MIX, TMP, HG_HEADS)
            act.wait_ge(sem("x_ready"), w.up(sem("x_ready")))
            rms()
            peer(0)
            act.wait_ge(sem("x_ready"), w.up(sem("x_ready")))
            rms()
            evacuate("lru_in", LRU["y"], ACT.Gelu_apprx_tanh, first=8)
            act.wait_ge(sem("lam_negated"), w.up(sem("lam_negated")))
            fn(coef[:, 80:96], coef[:, 64:80], ACT.Abs).then_inc(sem("act_step"), 1)
            act.wait_ge(sem("act_step"), w.up(sem("act_step")))
            fn(coef[:, 80:96], coef[:, 80:96], ACT.Exp, scale=-1.0).then_inc(sem("act_step"), 1)
            act.wait_ge(sem("act_step"), w.up(sem("act_step")))
            fn(coef[:, 80:96], coef[:, 80:96], ACT.Ln, bias=c("ones", 0, 1)).then_inc(sem("softplus_ln"), 1)
            r0, n = STREAM_AT["lru_gates"]
            for i in range(n):
                d, kind, half = i // 4, (i // 2) % 2, i % 2
                act.wait_ge(tile_done, r0 + i + 1)
                for j in range(4):
                    m = half * 4 + j
                    ins = fn(LRU["gate"][d * 2 + kind][:, m * T:(m + 1) * T],
                             PA[:, half * 1024 + j * T:half * 1024 + (j + 1) * T], ACT.Sigmoid,
                             bias=p(("lru_b_a", "lru_b_x")[kind], d * DC + m, 1))
                ins.then_inc(sem("lru_gate_taken"), 1)
            for d in range(2):
                act.wait_ge(sem("log_a"), w.up(sem("log_a")))
                fn(LRU["a"], LRU["la"], ACT.Exp).then_inc(sem("lru_a"), 1)
                fn(LRU["m"], LRU["la"], ACT.Tanh, scale=-1.0).then_inc(sem("lru_tanh"), 1)
                act.wait_ge(sem("mult_square"), w.up(sem("mult_square")))
                fn(LRU["m"], LRU["m"], ACT.Sqrt).then_inc(sem("lru_mult"), 1)
            act.wait_ge(sem("x_ready"), w.up(sem("x_ready")))
            rms()
            peer(1)
            act.wait_ge(sem("x_ready"), w.up(sem("x_ready")))
            rms()
            act.wait_ge(sem("bias_rows_psum"), w.up(sem("bias_rows_psum")))
            fn(ROWS, PA[:, :], ACT.Identity).then_inc(sem("bias_rows_taken"), 1)
            act.wait_ge(sem("bias_rows_stored"), w.up(sem("bias_rows_stored"), 16))
            even_mixer()
            act.wait_ge(sem("x_ready"), w.up(sem("x_ready")))
            layer_norm()
            conv_ffn(0)
            act.wait_ge(sem("x_ready"), w.up(sem("x_ready")))
            layer_norm()
            odd_mixer()
            act.wait_ge(sem("x_ready"), w.up(sem("x_ready")))
            layer_norm()
            conv_ffn(1)
            act.wait_ge(sem("x_ready"), w.up(sem("x_ready")))
            layer_norm()

        @block.vector
        def _(dve):
            w = Tally()
            v = nc.vector
            tt, ts, stt = v.tensor_tensor, v.tensor_scalar, v.scalar_tensor_tensor

            def all_taken(name):
                q0, n = product_at[name]
                dve.wait_ge(taken, q0 + n)

            def loop(n, body):
                full = n // 8
                if full >= 2:
                    with dve.Fori(0, full) as it:
                        for i in range(8):
                            body(i, it)
                else:
                    full = 0
                for i in range(8 * full, n):
                    body(i, 0)

            def convolve(name, n, dst, weight, taps, shifts, bias):
                q0, r0 = product_at[name][0], STREAM_AT[name][0]
                s0, per = w.value(sem("conv_step")), len(shifts) - 1
                if q0 > 0:
                    dve.wait_ge(taken, q0)
                order = [taps.index(0)] + [i for i in range(len(taps)) if taps[i] != 0]

                def body(i, it):
                    dve.wait_ge(tile_done, it * 8 + (r0 + i + 1))
                    ps = product_slot(q0 + i)
                    for q, tap in enumerate(order):
                        sh = taps[tap]
                        wc = weight(tap)[:, bass.ds(it * 8 + i, 1)]
                        out_ = dst[:, bass.ds(it * (8 * T) + (i * T + max(0, -sh)), T - abs(sh))]
                        src = ps[:, max(0, sh):T - max(0, -sh)]
                        if q:
                            dve.wait_ge(sem("conv_step"), it * (8 * per) + (s0 + i * per + q))
                            ins = stt(out_, src, wc, out_, ALU.mult, ALU.add)
                        elif bias is None:
                            ins = ts(out_, src, wc, None, ALU.mult)
                        else:
                            ins = ts(out_, src, wc, bias[:, bass.ds(it * 8 + i, 1)], ALU.mult, ALU.add)
                        ins.then_inc(sem("conv_step") if q < per else taken, 1)

                loop(n, body)
                w.up(sem("conv_step"), n * per)

            def add_product(name, gate=None):
                q0, n = product_at[name]
                r0 = STREAM_AT[name][0]
                dve.wait_ge(taken, q0)
                for m in range(n):
                    dve.wait_ge(tile_done, r0 + m + 1)
                    add_chunk(m, product_slot(q0 + m), gate).then_inc(taken, 1)
                dve.wait_ge(taken, q0 + n)
                v.tensor_copy(stat[:, 15:16], X[:, 0:1]).then_inc(sem("x_ready"), 1)

            def add_chunk(m, src, gate):
                xm = X[:, m * T:(m + 1) * T]
                if gate is None:
                    return stt(xm, xm, ALPHA, src, ALU.mult, ALU.add)
                return stt(xm, src, gate[:, m:m + 1], xm, ALU.mult, ALU.add)

            def add_sums(stream, gate=None):
                r0, n = STREAM_AT[stream]
                dve.wait_ge(tile_done, r0 + n)
                for m in range(DC):
                    ins = add_chunk(m, PA[:, m * T:(m + 1) * T], gate)
                ins.then_inc(sem("x_ready"), 1)

            def modulation(layer, sub, part):
                at = (layer * 6 + sub * 3 + part) * DC
                return mod[:, at:at + DC]

            def gains(layer, sub):
                at = 8 + (layer * 2 + sub) * DC
                return coef[:, at:at + DC]

            def ada(first, last):
                def part(g):
                    for k in range(DC):
                        dve.wait_ge(ada_loaded[k], (g + 1) * 16)
                        dst = ADA_SUMS[:, bass.ds(g * D, D)]
                        src, cond = ADA_RING[:, k * TILE:(k + 1) * TILE], coef[:, k:k + 1]
                        if k:
                            dve.wait_ge(sem("ada_used"), g * DC + k)
                            ins = stt(dst, src, cond, dst, ALU.mult, ALU.add)
                        else:
                            ins = ts(dst, src, cond, None, ALU.mult)
                        ins.then_inc(sem("ada_used"), 1)
                    dve.wait_ge(sem("ada_used"), g * DC + DC)
                    v.tensor_copy(stat[:, 14:15], ADA_SUMS[:, 0:1]).then_inc(sem("ada_sums_ready"), 1)

                with dve.Fori(first, last) as g:
                    part(g)

            def modulate(first, last):
                dve.wait_ge(sem("ada_psum"), w.up(sem("ada_psum")))
                cols = slice(first * DC, last * DC)
                tt(mod[:, cols], PA[:, cols], p("b_ada", first * DC, (last - first) * DC), ALU.add)\
                    .then_inc(sem("dve_step"), 1)
                dve.wait_ge(sem("dve_step"), w.up(sem("dve_step")))
                for layer in range(2):
                    for sub in range(2):
                        if first <= layer * 6 + sub * 3 + 1 < last:
                            ins = stt(gains(layer, sub), modulation(layer, sub, 1), 1.0,
                                      p("norm_g", (layer * 2 + sub) * DC, DC), ALU.add, ALU.mult)
                ins.then_inc(sem("mod_ready"), 1)
                dve.wait_ge(sem("mod_ready"), w.up(sem("mod_ready")))

            def normalize(dst, gain, shift, name):
                dve.wait_ge(sem("root_ready"), w.up(sem("root_ready")))
                v.reciprocal(inv[:, :], inv[:, :]).then_inc(sem("dve_step"), 1)
                dve.wait_ge(sem("dve_step"), w.up(sem("dve_step")))
                tt(chunks(dst), chunks(X[:, :]), over(inv[:, :], DC), ALU.mult).then_inc(sem("dve_step"), 1)
                dve.wait_ge(sem("dve_step"), w.up(sem("dve_step")))
                for k in range(DC):
                    dk = dst[:, k * T:(k + 1) * T]
                    if shift is None:
                        ins = ts(dk, dk, gain[:, k:k + 1], None, ALU.mult)
                    else:
                        ins = ts(dk, dk, gain[:, k:k + 1], shift[:, k:k + 1], ALU.mult, ALU.add)
                if name == "x_normed":
                    ins.then_inc(sem("dve_step"), 1)
                    dve.wait_ge(sem("dve_step"), w.up(sem("dve_step")))
                    ins = v.tensor_copy(stat[:, 13:14], X[:, 0:1])
                ins.then_inc(sem(name), 1)

            def layer_norm(i):
                dve.wait_ge(sem("mean_ready"), w.up(sem("mean_ready")))
                tt(chunks(X[:, :]), chunks(X[:, :]), over(PA[:, 0:T], DC), ALU.subtract)\
                    .then_inc(sem("centered"), 1)
                dve.wait_ge(sem("centered"), w.up(sem("centered")))
                normalize(X[:, :], p("ln_g", i * DC, DC), p("ln_b", i * DC, DC), "x_normed")

            def head_norm(o, sq, n, gain, gate):
                dve.wait_ge(sem("head_roots"), w.up(sem("head_roots")))
                v.reciprocal(sq, sq).then_inc(sem("dve_step"), 1)
                dve.wait_ge(sem("dve_step"), w.up(sem("dve_step")))
                tt(o, o, sq, ALU.mult).then_inc(sem("dve_step"), 1)
                dve.wait_ge(sem("dve_step"), w.up(sem("dve_step")))
                if gate is not None:
                    dve.wait_ge(sem("gate_silu"), w.up(sem("gate_silu")))
                for h in range(n):
                    oh = o[:, h * T:(h + 1) * T]
                    if gate is None:
                        ins = ts(oh, oh, gain(h), 1.0 - LAM_INIT, ALU.mult, ALU.mult)
                    else:
                        ins = stt(oh, oh, gain(h), gate[:, h * T:(h + 1) * T], ALU.mult, ALU.mult)
                return ins

            def cumulate(cfg):
                for i in range(cfg["chunks"]):
                    ins = v.tensor_tensor_scan(cfg["b"][:, i * T:(i + 1) * T], wide(c("ones", 0, 1), P, T),
                                               cfg["e"][:, i * T:(i + 1) * T], 0.0, ALU.mult, ALU.add)
                ins.then_inc(sem("dve_step"), 1)
                dve.wait_ge(sem("dve_step"), w.up(sem("dve_step")))

            def decay_attention(cfg):
                b, e, k_, q_, kh, qh = (cfg[x] for x in ("b", "e", "k", "q", "kh", "qh"))
                per = cfg["heads"] // cfg["chunks"]
                nm = cfg["chunks"] * TT

                def by_rows(x, n):
                    return x.rearrange("p (r n c) -> p r n c", r=per, n=n)

                def diff(lev):
                    size = 2 << lev if lev < DIAGONAL else T
                    bv, ev = (x.rearrange("p (n l) -> p n l", l=size) for x in (b, e))
                    ref = bv[:, :, size // 2 - 1:size // 2]
                    tt(ev, bv, wide(ref, P, b.shape[1] // size, size), ALU.subtract)\
                        .then_inc(sem("decay_diff"), 1)

                v.memset(cfg["at"], 0.0).then_inc(sem("dve_step"), 1)
                dve.wait_ge(sem("dve_step"), w.up(sem("dve_step")))
                diff(0)
                for lev in range(CROSS + 1):
                    if lev != DIAGONAL:
                        dve.wait_ge(sem("decay_exp"), w.up(sem("decay_exp")))
                        tt(kh, k_, e, ALU.mult)
                        tt(qh, q_, e, ALU.mult).then_inc(sem("decay_keys_ready"), 1)
                        dve.wait_ge(sem("decay_keys_ready"), w.up(sem("decay_keys_ready")))
                        nxt = CROSS if lev == DIAGONAL - 1 else lev + 1
                        if lev < DIAGONAL:
                            diff(nxt)
                    dve.wait_ge(sem("decay_scores"), w.up(sem("decay_scores")))
                    src = (PB, PA)[lev % 2]
                    if lev == CROSS:
                        n = cfg["chunks"]
                        got = by_rows(src[:, :], 2048 // per // P)[:, :, 0:n, :]
                        v.tensor_copy(by_rows(cfg["ax"], n), got).then_inc(sem("decay_masked"), 1)
                    else:
                        mask = ident if lev == DIAGONAL else c("pairs", lev * P, P)
                        got = by_rows(src[:, :], 2048 // per // P)[:, :, 0:nm, :]
                        v.copy_predicated(by_rows(cfg["at"], nm),
                                          wide(mask.unsqueeze(1).unsqueeze(1), P, per, nm, P).bitcast(U32),
                                          got).then_inc(sem("decay_masked"), 1)
                    dve.wait_ge(sem("decay_masked"), w.up(sem("decay_masked")))
                dve.wait_ge(sem("decay_out"), w.up(sem("decay_out")))

            def top16(scores, spare, n, width, val, idx):
                def row(a, i):
                    return a[:, i * width:(i + 1) * width]
                for half in range(2):
                    src = spare if half else scores
                    for i in range(n):
                        ins = v.max(val[:, i * 16 + half * 8:i * 16 + half * 8 + 8], row(src, i))
                    ins.then_inc(sem("dve_step"), 1)
                    dve.wait_ge(sem("dve_step"), w.up(sem("dve_step")))
                    for i in range(n):
                        at = slice(i * 16 + half * 8, i * 16 + half * 8 + 8)
                        ins = v.max_index(idx[:, at], val[:, at], row(src, i))
                        if not half:
                            ins = v.match_replace(row(spare, i), val[:, at], row(src, i), -3e38)
                    ins.then_inc(sem("dve_step"), 1)
                    dve.wait_ge(sem("dve_step"), w.up(sem("dve_step")))

            def peer(layer):
                nh, hk = PEER_HEADS, PEER_HEADS * TOPK
                idx, cpos, high, low = (x.bitcast(U32) for x in (IDX, CPOS, HIGH, LOW))
                dve.wait_ge(sem("key_scores"), w.up(sem("key_scores"), TT))
                dve.wait_ge(sem("h_high"), w.up(sem("h_high")))
                tt(h_low[:, :], H[:, :], h_high[:, :].bitcast(F32), ALU.subtract)\
                    .then_inc(sem("h_split"), 1)
                for t in range(TT):
                    top16(KEY_SCORES[t], SPARE, 2 * nh, NKEYS, VAL, idx)
                    v.tensor_copy(IDX_F, idx).then_inc(sem("dve_step"), 1)
                    dve.wait_ge(sem("dve_step"), w.up(sem("dve_step")))
                    s = VAL.rearrange("p (h s a) -> p h s a", s=2, a=TOPK)
                    tt(CAND.rearrange("p (h a b) -> p h a b", a=TOPK, b=TOPK),
                       wide(s[:, :, 0, :].unsqueeze(3), P, nh, TOPK, TOPK),
                       wide(s[:, :, 1, :].unsqueeze(2), P, nh, TOPK, TOPK), ALU.add).then_inc(sem("dve_step"), 1)
                    dve.wait_ge(sem("dve_step"), w.up(sem("dve_step")))
                    top16(CAND, CAND_SPARE, nh, TOPK * TOPK, CVAL, cpos)
                    v.tensor_scalar(high, cpos, 4, None, ALU.logical_shift_right)
                    v.tensor_scalar(low, cpos, 15, None, ALU.bitwise_and).then_inc(sem("dve_step"), 1)
                    dve.wait_ge(sem("dve_step"), w.up(sem("dve_step")))
                    v.tensor_copy(HIGH_F, high)
                    v.tensor_copy(LOW_F, low).then_inc(sem("dve_step"), 1)
                    dve.wait_ge(sem("dve_step"), w.up(sem("dve_step")))
                    ids = IDX_F.rearrange("p (h s a) -> p h s a", s=2, a=TOPK)
                    for side, rank in enumerate((HIGH_F, LOW_F)):
                        pick = PICK.rearrange("p (n a) -> p n a", a=TOPK)
                        tt(pick, wide(rank.unsqueeze(2), P, hk, TOPK), over(c("iota16"), hk),
                           ALU.is_equal).then_inc(sem("dve_step"), 1)
                        dve.wait_ge(sem("dve_step"), w.up(sem("dve_step")))
                        pick4 = PICK.rearrange("p (h k a) -> p h k a", k=TOPK, a=TOPK)
                        tt(pick4, pick4, wide(ids[:, :, side, :].unsqueeze(2), P, nh, TOPK, TOPK),
                           ALU.mult).then_inc(sem("dve_step"), 1)
                        dve.wait_ge(sem("dve_step"), w.up(sem("dve_step")))
                        v.tensor_reduce(chosen(t, side), pick, AX.X, ALU.add).then_inc(sem("dve_step"), 1)
                        dve.wait_ge(sem("dve_step"), w.up(sem("dve_step")))
                    cv = CVAL.rearrange("p (h k) -> p h k", k=TOPK)
                    gt = GATE.rearrange("p (h k) -> p h k", k=TOPK)
                    tt(gt, cv, wide(cv[:, :, 0:1], P, nh, TOPK), ALU.subtract).then_inc(sem("gate_diff"), 1)
                    dve.wait_ge(sem("gate_exp"), w.up(sem("gate_exp")))
                    v.tensor_reduce(GSUM, gt, AX.X, ALU.add).then_inc(sem("dve_step"), 1)
                    dve.wait_ge(sem("dve_step"), w.up(sem("dve_step")))
                    v.reciprocal(GSUM, GSUM).then_inc(sem("dve_step"), 1)
                    dve.wait_ge(sem("dve_step"), w.up(sem("dve_step")))
                    tt(chosen(t, 2).rearrange("p (h k) -> p h k", k=TOPK), gt,
                       wide(GSUM.unsqueeze(2), P, nh, TOPK), ALU.mult).then_inc(sem("chosen_ready"), 1)
                dve.wait_ge(sem("slots_ready"), w.up(sem("slots_ready")))
                g0 = layer * 64

                def group(r, it):
                    if not isinstance(it, int) or g0 + r >= 2:
                        dve.wait_ge(sem("gates_psum"), it * 4 + (g0 + r - 1))
                    for j in range(4):
                        at = ((r % 2) * 4 + j) * P
                        tok = it * 16 + (r * 4 + j)
                        ts(onehot_a[:, at:at + P], c("iota"), slots[:, bass.ds(tok, 1)],
                           slots[:, bass.ds(tok + 2 * T, 1)], ALU.is_equal, ALU.mult)
                        ins = ts(onehot_b[:, at:at + P], c("iota"), slots[:, bass.ds(tok + T, 1)],
                                 None, ALU.is_equal)
                    ins.then_inc(sem("onehots_ready"), 1)

                gates = chunks(BIG[:, :])

                def fold(g, it):
                    dve.wait_ge(sem("gates_copied"), it * 4 + (g0 + g + 1))
                    dst = gates[:, MAIN:, bass.ds(it * 16 + g * 4, 4)]
                    bank = PA[:, (g % 4) * 512:(g % 4 + 1) * 512]
                    tt(dst, bank.rearrange("p (t j) -> p j t", t=4)[:, MAIN:, :], dst, ALU.mult)\
                        .then_inc(sem("gates_folded"), 1)

                dve.wait_ge(sem("early_gelu"), (layer + 1) * EARLY)
                for r in range(4):
                    group(r, 0)
                    if r >= 2:
                        fold(r - 2, 0)
                with dve.Fori(1, 16) as it:
                    for r in range(4):
                        group(r, it)
                        fold(r - 2, it)
                fold(62, 0)
                fold(63, 0)
                r0, n = STREAM_AT[f"experts{layer}"]
                dve.wait_ge(sem("gates_psum"), g0 + 64)

                def low(k, it=0, step=8):
                    n = r0 + k
                    for b in range(2):
                        dve.wait_ge(sem("high_ready"), it * (2 * step) + (split_at(layer, k) + b + 1))
                        at = (n % RING) * TILE + b * HALF
                        tt(tile_half(w_low, k, b), ring[:, at:at + HALF], tile_half(w_high, k, b).bitcast(F32),
                           ALU.subtract).then_inc(sem("low_ready"), 1)

                def split_gated(j, a, it=0, step=4):
                    if j >= 2:
                        dve.wait_ge(tile_done, it * step + (r0 + down_at(j - 2) + 1))
                    v.tensor_copy(pair(a_high, j), a).then_inc(sem("gated_high"), 1)
                    dve.wait_ge(sem("gated_high"), it * 4 + (layer * NKEYS + j + 1))
                    tt(pair(a_low, j), a, pair(a_high, j).bitcast(F32), ALU.subtract)\
                        .then_inc(sem("gated_ready"), 1)

                def gated(j, it=0):
                    dve.wait_ge(sem("gelu_ready"), it * 4 + (layer * MAIN + j + 1))
                    a = pair(act_v, j)
                    tt(a, a, BIG[:, bass.ds(it * (4 * T) + j * T, T)], ALU.mult).then_inc(sem("gated"), 1)
                    dve.wait_ge(sem("gated"), it * 4 + (layer * MAIN + j + 1))
                    split_gated(j, a, it, 8)

                def column(j, it=0):
                    low(2 * j, it)
                    low(2 * j + 1, it)
                    gated(j, it)

                def late(j, it=0):
                    low(down_at(j), it, 4)
                    split_gated(j, BIG[:, bass.ds(it * (4 * T) + j * T, T)], it)

                low(0)
                low(1)
                low(2)
                gated(0)
                low(3)
                gated(1)
                steps = (MAIN - 2) // 4
                with dve.Fori(0, steps) as it:
                    for j in range(2, 6):
                        column(j, it)
                for j in range(4 * steps + 2, MAIN):
                    column(j)
                for j in range(MAIN, MAIN + 2):
                    late(j)
                steps = (EARLY - 2) // 4
                with dve.Fori(0, steps) as it:
                    for j in range(MAIN + 2, MAIN + 6):
                        late(j, it)
                for j in range(MAIN + 2 + 4 * steps, NKEYS):
                    late(j)
                add_sums(f"late{layer}", modulation(layer, 1, 2))

            def conv_ffn(i):
                wt = [p("ffn_conv_w", i * 132 + tap * 44, 44) for tap in range(3)]
                convolve(f"up{i}", 2 * FC, BIG[:, :], lambda tap: wt[tap], [-2, -1, 0], [0] * 3,
                         p("ffn_conv_b", i * 44, 44))
                all_taken(f"up{i}")
                dve.wait_ge(sem("gate_silu"), w.up(sem("gate_silu")))
                tt(big(0, FC * T), big(0, FC * T), big(FC * T, FC * T), ALU.mult)\
                    .then_inc(sem("ffn_hidden_ready"), 1)
                add_sums(f"down{i}")

            def attend(kind, e):
                groups = 3 if kind == "swa" else 2
                pr = chunks(e["prob"])
                for h in range(4):
                    for t in range(TT):
                        dve.wait_ge(sem("attention_scores"), w.up(sem("attention_scores")))
                        bias = over(e["bias"][:, (t * 4 + h) * T:(t * 4 + h + 1) * T], groups)
                        src = chunks(PA[:, 0:3 * T]) if kind == "swa" else chunks(PA[:, 0:1024], 512)[:, :, 0:T]
                        stt(pr, src, SWA_DH ** -0.5, bias, ALU.mult, ALU.add)\
                            .then_inc(sem("attention_scores_taken"), 1)
                        dve.wait_ge(sem("attention_scores_taken"), w.up(sem("attention_scores_taken")))
                        if kind == "swa":
                            tt(e["prob"], e["prob"], e["neg"][:, t * 3 * T:(t + 1) * 3 * T], ALU.add).then_inc(sem("dve_step"), 1)
                            dve.wait_ge(sem("dve_step"), w.up(sem("dve_step")))
                            v.reduce_max(stat[:, 0:1], e["prob"], AX.X).then_inc(sem("dve_step"), 1)
                            dve.wait_ge(sem("dve_step"), w.up(sem("dve_step")))
                            n = 1
                        else:
                            tt(pr, pr, over(e["neg"][:, t * T:(t + 1) * T], 2), ALU.add).then_inc(sem("dve_step"), 1)
                            dve.wait_ge(sem("dve_step"), w.up(sem("dve_step")))
                            v.reduce_max(stat[:, 0:2], pr, AX.X).then_inc(sem("dve_step"), 1)
                            dve.wait_ge(sem("dve_step"), w.up(sem("dve_step")))
                            n = 2
                        ts(stat[:, 0:n], stat[:, 0:n], -1.0, None, ALU.mult).then_inc(sem("attention_max"), 1)
                        dve.wait_ge(sem("attention_exp"), w.up(sem("attention_exp"), n))
                        v.reciprocal(stat[:, 2:2 + n], stat[:, 2:2 + n]).then_inc(sem("dve_step"), 1)
                        dve.wait_ge(sem("dve_step"), w.up(sem("dve_step")))
                        if kind == "swa":
                            ts(e["prob"], e["prob"], stat[:, 2:3], None, ALU.mult)\
                                .then_inc(sem("attention_weights"), 1)
                        else:
                            tt(stat[:, 3:4], stat[:, 3:4], stat[:, 4:5], ALU.mult).then_inc(sem("dve_step"), 1)
                            dve.wait_ge(sem("dve_step"), w.up(sem("dve_step")))
                            ts(pr[:, 0, :], pr[:, 0, :], stat[:, 2:3], None, ALU.mult).then_inc(sem("dve_step"), 1)
                            dve.wait_ge(sem("dve_step"), w.up(sem("dve_step")))
                            stt(pr[:, 0, :], pr[:, 1, :], stat[:, 3:4], pr[:, 0, :], ALU.mult, ALU.add)\
                                .then_inc(sem("attention_weights"), 1)

            def even_mixer():
                e = EVEN
                dve.wait_ge(sem("bias_rows_stored"), w.up(sem("bias_rows_stored"), 16))
                convolve("even_in", 18, BIG[:, :],
                         lambda tap: p("gdn_conv_w", tap * 18, 18), [-3, -2, -1, 0], [0] * 4, None)
                dve.wait_ge(sem("ba_psum"), w.up(sem("ba_psum")))
                for t in range(TT):
                    ins = v.tensor_copy(e["ba"][:, t * 12:(t + 1) * 12], PB[:, t * 512:t * 512 + 12])
                ins.then_inc(sem("dve_step"), 1)
                dve.wait_ge(sem("dve_step"), w.up(sem("dve_step")))
                ba = e["ba"].rearrange("p (t n) -> p t n", t=2)
                tt(e["t0"].rearrange("p (t n) -> p t n", t=2), ba[:, :, 6:12],
                   over(p("gdn_dt_bias", 0, 6), TT), ALU.add).then_inc(sem("ba_ready"), 1)
                dve.wait_ge(sem("ba_ready"), w.up(sem("ba_ready")))
                for i, (x, y) in enumerate((("q", "x"), ("k", "y"))):
                    dve.wait_ge(sem("qk_roots"), w.up(sem("qk_roots")))
                    v.reciprocal(e[y], e[y]).then_inc(sem("dve_step"), 1)
                    dve.wait_ge(sem("dve_step"), w.up(sem("dve_step")))
                    if i == 0:
                        ins = stt(e["q"], e["q"], float(P) ** -0.5, e[y], ALU.mult, ALU.mult)
                        ins.then_inc(sem("dve_step"), 1)
                        dve.wait_ge(sem("dve_step"), w.up(sem("dve_step")))
                    else:
                        tt(e["k"], e["k"], e[y], ALU.mult).then_inc(sem("qk_normed"), 1)
                        dve.wait_ge(sem("qk_normed"), w.up(sem("qk_normed")))
                dve.wait_ge(sem("softplus_ln"), w.up(sem("softplus_ln")))
                stt(e["t0"], e["t0"], 0.0, e["t1"], ALU.max, ALU.add).then_inc(sem("dve_step"), 1)
                dve.wait_ge(sem("dve_step"), w.up(sem("dve_step")))
                dve.wait_ge(sem("a_ready"), w.up(sem("a_ready")))
                g2 = e["g"].rearrange("p (t n) -> p t n", t=2)
                stt(g2, e["t0"].rearrange("p (t n) -> p t n", t=2), -1.0, over(e["ea"], 2),
                    ALU.mult, ALU.mult).then_inc(sem("dve_step"), 1)
                dve.wait_ge(sem("dve_step"), w.up(sem("dve_step")))
                dve.wait_ge(sem("beta_ready"), w.up(sem("beta_ready")))
                ts(e["nbeta"], e["beta"], -1.0, None, ALU.mult).then_inc(sem("g_ready"), 1)
                dve.wait_ge(sem("g_ready"), w.up(sem("g_ready")))
                dve.wait_ge(sem("gam_col_psum"), w.up(sem("gam_col_psum")))
                for t in range(TT):
                    ins = v.tensor_copy(e["gam"][:, t * 6:t * 6 + 6], PB[:, 1024 + t * 8:1024 + t * 8 + 6])
                ins.then_inc(sem("dve_step"), 1)
                dve.wait_ge(sem("dve_step"), w.up(sem("dve_step")))
                for h in range(GDN_HEADS):
                    dve.wait_ge(sem("gam_row_psum"), w.up(sem("gam_row_psum")))
                    src, dt = PB[:, (h % 2) * 512:(h % 2) * 512 + T], e["dt"][:, h * 384:(h + 1) * 384]
                    ts(dt[:, 0:T], src, e["gam"][:, h:h + 1], 0.0, ALU.subtract, ALU.min)
                    ts(dt[:, T:T + P], src[:, P:T], e["gam"][:, 6 + h:7 + h], 0.0, ALU.subtract, ALU.min)\
                        .then_inc(sem("decay_taken"), 1)
                    dve.wait_ge(sem("decay_taken"), w.up(sem("decay_taken")))
                    v.tensor_copy(stat[:, 12:13], dt[:, 0:1]).then_inc(sem("decay_diff_h"), 1)
                dve.wait_ge(sem("gdn_decay"), w.up(sem("gdn_decay"), GDN_HEADS))
                dts = e["dt"].rearrange("p (h c) -> p h c", h=GDN_HEADS)
                up_incl = over(c("tri"), GDN_HEADS)
                mt = e["mt"].rearrange("p (h t c) -> p h t c", t=TT, c=P)
                for i in range(2):
                    for j in range(3):
                        n = i * 3 + j
                        dve.wait_ge(sem("pair_psum"), w.up(sem("pair_psum")))
                        src = chunks((PA, PB)[n % 2][:, 0:6 * P], P)
                        dcy = dts[:, :, j * P:(j + 1) * P]
                        if i == 0:
                            dst = chunks(e["m01"], P) if j == 1 else mt[:, :, 0 if j == 0 else 1, :]
                        else:
                            dst = chunks((e["qk0"], e["qk01"], e["qk1"])[j], P)
                        ins = tt(dst, src, dcy, ALU.mult)
                        if j != 1:
                            ins.then_inc(sem("dve_step"), 1)
                            dve.wait_ge(sem("dve_step"), w.up(sem("dve_step")))
                            ins = tt(dst, dst, up_incl, ALU.mult)
                            if i == 0:
                                ins.then_inc(sem("dve_step"), 1)
                                dve.wait_ge(sem("dve_step"), w.up(sem("dve_step")))
                                ins = tt(dst, dst, over(c("strict"), GDN_HEADS), ALU.mult)
                        ins.then_inc(sem("pair_taken"), 1)
                dve.wait_ge(sem("pair_taken"), w.up(sem("pair_taken"), 6))
                n3, nt3, x3, y3, c3, ct3 = (chunks(e[k], P) for k in ("n", "nt", "x", "y", "c", "ct"))
                dve.wait_ge(sem("low_masks_loaded"), w.up(sem("low_masks_loaded"), 16))
                dve.wait_ge(sem("n_ready"), w.up(sem("n_ready")))
                dve.wait_ge(sem("nt_ready"), w.up(sem("nt_ready")))

                def blocks(lev):
                    tt(c3, n3, over(e["low"][:, lev * P:(lev + 1) * P], 12), ALU.mult)
                    return tt(ct3, nt3, over(c("pairs", lev * P, P), 12), ALU.mult)

                blocks(0).then_inc(sem("dve_step"), 1)
                dve.wait_ge(sem("dve_step"), w.up(sem("dve_step")))
                tt(x3, over(ident, 12), c3, ALU.subtract)
                tt(y3, over(ident, 12), ct3, ALU.subtract).then_inc(sem("dve_step"), 1)
                dve.wait_ge(sem("dve_step"), w.up(sem("dve_step")))
                for lev in range(1, PAIR_LEVELS):
                    blocks(lev).then_inc(sem("block_ready"), 1)
                    dve.wait_ge(sem("block_ready"), w.up(sem("block_ready")))
                    dve.wait_ge(sem("inv_xpx"), w.up(sem("inv_xpx")))
                    dve.wait_ge(sem("inv_ypy"), w.up(sem("inv_ypy")))
                    tt(e["x"], e["x"], PA[:, 0:12 * P], ALU.subtract)
                    ins = tt(e["y"], e["y"], PB[:, 0:12 * P], ALU.subtract)
                    if lev < PAIR_LEVELS - 1:
                        ins.then_inc(sem("dve_step"), 1)
                        dve.wait_ge(sem("dve_step"), w.up(sem("dve_step")))
                ins.then_inc(sem("inverse_ready"), 1)
                dve.wait_ge(sem("carry_psum"), w.up(sem("carry_psum")))
                vt = e["vt"].rearrange("p (h t c) -> p h t c", t=TT, c=P)
                for h in range(GDN_HEADS):
                    ins = stt(e["r1"][:, h * P:(h + 1) * P], PB[:, h * P:(h + 1) * P],
                              e["nbeta"][:, 6 + h:7 + h], vt[:, h, 1, :], ALU.mult, ALU.add)
                ins.then_inc(sem("carry_ready"), 1)
                head_norm(e["mix"][:, 0:6 * T], e["sq"], 6, lambda h: p("gdn_norm_w"), e["z"])\
                    .then_inc(sem("gdn_done"), 1)
                dve.wait_ge(sem("attention_tables_loaded"), w.up(sem("attention_tables_loaded"), 48))
                attend("swa", e)
                dve.wait_ge(sem("attention_done"), w.up(sem("attention_done")))
                add_product("even_out")

            def odd_mixer():
                e = ODD
                dve.wait_ge(sem("gate_psum"), w.up(sem("gate_psum")))
                for i in range(2):
                    ins = ts(e["g1"][:, i * T:(i + 1) * T], PB[:, 512 + i * 512:512 + i * 512 + T],
                             p("gla_b_gate", i, 1), None, ALU.add)
                ins.then_inc(sem("gate_taken"), 1)
                dve.wait_ge(sem("gate_taken"), w.up(sem("gate_taken")))
                all_taken("odd_in")
                dve.wait_ge(sem("softplus_ln"), w.up(sem("softplus_ln")))
                stt(e["g1"], e["g1"], 0.0, e["g2"], ALU.min, ALU.subtract).then_inc(sem("dve_step"), 1)
                dve.wait_ge(sem("dve_step"), w.up(sem("dve_step")))
                ts(GLA["e"], e["g1"], 1.0 / GLA_TAU, None, ALU.mult)
                ts(GLA["q"], GLA["q"], GLA_DK ** -0.5, None, ALU.mult).then_inc(sem("dve_step"), 1)
                dve.wait_ge(sem("dve_step"), w.up(sem("dve_step")))
                cumulate(GLA)
                decay_attention(GLA)
                o = e["mix"][:, 4 * T:8 * T]
                v.tensor_copy(o, PA[:, 0:4 * T]).then_inc(sem("heads_ready"), 1)
                dve.wait_ge(sem("heads_ready"), w.up(sem("heads_ready")))
                head_norm(o, e["sq"], 4, lambda h: p("gla_norm_w"), e["r"]).then_inc(sem("dve_step"), 1)
                dve.wait_ge(sem("dve_step"), w.up(sem("dve_step")))
                dve.wait_ge(sem("attention_tables_loaded"), w.up(sem("attention_tables_loaded"), 64))
                lv = e["lamv"].rearrange("p (a b c) -> p a b c", a=2, b=2)
                tt(lv[:, :, 0, :], lv[:, :, 0, :], lv[:, :, 1, :], ALU.mult).then_inc(sem("dve_step"), 1)
                dve.wait_ge(sem("dve_step"), w.up(sem("dve_step")))
                v.tensor_reduce(stat[:, 6:8], lv[:, :, 0, :], AX.X, ALU.add).then_inc(sem("lam_sums"), 1)
                dve.wait_ge(sem("lam_exp"), w.up(sem("lam_exp")))
                tt(stat[:, 4:5], stat[:, 9:10], stat[:, 8:9], ALU.subtract).then_inc(sem("dve_step"), 1)
                dve.wait_ge(sem("dve_step"), w.up(sem("dve_step")))
                ts(stat[:, 4:5], stat[:, 4:5], -LAM_INIT, None, ALU.add).then_inc(sem("dve_step"), 1)
                dve.wait_ge(sem("dve_step"), w.up(sem("dve_step")))
                attend("diff", e)
                head_norm(e["mix"][:, 0:4 * T], e["sq"], 4, lambda h: p("diff_norm_w"), None).then_inc(sem("dve_step"), 1)
                dve.wait_ge(sem("dve_step"), w.up(sem("dve_step")))
                v.tensor_copy(stat[:, 11:12], e["mix"][:, 0:1]).then_inc(sem("mix_ready"), 1)
                add_product("odd_out")

            dve.wait_ge(sem("params_loaded"), w.up(sem("params_loaded"), 16))
            dve.wait_ge(sem("consts_loaded"), w.up(sem("consts_loaded"), 16))
            lb, om = coef[:, 40:48], coef[:, 48:56]
            tt(lb, p("hg_lb"), p("hg_lb"), ALU.subtract).then_inc(sem("lb_shifted"), 1)
            dve.wait_ge(sem("lb_exp"), w.up(sem("lb_exp")))
            v.reciprocal(om, lb).then_inc(sem("dve_step"), 1)
            dve.wait_ge(sem("dve_step"), w.up(sem("dve_step")))
            tt(lb, lb, om, ALU.mult).then_inc(sem("dve_step"), 1)
            dve.wait_ge(sem("dve_step"), w.up(sem("dve_step")))
            tt(lb, lb, lb, ALU.subtract).then_inc(sem("dve_step"), 1)
            dve.wait_ge(sem("dve_step"), w.up(sem("dve_step")))
            ts(om, lb, -1.0, 1.0, ALU.mult, ALU.add).then_inc(sem("dve_step"), 1)
            dve.wait_ge(sem("dve_step"), w.up(sem("dve_step")))
            dve.wait_ge(sem("cond_ready"), w.up(sem("cond_ready")))
            ada(0, 2)
            modulate(0, 2)
            dve.wait_ge(sem("x_loaded"), w.up(sem("x_loaded"), 16))
            normalize(H[:, :], gains(0, 0), modulation(0, 0, 0), "h_ready")
            ada(2, 12)
            all_taken("hg_in")
            for d in range(2):
                cfg = HG[d]
                if d == 1:
                    v.tensor_copy(chunks(cfg["q"]), chunks(HG[0]["q"])[:, :, ::-1])
                dve.wait_ge(sem("gate_sigmoid"), w.up(sem("gate_sigmoid")))
                if d == 1:
                    v.tensor_copy(chunks(cfg["v"]), chunks(HG[0]["v"])[:, :, ::-1])\
                        .then_inc(sem("decay_v_ready"), 1)
                for m in range(DC):
                    s_ = slice(m * T, (m + 1) * T)
                    ins = ts(cfg["k"][:, s_], cfg["e"][:, s_], om[:, m:m + 1], lb[:, m:m + 1],
                             ALU.mult, ALU.add)
                ins.then_inc(sem("dve_step"), 1)
                dve.wait_ge(sem("dve_step"), w.up(sem("dve_step")))
                ts(cfg["e"], cfg["k"], 2.0 ** -63, None, ALU.max).then_inc(sem("gate_clamped"), 1)
                ts(cfg["k"], cfg["k"], -1.0, 1.0, ALU.mult, ALU.add)
                dve.wait_ge(sem("log_gate"), w.up(sem("log_gate")))
                cumulate(cfg)
                if d == 0:
                    modulate(2, 12)
                decay_attention(cfg)
                if d == 0:
                    v.tensor_copy(HG_MIX, PA[:, :]).then_inc(sem("decay_out_taken"), 1)
                    dve.wait_ge(sem("decay_out_taken"), w.up(sem("decay_out_taken")))
                else:
                    tt(chunks(HG_MIX), chunks(HG_MIX), chunks(PA[:, :])[:, :, ::-1], ALU.add)\
                        .then_inc(sem("heads_ready"), 1)
                    dve.wait_ge(sem("heads_ready"), w.up(sem("heads_ready")))
            head_norm(HG_MIX, TMP, HG_HEADS, lambda h: p("hg_norm_g", h, 1), HG_G)\
                .then_inc(sem("mix_ready"), 1)
            add_product("hg_out", modulation(0, 0, 2))
            normalize(H[:, :], gains(0, 1), modulation(0, 1, 0), "h_ready")
            peer(0)
            normalize(H[:, :], gains(1, 0), modulation(1, 0, 0), "h_ready")
            nlam, ln1, rate = coef[:, 64:80], coef[:, 80:96], coef[:, 96:112]
            ts(nlam, p("lru_lam"), -1.0, None, ALU.mult).then_inc(sem("lam_negated"), 1)
            convolve("lru_in", DC, LRU["xc"], lambda tap: p("lru_conv_w", tap * DC, DC),
                     [-2, -1, 0, 1], [0] * 4, p("lru_conv_b"))
            dve.wait_ge(sem("lam_negated"), w.up(sem("lam_negated")))
            dve.wait_ge(sem("softplus_ln"), w.up(sem("softplus_ln")))
            stt(rate, nlam, 0.0, ln1, ALU.max, ALU.add).then_inc(sem("dve_step"), 1)
            dve.wait_ge(sem("dve_step"), w.up(sem("dve_step")))
            ts(rate, rate, -LRU_C, None, ALU.mult).then_inc(sem("dve_step"), 1)
            dve.wait_ge(sem("dve_step"), w.up(sem("dve_step")))
            dve.wait_ge(sem("lru_gate_taken"), w.up(sem("lru_gate_taken"), 8))
            all_taken("lru_in")
            for d in range(2):
                la, a, m_, h_ = LRU["la"], LRU["a"], LRU["m"], (LRU["h0"], LRU["h1"])[d]
                for m in range(DC):
                    s_ = slice(m * T, (m + 1) * T)
                    ins = ts(la[:, s_], LRU["gate"][2 * d][:, s_], rate[:, d * DC + m:d * DC + m + 1],
                             None, ALU.mult)
                ins.then_inc(sem("log_a"), 1)
                dve.wait_ge(sem("lru_a"), w.up(sem("lru_a")))
                dve.wait_ge(sem("lru_tanh"), w.up(sem("lru_tanh")))
                tt(la, a, a, ALU.mult).then_inc(sem("dve_step"), 1)
                dve.wait_ge(sem("dve_step"), w.up(sem("dve_step")))
                stt(m_, la, 1.0, m_, ALU.add, ALU.mult).then_inc(sem("mult_square"), 1)
                dve.wait_ge(sem("mult_square"), w.up(sem("mult_square")))
                tt(la, LRU["gate"][2 * d + 1], LRU["xc"], ALU.mult).then_inc(sem("dve_step"), 1)
                dve.wait_ge(sem("dve_step"), w.up(sem("dve_step")))
                dve.wait_ge(sem("lru_mult"), w.up(sem("lru_mult")))
                tt(m_, m_, la, ALU.mult).then_inc(sem("dve_step"), 1)
                dve.wait_ge(sem("dve_step"), w.up(sem("dve_step")))
                for m in range(DC):
                    s_ = slice(m * T, (m + 1) * T)
                    a1, u1, h1 = a[:, s_], m_[:, s_], h_[:, s_]
                    if d:
                        a1, u1, h1 = a1[:, ::-1], u1[:, ::-1], h1[:, ::-1]
                    ins = v.tensor_tensor_scan(h1, a1, u1, 0.0, ALU.mult, ALU.add)
                ins.then_inc(sem("dve_step"), 1)
                dve.wait_ge(sem("dve_step"), w.up(sem("dve_step")))
            tt(LRU["h0"], LRU["h0"], LRU["h1"], ALU.add).then_inc(sem("dve_step"), 1)
            dve.wait_ge(sem("dve_step"), w.up(sem("dve_step")))
            tt(LRU["h0"], LRU["h0"], LRU["y"], ALU.mult).then_inc(sem("mix_ready"), 1)
            add_product("lru_out", modulation(1, 0, 2))
            normalize(H[:, :], gains(1, 1), modulation(1, 1, 0), "h_ready")
            peer(1)
            dve.wait_ge(sem("x_ready"), w.up(sem("x_ready"), 4))
            normalize(X[:, :], p("final_g"), None, "x_normed")
            dve.wait_ge(sem("x_normed"), w.up(sem("x_normed")))
            even_mixer()
            layer_norm(0)
            dve.wait_ge(sem("x_normed"), w.up(sem("x_normed")))
            conv_ffn(0)
            layer_norm(1)
            dve.wait_ge(sem("x_normed"), w.up(sem("x_normed")))
            odd_mixer()
            layer_norm(2)
            dve.wait_ge(sem("x_normed"), w.up(sem("x_normed")))
            conv_ffn(1)
            layer_norm(3)
            dve.wait_ge(sem("x_normed"), w.up(sem("x_normed")))
            v.tensor_copy(stat[:, 12:13], X[:, 0:1]).then_inc(sem("result_ready"), 1)

        @block.gpsimd
        def _(pool):
            w = Tally()

            def load_ada(k, g):
                pool.dma_start(ADA_RING[:, k * TILE:(k + 1) * TILE], ada_in[g, k])\
                    .then_inc(ada_loaded[k], 16)

            for k in range(DC):
                load_ada(k, 0)
            with pool.Fori(1, 12) as g:
                for k in range(DC):
                    pool.wait_ge(sem("ada_used"), g * DC + (k - DC + 1))
                    load_ada(k, g)

            def attention_bias(dst, n_tiles=TT):
                for t in range(n_tiles):
                    src = bass.AP(skew.tensor, 255 - P * t, [[4 * SKEW - 1, P], [SKEW, 4], [1, T]])
                    pool.dma_start(dst[:, t * 4 * T:(t + 1) * 4 * T].rearrange("p (h k) -> p h k", h=4),
                                   src).then_inc(sem("attention_tables_loaded"), 16)

            e = EVEN
            pool.wait_ge(sem("x_normed"), w.up(sem("x_normed")))
            pool.dma_start(REL, bias_in).then_inc(sem("bias_loaded"), 16)
            pool.dma_start(ONEHOT, masks_in[:, MASK_BUCKET:MASK_BUCKET + SKEW])\
                .then_inc(sem("bias_loaded"), 16)
            pool.dma_start(e["low"], masks_in[:, MASK_LOW:MASK_LOW + PAIR_LEVELS * P])\
                .then_inc(sem("low_masks_loaded"), 16)
            pool.wait_ge(sem("bias_rows_taken"), w.up(sem("bias_rows_taken")))
            pool.dma_start(skew, ROWS).then_inc(sem("bias_rows_stored"), 16)
            pool.wait_ge(sem("bias_rows_stored"), w.up(sem("bias_rows_stored"), 16))
            pool.wait_ge(sem("gdn_out_psum"), w.up(sem("gdn_out_psum")))
            attention_bias(e["bias"])
            pool.dma_start(e["neg"], masks_in[:, MASK_SWA:MASK_SWA + 6 * T])\
                .then_inc(sem("attention_tables_loaded"), 16)
            pool.wait_ge(sem("x_normed"), w.up(sem("x_normed"), 2))
            e = ODD
            attention_bias(e["bias"])
            pool.dma_start(e["neg"], masks_in[:, MASK_CAUSAL:MASK_CAUSAL + 2 * T])\
                .then_inc(sem("attention_tables_loaded"), 16)
            pool.dma_start(e["lamv"], lam_in).then_inc(sem("attention_tables_loaded"), 16)


def constants():
    i = np.arange(P)
    s, t = i[:, None], i[None, :]
    eye = np.eye(P)
    ones = np.ones((P, P))
    pairs = [((s >> (l + 1)) == (t >> (l + 1))) & (((s >> l) & 1) == 0) & (((t >> l) & 1) == 1)
             for l in range(PAIR_LEVELS)]
    parts = {
        "ident": eye, "ones": ones, "mean_d": ones / D, "mean_head": ones / P,
        "iota": np.tile(i, (P, 1)), "iota16": np.tile(np.arange(TOPK), (P, 1)),
        "tri": s <= t, "strict": s < t, "pairs": np.concatenate(pairs, 1),
        "eps": np.tile([1e-6, 1e-5], (P, 1)), "zero": np.zeros((P, P)),
    }
    consts = np.concatenate([np.asarray(parts[n], np.float32) for n, _ in CONSTS], 1)
    q, k = np.arange(T)[:, None], np.arange(T)[None, :]
    dist = q - k
    swa = np.zeros((TT, P, SWA_GROUPS, T), np.float32)
    for g, (window, dil) in enumerate(SWA_CONFIGS):
        ok = (dist >= 0) & (dist % dil == 0) & (dist // dil <= window // dil)
        swa[:, :, g] = np.where(ok, 0.0, NEG).reshape(TT, P, T)
    causal = np.where(dist >= 0, 0.0, NEG).reshape(TT, P, T)
    dd = np.maximum(255 - np.arange(SKEW), 0)
    exact = NUM_BUCKETS // 2
    f = np.float32
    large = exact + (np.log(np.maximum(dd, 1).astype(f) / f(exact)) / f(math.log(REL_MAX / exact))
                     * f(NUM_BUCKETS - exact)).astype(np.int32)
    bucket = np.where(dd < exact, dd, np.minimum(large, NUM_BUCKETS - 1))
    onehot = np.zeros((P, SKEW), np.float32)
    onehot[bucket, np.arange(SKEW)] = 1
    low = np.concatenate([m.T for m in pairs], 1)
    masks = np.concatenate([low, swa.transpose(1, 0, 2, 3).reshape(P, -1),
                            causal.transpose(1, 0, 2).reshape(P, -1), onehot], 1)
    return consts, np.ascontiguousarray(masks, np.float32)


def tiles_of(w):
    k, m = w.shape
    return w.reshape(k // P, P, m // P, P).transpose(2, 1, 0, 3).reshape(m // P, P, -1)


def column_chunks(v):
    return v.reshape(-1, P).T


def lay_out(a):
    a = {k: np.asarray(v) for k, v in a.items()}
    f = np.float32
    tiles = np.zeros((STREAM_USED, P, TILE), f)

    def put(name, arr):
        at, n = STREAM_AT[name]
        tiles[at:at + n] = arr

    for l in range(2):
        put(f"wq{l}", tiles_of(a["peer_w_q"][l]))
        put(f"keys{l}", a["peer_keys"][l].reshape(2, 8, NKEYS, P).transpose(0, 3, 1, 2).reshape(2, P, TILE))
        at, n = STREAM_AT[f"experts{l}"]
        up = a["peer_u"][l].reshape(NKEYS, NKEYS, DC, P).transpose(1, 3, 2, 0)
        down = a["peer_v"][l].reshape(NKEYS, NKEYS, D).transpose(1, 0, 2)
        tiles[at:at + 2] = up[:2].reshape(2, P, TILE)
        tiles[at + 2:at + n - 2:2] = up[2:MAIN].reshape(MAIN - 2, P, TILE)
        for j in range(MAIN):
            tiles[at + down_at(j)] = down[j]
        put(f"early{l}", up[MAIN:].reshape(EARLY, P, TILE))
        put(f"late{l}", down[MAIN:])
        put(f"up{l}", tiles_of(a["ffn_w_up_2"][l]))
        put(f"down{l}", a["ffn_w_down_2"][l].reshape(FC, P, D))
    put("hg_in", tiles_of(a["hg_w_in"][0]))
    put("hg_out", tiles_of(a["hg_w_out"][0]))
    put("lru_in", tiles_of(a["lru_w_in"][0]))
    put("lru_out", tiles_of(a["lru_w_out"][0]))
    g = np.stack([a["lru_w_a"][0], a["lru_w_x"][0]], 1)
    g = g.reshape(2, 2, 2, 2, 2, P, 2, P)
    put("lru_gates", g.transpose(0, 1, 2, 5, 3, 6, 4, 7).reshape(8, P, TILE))
    we, wo = a["w_in_even_2"][0], a["w_in_odd_2"][0]
    nba = 4 * GDN_HEADS * P
    put("even_in", tiles_of(np.concatenate([we[:, :nba], we[:, nba + 12:]], 1)))
    put("even_out", tiles_of(a["w_out_even_2"][0]))
    put("odd_in", tiles_of(wo[:, :24 * P]))
    put("odd_out", tiles_of(a["w_out_odd_2"][0]))

    vec = {
        "c": a["c"], "norm_g": a["norm_g"], "b_ada": a["b_ada"], "hg_lb": a["hg_lb"],
        "hg_norm_g": a["hg_norm_g"], "lru_conv_w": a["lru_conv_w"], "lru_conv_b": a["lru_conv_b"],
        "lru_b_a": a["lru_b_a"], "lru_b_x": a["lru_b_x"], "lru_lam": a["lru_lam"],
        "final_g": a["final_g"], "gdn_conv_w": a["gdn_conv_w_2"], "gdn_norm_w": a["gdn_norm_w_2"],
        "diff_norm_w": a["diff_norm_w_2"], "gla_b_gate": a["gla_b_gate_2"],
        "gla_norm_w": a["gla_norm_w_2"], "ffn_conv_w": a["ffn_conv_w_2"],
        "ffn_conv_b": a["ffn_conv_b_2"], "ln_g": a["ln_g_2"], "ln_b": a["ln_b_2"],
    }
    cols = {n: column_chunks(x) for n, x in vec.items()}
    for n in ("gdn_dt_bias", "gdn_a_log"):
        cols[n] = np.repeat(a[n + "_2"].reshape(1, GDN_HEADS), P, 0)
    for n, size in PARAMS:
        assert cols[n].shape == (P, size), (n, cols[n].shape)
    params = np.concatenate([cols[n] for n, _ in PARAMS], 1)

    def by_rows(w):
        return w.reshape(DC, P, -1).transpose(1, 0, 2).reshape(P, -1)

    gate = np.zeros((P, 2 * P), f)
    gate[:GATE_RANK] = a["gla_w_gate_2"][0]
    small = np.concatenate([by_rows(we[:, nba:nba + 12]), by_rows(wo[:, 24 * P:]), gate], 1)
    bias = np.zeros((P, 4, P), f)
    bias[:NUM_BUCKETS] = a["rel_bias_2"][:, :, None]
    consts, masks = constants()
    x = a["x"][0].reshape(T, DC, P).transpose(2, 1, 0).reshape(P, -1)
    lam = np.repeat(a["diff_lambda_2"][0].reshape(1, -1), P, 0)
    ada = a["w_ada"].reshape(2, DC, P, 6, D).transpose(0, 3, 1, 2, 4).reshape(12, DC, P, D)
    return {"tiles": tiles, "ada": ada, "x": x, "params": params, "consts": consts, "small": small, "masks": masks,
            "lam": lam, "bias": bias.reshape(P, -1)}


ORDER = ["tiles", "ada", "x", "params", "consts", "small", "masks", "lam", "bias"]


def kernel(**inputs):
    import concourse.bacc as _bacc
    from concourse.bass_utils import run_bass_kernel_spmd as _run

    nc = _bacc.Bacc("TRN2", target_bir_lowering=False, num_devices=1)
    arrays = {n: np.ascontiguousarray(v) for n, v in lay_out(inputs).items()}
    args = [nc.dram_tensor(n, arrays[n].shape, F32, kind="ExternalInput").ap() for n in ORDER]
    skew = nc.dram_tensor("skew", (P, 4 * SKEW), F32, kind="Internal").ap()
    out = nc.dram_tensor("out", (P, DC * T), F32, kind="ExternalOutput").ap()
    build(nc, *args, skew, out)
    r = _run(nc, [arrays], core_ids=[0])
    got = r.results[0]["out"]
    return np.ascontiguousarray(got.reshape(P, DC, T).transpose(2, 1, 0).reshape(1, T, D))
```

```python
import math
from contextlib import ExitStack

import numpy as np

import concourse.bass as bass
from concourse import mybir

F32 = mybir.dt.float32
F32R = mybir.dt.float32r
U32 = mybir.dt.uint32
ALU = mybir.AluOpType
ACT = mybir.ActivationFunctionType
AX = mybir.AxisListType

P = 128
T = 256
TT = T // P
D = 1024
DC = D // P
RING = 4
UNROLL = 8
HALF = 512
TILE = 1024
HG_HEADS = 8
LRU_BLOCKS = 4
PEER_HEADS = 8
NKEYS = 128
TOPK = 16
EARLY = 36
MAIN = NKEYS - EARLY
GDN_HEADS = 6
SWA_GROUPS, SWA_HEADS, SWA_DH = 3, 4, 64
SWA_CONFIGS = ((128, 1), (512, 4), (2048, 16))
DIFF_HEADS = 4
GLA_HEADS, GLA_DK = 4, 64
GLA_TAU = 16.0
GATE_RANK = 16
D_FF = 2816
FC = D_FF // P
NUM_BUCKETS, REL_MAX = 32, 2048
LRU_C = 8.0
DEPTH = 2
ALPHA = (2 * DEPTH) ** 0.25
LAM_INIT = 0.8 - 0.6 * math.exp(-0.3)
PAIR_LEVELS = 7
DIAGONAL, CROSS = PAIR_LEVELS, PAIR_LEVELS + 1
SKEW = 512
NEG = -1e30

PARAMS = [
    ("c", DC), ("norm_g", 4 * DC), ("b_ada", 2 * 6 * DC), ("hg_lb", DC), ("hg_norm_g", DC),
    ("lru_conv_w", 4 * DC), ("lru_conv_b", DC), ("lru_b_a", 2 * DC), ("lru_b_x", 2 * DC),
    ("lru_lam", 2 * DC), ("final_g", DC), ("gdn_conv_w", 4 * 18), ("gdn_norm_w", 1),
    ("gdn_dt_bias", GDN_HEADS), ("gdn_a_log", GDN_HEADS), ("diff_norm_w", 1),
    ("gla_b_gate", 2), ("gla_norm_w", 1), ("ffn_conv_w", 2 * 3 * 2 * FC),
    ("ffn_conv_b", 2 * 2 * FC), ("ln_g", 4 * DC), ("ln_b", 4 * DC),
]
CONSTS = [
    ("ident", P), ("ones", P), ("mean_d", P), ("mean_head", P), ("iota", NKEYS), ("iota16", TOPK),
    ("tri", P), ("strict", P), ("pairs", PAIR_LEVELS * P), ("eps", 2), ("zero", P),
]
SMALL = [("w_ba", DC * 2 * GDN_HEADS), ("w_gd", DC * GATE_RANK), ("w_gate", 2 * P)]


def columns(table):
    at, out = 0, {}
    for name, n in table:
        out[name] = (at, n)
        at += n
    return out, at


STREAM = [
    ("hg_in", 5 * DC), ("hg_out", DC), ("wq0", 2 * PEER_HEADS), ("keys0", 2),
    ("early0", EARLY), ("experts0", 2 * MAIN), ("late0", EARLY),
    ("lru_in", 2 * DC), ("lru_gates", 8), ("lru_out", DC),
    ("wq1", 2 * PEER_HEADS), ("keys1", 2),
    ("early1", EARLY), ("experts1", 2 * MAIN), ("late1", EARLY),
    ("even_in", 42), ("even_out", DC), ("up0", 2 * FC), ("down0", FC),
    ("odd_in", 24), ("odd_out", DC), ("up1", 2 * FC), ("down1", FC),
]
STREAM_AT, STREAM_USED = columns(STREAM)
RUNS = [("experts0", 2 * MAIN + EARLY), ("experts1", 2 * MAIN + EARLY), ("even_in", 42),
        ("up0", 3 * FC), ("odd_in", 24), ("up1", 3 * FC)]
SPLIT_AT, _ = columns(RUNS)


def down_at(j):
    return 3 + 2 * j if j < MAIN - 2 else MAIN + j


class Tally:

    def __init__(self):
        self.count = {}

    def up(self, sem, by=1):
        self.count[id(sem)] = self.count.get(id(sem), 0) + by
        return self.count[id(sem)]

    def value(self, sem):
        return self.count.get(id(sem), 0)


def spans(eng, body, edges):
    for first, last in zip(edges, edges[1:]):
        steps = (last - first) // 4
        if steps > 1:
            with eng.Fori(0, steps) as it:
                for k in range(first, first + 4):
                    body(k, it)
        else:
            steps = 0
        for k in range(first + 4 * steps, last):
            body(k, 0)


def wide(ap, *shape):
    return ap.broadcast_to(list(shape))


def over(ap, n):
    return wide(ap.unsqueeze(1), ap.shape[0], n, ap.shape[1])


def build(nc, tiles, ada_in, x_in, params_in, consts_in, small_in, masks_in, lam_in, bias_in, skew, out):
    pcol, n_params = columns(PARAMS)
    ccol, n_consts = columns(CONSTS)
    scol, n_small = columns(SMALL)

    ctx = ExitStack()
    with ctx:
        def sb(name, cols, dt=F32):
            return ctx.enter_context(nc.sbuf_tensor(name, [P, cols], dt))

        sems = {}

        def sem(name):
            if name not in sems:
                sems[name] = ctx.enter_context(nc.semaphore(name))
            return sems[name]

        def overlaid(name, cols, *others):
            with nc.sbuf_tensor(name, [P, cols], F32) as whole:
                pass
            parts = [sb(n, size, F32R) for n, size in others]
            if cols > sum(size for _, size in others):
                sb(name + "_rest", cols - sum(size for _, size in others))
            return whole, *parts

        X = sb("X", DC * T)
        H, w_high = overlaid("H", DC * T, ("w_high", 2 * TILE))
        h_high = sb("h_high", DC * T, F32R)
        h_low = sb("h_low", DC * T, F32R)
        ring = sb("ring", RING * TILE)
        BIG = sb("BIG", 128 * T)
        par = sb("par", n_params)
        con = sb("con", n_consts)
        mod = sb("mod", 2 * 6 * DC)
        coef = sb("coef", 112)
        slots, a_low = overlaid("slots", 3 * T, ("a_low", 2 * T))
        onehots, w_low = overlaid("onehots", 2 * 2 * 4 * P, ("w_low", 2 * TILE))
        onehot_a, onehot_b = onehots[:, 0:2 * 4 * P], onehots[:, 2 * 4 * P:]
        act_v = sb("act_v", 2 * T)
        a_high = sb("a_high", 2 * T, F32R)
        inv = sb("inv", T)
        SM = sb("SM", n_small)
        stat = sb("stat", 24)
        PA = ctx.enter_context(nc.psum_tensor("PA", [P, 4 * 512], F32))
        PB = ctx.enter_context(nc.psum_tensor("PB", [P, 4 * 512], F32))

        def p(name, i=0, n=None):
            at, size = pcol[name]
            return par[:, at + i:at + i + (size if n is None else n)]

        def c(name, i=0, n=None):
            at, size = ccol[name]
            return con[:, at + i:at + i + (size if n is None else n)]

        def big(at, n):
            return BIG[:, at:at + n]

        def chunks(ap, t=T):
            return ap.rearrange("p (c t) -> p c t", t=t)

        ident = c("ident")
        TMP = big(120 * T, DC * T)

        def tile_half(ap, k, b):
            return ap[:, (k % 2) * TILE + b * HALF:(k % 2) * TILE + (b + 1) * HALF]

        def pair(ap, j):
            return ap[:, (j % 2) * T:(j % 2 + 1) * T]

        loaded = [sem(f"tile_loaded_{i}") for i in range(RING)]
        tile_done = sem("tile_done")
        ada_loaded = [sem(f"ada_loaded_{i}") for i in range(DC)]
        taken = sem("product_taken")

        PRODUCTS = [("hg_in", 5 * DC), ("hg_out", DC), ("wq0", 16), ("lru_in", 16), ("lru_out", DC),
                    ("wq1", 16), ("even_in", 42), ("even_out", DC), ("up0", 2 * FC),
                    ("odd_in", 24), ("odd_out", DC), ("up1", 2 * FC)]
        product_at, _ = columns(PRODUCTS)

        def product_slot(i):
            return PB[:, (i % 4) * 512:(i % 4) * 512 + T]


        HG = []
        for d in range(2):
            HG.append(dict(chunks=DC, heads=HG_HEADS, v_made=d == 1,
                           q=big((0, 40 * T)[d], DC * T), v=big((24 * T, 8 * T)[d], DC * T),
                           logit=big((8 * T, 16 * T)[d], DC * T), k=big(48 * T, DC * T),
                           b=big(56 * T, DC * T), e=big(64 * T, DC * T), e_next=big(120 * T, DC * T), kh=big(72 * T, DC * T),
                           qh=big(80 * T, DC * T), at=big(88 * T, DC * T), ax=big(96 * T, 4 * T),
                           vt=big(100 * T, DC * T)))
        ADA_RING, ADA_SUMS = big(40 * T, DC * TILE), big(72 * T, 12 * D)
        HG_G = big(32 * T, DC * T)
        HG_MIX = big(108 * T, DC * T)
        LRU = dict(xc=big(0, 8 * T), y=big(8 * T, 8 * T),
                   gate=[big((16 + 8 * i) * T, 8 * T) for i in range(4)],
                   la=big(48 * T, 8 * T), a=big(56 * T, 8 * T), m=big(64 * T, 8 * T),
                   h0=big(72 * T, 8 * T), h1=big(80 * T, 8 * T))
        EVEN = dict(q=big(0, 6 * T), k=big(6 * T, 6 * T), v=big(12 * T, 6 * T), z=big(18 * T, 6 * T),
                    qb=big(24 * T, 6 * T), kb=big(30 * T, 6 * T), vb=big(36 * T, 6 * T),
                    sq=big(42 * T, 6 * T), vt=big(48 * T, 6 * T), dt=big(54 * T, 9 * T),
                    mt=big(63 * T, 6 * T), m01=big(69 * T, 3 * T), qk0=big(72 * T, 3 * T),
                    qk01=big(75 * T, 3 * T), qk1=big(78 * T, 3 * T), n=big(81 * T, 6 * T),
                    nt=big(87 * T, 6 * T), x=big(93 * T, 6 * T), y=big(99 * T, 6 * T),
                    c=big(105 * T, 6 * T), ct=big(111 * T, 6 * T), p1=big(42 * T, 6 * T),
                    p2=big(117 * T, 6 * T), d0=big(105 * T, 3 * T), r1=big(108 * T, 3 * T),
                    d1=big(111 * T, 3 * T), ba=big(123 * T, 24), g=big(123 * T + 24, 12),
                    beta=big(123 * T + 36, 12), nbeta=big(123 * T + 48, 12),
                    gam=big(123 * T + 60, 12), t0=big(123 * T + 72, 12), t1=big(123 * T + 84, 12),
                    ea=big(123 * T + 96, 6), low=big(124 * T, PAIR_LEVELS * P),
                    mix=big(81 * T, 8 * T), vbt=big(54 * T, 6 * T), bias=big(60 * T, 8 * T),
                    neg=big(68 * T, 6 * T), prob=[big(74 * T, 3 * T), big(117 * T, 3 * T)], probt=big(77 * T, 3 * T))
        ODD = dict(qc=big(0, 4 * T), kc=big(4 * T, 4 * T), vc=big(8 * T, 4 * T), r=big(20 * T, 4 * T),
                   gd=big(42 * T, T), g1=big(43 * T, 2 * T), g2=big(45 * T, 2 * T),
                   sq=big(47 * T, 4 * T), vct=big(51 * T, 4 * T), bias=big(55 * T, 8 * T),
                   neg=big(63 * T, 2 * T), prob=[big(65 * T, 2 * T), big(80 * T, 2 * T)], probt=big(67 * T, T),
                   lamv=big(69 * T, T), mix=big(70 * T, 8 * T))
        GLA = dict(chunks=2, heads=GLA_HEADS, v_made=False, q=big(12 * T, 2 * T), k=big(14 * T, 2 * T),
                   v=big(16 * T, 4 * T), b=big(24 * T, 2 * T), e=big(26 * T, 2 * T), e_next=big(120 * T, 2 * T),
                   kh=big(28 * T, 2 * T), qh=big(30 * T, 2 * T), at=big(32 * T, 4 * T),
                   ax=big(36 * T, 2 * T), vt=big(38 * T, 4 * T))
        REL, ONEHOT, ROWS = big(0, 512), big(512, SKEW), big(1024, 4 * SKEW)
        MASK_LOW, MASK_SWA, MASK_CAUSAL, MASK_BUCKET = 0, 7 * P, 7 * P + 6 * T, 7 * P + 8 * T
        KEY_SCORES = [big((16 + 8 * t) * T, 8 * T) for t in range(TT)]
        SPARE, CAND, CAND_SPARE, PICK = (big((32 + 8 * i) * T, 8 * T) for i in range(4))
        VAL, IDX, IDX_F = (big((64 + i) * T, T) for i in range(3))
        CVAL, CPOS, HIGH, LOW, HIGH_F, LOW_F, GATE = (big(67 * T + i * P, P) for i in range(7))
        GSUM = big(71 * T, PEER_HEADS)

        def chosen(t, j):
            return big(72 * T + (t * 3 + j) * P, P)

        block = ctx.enter_context(nc.Block())

        @block.sync
        def _(sp):
            w = Tally()
            sp.dma_start(par[:, :], params_in).then_inc(sem("params_loaded"), 16)
            sp.dma_start(X[:, :], x_in).then_inc(sem("x_loaded"), 16)
            sp.dma_start(con[:, :], consts_in).then_inc(sem("consts_loaded"), 16)
            sp.dma_start(SM[:, :], small_in).then_inc(sem("small_loaded"), 16)

            def load(s, n):
                sp.dma_start(ring[:, s * TILE:(s + 1) * TILE], tiles[n]).then_inc(loaded[s], 16)

            for s in range(RING):
                load(s, s)

            def reload(n, it, run):
                if run is None:
                    sp.wait_ge(tile_done, it * RING + (n + 1))
                else:
                    k = SPLIT_AT[run][0] + n - STREAM_AT[run][0]
                    sp.wait_ge(sem("low_ready"), it * (2 * RING) + 2 * (k + 1))
                load(n % RING, it * RING + (n + RING))

            starts = [(0, None)]
            for run, n in RUNS:
                starts += [(STREAM_AT[run][0], run), (STREAM_AT[run][0] + n, None)]
            for (n0, run), (n1, _) in zip(starts, starts[1:] + [(STREAM_USED, None)]):
                n1 = min(n1, STREAM_USED - RING)
                if n0 < n1:
                    full = (n1 - n0) // RING
                    if full > 1:
                        with sp.Fori(0, full) as it:
                            for s in range(RING):
                                reload(n0 + s, it, run)
                    else:
                        full = 0
                    for n in range(n0 + RING * full, n1):
                        reload(n, 0, run)
            sp.wait_ge(sem("result_ready"), w.up(sem("result_ready")))
            sp.dma_start(out, X[:, :]).then_inc(sem("result_stored"), 16)
            sp.wait_ge(sem("result_stored"), w.up(sem("result_stored"), 16))

        @block.tensor
        def _(pe):
            w = Tally()
            mm = nc.tensor.matmul

            def tile(n, it=0):
                pe.wait_ge(loaded[n % RING], it * (16 * UNROLL // RING) + (n // RING + 1) * 16)
                return ring[:, (n % RING) * TILE:(n % RING + 1) * TILE]

            def loop(n, body, peel=0):
                full = n // UNROLL
                if full < 2 + (peel > 0):
                    for i in range(n):
                        body(i, 0)
                    return
                for i in range(UNROLL * peel):
                    body(i, 0)
                with pe.Fori(peel, full) as it:
                    for i in range(UNROLL):
                        body(i, it)
                for i in range(UNROLL * full, n):
                    body(i, 0)

            def linear(name, src):
                r0, n = STREAM_AT[name]
                q0 = product_at[name][0]

                def body(i, it):
                    wt = tile(r0 + i, it)
                    if not isinstance(it, int) or q0 + i >= 4:
                        pe.wait_ge(taken, it * UNROLL + (q0 + i - 3))
                    for k in range(DC):
                        ins = mm(product_slot(q0 + i), wt[:, k * P:(k + 1) * P],
                                 src[:, k * T:(k + 1) * T], start=k == 0, stop=k == DC - 1)
                    ins.then_inc(tile_done, 1)

                loop(n, body, peel=1 if q0 == 0 else 0)

            def passes(dst, k, b, at, high, low, start, stop):
                lhs_h = tile_half(w_high, k, b)[:, at * P:(at + 1) * P]
                lhs_l = tile_half(w_low, k, b)[:, at * P:(at + 1) * P]
                mm(dst, lhs_l, high, start=start, stop=False, skip_group_check=True)
                mm(dst, lhs_h, low, start=False, stop=False, skip_group_check=True)
                return mm(dst, lhs_h, high, start=False, stop=stop, skip_group_check=True)

            def split_product(dst, k, it, step):
                for b in range(2):
                    pe.wait_ge(sem("low_ready"), it * (2 * step) + (2 * k + b + 1))
                    for q in range(4):
                        m = 4 * b + q
                        ins = passes(dst, k, b, q, h_high[:, m * T:(m + 1) * T],
                                     h_low[:, m * T:(m + 1) * T], m == 0, m == DC - 1)
                    ins.then_inc((sem("mid_tile"), tile_done)[b], 1)

            def split_linear(name):
                s0, (q0, n) = SPLIT_AT[name][0], product_at[name]

                def body(k, it):
                    pe.wait_ge(taken, it * 4 + (q0 + k - 3))
                    split_product(product_slot(q0 + k), s0 + k, it, 4)

                pe.wait_ge(sem("h_split"), w.up(sem("h_split")))
                spans(pe, body, (0, n))

            def split_sums(j, k, it, step, first=False, last=False):
                pe.wait_ge(sem("gated_ready"), it * 4 + (j + 1))
                for b in range(2):
                    pe.wait_ge(sem("low_ready"), it * (2 * step) + (2 * k + b + 1))
                    for q in range(4):
                        m = 4 * b + q
                        ins = passes(PA[:, m * T:(m + 1) * T], k, b, q, pair(a_high, j), pair(a_low, j),
                                     first and m % 2 == 0, last)
                    ins.then_inc((sem("mid_tile"), tile_done)[b], 1)

            def all_taken(name):
                q0, n = product_at[name]
                pe.wait_ge(taken, q0 + n)

            def ada(first, last):
                pe.wait_ge(sem("ada_sums_ready"), last)
                for m in range(first * DC, last * DC):
                    ins = mm(PA[:, m:m + 1], ADA_SUMS[:, m * P:(m + 1) * P], c("ones", 0, 1),
                             start=True, stop=True)
                ins.then_inc(sem("ada_psum"), 1)

            def column_sums(squares, mat, dst):
                for k in range(DC):
                    ins = mm(dst, mat, squares[:, k * T:(k + 1) * T], start=k == 0, stop=k == DC - 1)
                return ins

            def rms():
                pe.wait_ge(sem("squares_ready"), w.up(sem("squares_ready")))
                column_sums(TMP, c("mean_d"), PA[:, 0:T]).then_inc(sem("mean_square_ready"), 1)

            def layer_norm():
                pe.wait_ge(sem("x_ready"), w.up(sem("x_ready")))
                column_sums(X[:, :], c("mean_d"), PA[:, 0:T]).then_inc(sem("mean_ready"), 1)
                rms()

            def head_sums(n, src, mat, dst):
                for h in range(n):
                    ins = mm(dst[:, h * T:(h + 1) * T], mat, src[:, h * T:(h + 1) * T],
                             start=True, stop=True)
                return ins

            def decay_attention(cfg):
                nh, kh, qh = cfg["heads"], cfg["kh"], cfg["qh"]
                per = nh // cfg["chunks"]
                rows = P // per

                def operand(buf, h, ch):
                    lo = (h % per) * rows
                    at = (h // per) * T + ch * P
                    return buf[lo:lo + rows, at:at + P]

                if cfg["v_made"]:
                    pe.wait_ge(sem("decay_v_ready"), w.up(sem("decay_v_ready")))
                for h in range(nh):
                    for ch in range(TT):
                        ins = nc.tensor.transpose(PA[:, (h * TT + ch) * P:(h * TT + ch + 1) * P],
                                                  cfg["v"][:, h * T + ch * P:h * T + (ch + 1) * P], ident)
                ins.then_inc(sem("decay_vt_psum"), 1)
                for lev in range(CROSS + 1):
                    dst = (PB, PA)[lev % 2]
                    if lev == 1:
                        pe.wait_ge(sem("decay_vt_ready"), w.up(sem("decay_vt_ready")))
                    if lev >= 2:
                        pe.wait_ge(sem("decay_masked"), w.up(sem("decay_masked")))
                    if lev != DIAGONAL:
                        pe.wait_ge(sem("decay_keys_ready"), w.up(sem("decay_keys_ready")))
                    k_, q_ = (cfg["k"], cfg["q"]) if lev == DIAGONAL else (kh, qh)
                    for h in range(nh):
                        for ch in range(TT if lev != CROSS else 1):
                            at = (h % per) * 1024 + (h // per * TT + ch if lev != CROSS else h // per) * P
                            ins = mm(dst[:, at:at + P], operand(k_, h, ch),
                                     operand(q_, h, 1 if lev == CROSS else ch), start=True, stop=True)
                    ins.then_inc(sem("decay_scores"), 1)
                pe.wait_ge(sem("decay_masked"), w.up(sem("decay_masked")))
                pe.wait_ge(sem("decay_masked"), w.up(sem("decay_masked")))
                vt, at_, ax = cfg["vt"], cfg["at"], cfg["ax"]
                for h in range(nh):
                    for ch in range(TT):
                        o = PA[:, (h * TT + ch) * P:(h * TT + ch + 1) * P]
                        v_own = vt[:, (h * TT + ch) * P:(h * TT + ch + 1) * P]
                        i = (h % per) * (nh // per) + h // per
                        a_own = at_[:, (i * TT + ch) * P:(i * TT + ch + 1) * P]
                        ins = mm(o, v_own, a_own, start=True, stop=ch == 0)
                        if ch == 1:
                            ins = mm(o, vt[:, h * TT * P:(h * TT + 1) * P], ax[:, i * P:(i + 1) * P],
                                     start=False, stop=True)
                ins.then_inc(sem("decay_out"), 1)

            def peer(layer):
                linear(f"wq{layer}", H)
                all_taken(f"wq{layer}")
                QT = big(0, 16 * T)
                r0, n = STREAM_AT[f"keys{layer}"]
                for i in range(n):
                    kt = tile(r0 + i)
                    for j in range(8):
                        hp = i * 8 + j
                        for t, dst in enumerate((PA, PB)):
                            ins = mm(dst[:, hp * NKEYS:(hp + 1) * NKEYS],
                                     QT[:, hp * T + t * P:hp * T + (t + 1) * P],
                                     kt[:, j * NKEYS:(j + 1) * NKEYS], start=True, stop=True)
                    ins.then_inc(tile_done, 1)
                pe.wait_ge(sem("key_scores"), TT * (layer + 1))
                r0, n = STREAM_AT[f"early{layer}"]
                e0 = layer * EARLY

                def early(i, it):
                    ut = tile(r0 + i, it)
                    if not isinstance(it, int) or e0 + i >= 4:
                        pe.wait_ge(sem("early_gelu"), it * UNROLL + (e0 + i - 3))
                    for k in range(DC):
                        ins = mm(PB[:, (i % 4) * 512:(i % 4) * 512 + T], ut[:, k * P:(k + 1) * P],
                                 H[:, k * T:(k + 1) * T], start=k == 0, stop=k == DC - 1)
                    ins.then_inc(tile_done, 1)

                loop(n, early, peel=1)
                for t in range(TT):
                    pe.wait_ge(sem("chosen_ready"), w.up(sem("chosen_ready")))
                    for j in range(3):
                        ins = nc.tensor.transpose(PA[:, (t * 3 + j) * P:(t * 3 + j + 1) * P],
                                                  chosen(t, j), ident)
                ins.then_inc(sem("slots_psum"), 1)
                pe.wait_ge(sem("slots_ready"), w.up(sem("slots_ready")))

                g0 = layer * 64

                def group(r, it):
                    pe.wait_ge(sem("onehots_ready"), it * 4 + (g0 + r + 1))
                    if not isinstance(it, int) or g0 + r >= 4:
                        pe.wait_ge(sem("gates_folded"), it * 4 + (g0 + r - 3))
                    for j in range(4):
                        at = ((r % 2) * 4 + j) * P
                        ins = mm(PA[:, (r * 4 + j) * P:(r * 4 + j + 1) * P],
                                 onehot_a[:, at:at + P], onehot_b[:, at:at + P], start=True, stop=True)
                    ins.then_inc(sem("gates_psum"), 1)

                for r in range(4):
                    group(r, 0)
                with pe.Fori(1, 16) as it:
                    for r in range(4):
                        group(r, it)

                pe.wait_ge(sem("gates_folded"), g0 + 64)
                for b in range(4):
                    mm(PA[:, b * 512:(b + 1) * 512], c("zero", 0, P), wide(c("zero", 0, 1), P, 512),
                       start=True, stop=False, skip_group_check=True)
                pe.wait_ge(sem("h_split"), w.up(sem("h_split")))

                s0, c0 = SPLIT_AT[f"experts{layer}"][0], layer * NKEYS

                def up(j, k, it=0):
                    split_product(PB[:, (j % 4) * 512:(j % 4) * 512 + T], s0 + k, it, 8)

                def down(j, k, it=0, step=8):
                    split_sums(c0 + j, s0 + k, it, step, last=j == NKEYS - 1)

                up(0, 0)
                up(1, 1)
                steps = (MAIN - 2) // 4
                with pe.Fori(0, steps) as it:
                    for j in range(4):
                        up(j + 2, 2 + 2 * j, it)
                        down(j, down_at(j), it)
                for j in range(4 * steps, MAIN - 2):
                    up(j + 2, 2 + 2 * j)
                    down(j, down_at(j))
                down(MAIN - 2, down_at(MAIN - 2))
                down(MAIN - 1, down_at(MAIN - 1))
                steps = EARLY // 4
                with pe.Fori(0, steps - 1) as it:
                    for j in range(MAIN, MAIN + 4):
                        down(j, down_at(j), it, 4)
                for j in range(NKEYS - 4, NKEYS):
                    down(j, down_at(j))
            def conv_ffn(i):
                s0, c0 = SPLIT_AT[f"up{i}"][0], 2 * NKEYS + i * FC
                split_linear(f"up{i}")

                def down(j, it=0):
                    split_sums(c0 + j, s0 + 2 * FC + j, it, 4, j == 0, j == FC - 1)

                down(0)
                steps = (FC - 2) // 4
                with pe.Fori(0, steps) as it:
                    for j in range(1, 5):
                        down(j, it)
                for j in range(4 * steps + 1, FC):
                    down(j)

            def bias_rows():
                pe.wait_ge(sem("bias_loaded"), w.up(sem("bias_loaded"), 32))
                for h in range(4):
                    ins = mm(PA[:, h * SKEW:(h + 1) * SKEW], REL[0:32, h * P:(h + 1) * P],
                             ONEHOT[0:32, :], start=True, stop=True)
                ins.then_inc(sem("bias_rows_psum"), 1)

            def even_mixer():
                split_linear("even_in")
                e = EVEN
                all_taken("even_in")
                pe.wait_ge(sem("small_loaded"), w.up(sem("small_loaded"), 16))
                for t in range(TT):
                    for k in range(DC):
                        ins = mm(PB[:, t * 512:t * 512 + 12], X[:, k * T + t * P:k * T + (t + 1) * P],
                                 SM[:, scol["w_ba"][0] + k * 12:scol["w_ba"][0] + (k + 1) * 12],
                                 start=k == 0, stop=k == DC - 1)
                ins.then_inc(sem("ba_psum"), 1)
                for i in range(2):
                    pe.wait_ge(sem("qk_squares"), w.up(sem("qk_squares")))
                    head_sums(GDN_HEADS, e["sq"], c("ones"), PA).then_inc(sem("qk_lengths"), 1)
                pe.wait_ge(sem("qk_roots"), w.up(sem("qk_roots"), 2))
                for h in range(GDN_HEADS):
                    for t in range(TT):
                        ins = nc.tensor.transpose(PA[:, (h * TT + t) * P:(h * TT + t + 1) * P],
                                                  e["v"][:, h * T + t * P:h * T + (t + 1) * P], ident)
                ins.then_inc(sem("gdn_vt_psum"), 1)
                pe.wait_ge(sem("g_ready"), w.up(sem("g_ready")))
                for t in range(TT):
                    for u in range(t + 1):
                        ins = mm(PB[:, 1024 + t * 8:1024 + t * 8 + 6],
                                 c("ones") if u < t else c("tri"), e["g"][:, u * 6:(u + 1) * 6],
                                 start=u == 0, stop=u == t)
                ins.then_inc(sem("gam_col_psum"), 1)
                for h in range(GDN_HEADS):
                    if h >= 2:
                        pe.wait_ge(sem("decay_taken"), w.up(sem("decay_taken")))
                    dst = PB[:, (h % 2) * 512:(h % 2) * 512 + T]
                    for t in range(TT):
                        for u in range(t + 1):
                            ins = mm(dst[:, t * P:(t + 1) * P],
                                     wide(e["g"][:, u * 6 + h:u * 6 + h + 1], P, P),
                                     c("ones") if u < t else c("tri"), start=u == 0, stop=u == t)
                    ins.then_inc(sem("gam_row_psum"), 1)
                pe.wait_ge(sem("decay_taken"), w.up(sem("decay_taken")))
                pe.wait_ge(sem("decay_taken"), w.up(sem("decay_taken")))
                pe.wait_ge(sem("gdn_vt_ready"), w.up(sem("gdn_vt_ready")))
                pe.wait_ge(sem("qk_normed"), w.up(sem("qk_normed")))
                for i, (a, b) in enumerate((("k", "k"), ("k", "q"))):
                    for j, (s, t) in enumerate(((0, 0), (0, 1), (1, 1))):
                        n = i * 3 + j
                        dst = (PA, PB)[n % 2]
                        if n >= 2:
                            pe.wait_ge(sem("pair_taken"), w.up(sem("pair_taken")))
                        for h in range(GDN_HEADS):
                            ins = mm(dst[:, h * P:(h + 1) * P], e[a][:, h * T + s * P:h * T + (s + 1) * P],
                                     e[b][:, h * T + t * P:h * T + (t + 1) * P], start=True, stop=True)
                        ins.then_inc(sem("pair_psum"), 1)
                pe.wait_ge(sem("pair_taken"), w.up(sem("pair_taken")))
                pe.wait_ge(sem("pair_taken"), w.up(sem("pair_taken")))
                NM = GDN_HEADS * TT

                def at(i):
                    return slice(i * P, (i + 1) * P)

                for i in range(NM):
                    ins = nc.tensor.transpose(PA[:, at(i)], e["mt"][:, at(i)], ident)
                ins.then_inc(sem("m_psum"), 1)
                pe.wait_ge(sem("n_ready"), w.up(sem("n_ready")))
                for i in range(NM):
                    ins = nc.tensor.transpose(PB[:, at(i)], e["n"][:, at(i)], ident)
                ins.then_inc(sem("nt_psum"), 1)
                def times(dst, g, lhs, rhs):
                    for i in range(6 * g, 6 * g + 6):
                        to = g * 1024 + (i % 6) * P
                        ins = mm(dst[:, to:to + P], e[lhs][:, at(i)], e[rhs][:, at(i)], start=True, stop=True)
                    return ins

                for lev in range(1, PAIR_LEVELS):
                    for g in range(2):
                        pe.wait_ge(sem("inverse_step"), w.up(sem("inverse_step")))
                        times(PA, g, "ct", "x").then_inc(sem("inv_p1"), 1)
                        times(PB, g, "c", "y").then_inc(sem("inv_p2"), 1)
                    for g in range(2):
                        pe.wait_ge(sem("inv_p1_ready"), w.up(sem("inv_p1_ready")))
                        times(PA, g, "y", "p1").then_inc(sem("inv_xpx"), 1)
                        pe.wait_ge(sem("inv_p2_ready"), w.up(sem("inv_p2_ready")))
                        times(PB, g, "x", "p2").then_inc(sem("inv_ypy"), 1)
                pe.wait_ge(sem("inverse_step"), w.up(sem("inverse_step"), 2))
                for h in range(GDN_HEADS):
                    ins = mm(PA[:, at(h)], e["y"][:, at(h * 2)], e["vt"][:, at(h * 2)], start=True, stop=True)
                ins.then_inc(sem("delta0_psum"), 1)
                pe.wait_ge(sem("delta0_ready"), w.up(sem("delta0_ready")))
                for h in range(GDN_HEADS):
                    ins = mm(PB[:, at(h)], e["m01"][:, at(h)], e["d0"][:, at(h)], start=True, stop=True)
                ins.then_inc(sem("carry_psum"), 1)
                pe.wait_ge(sem("carry_ready"), w.up(sem("carry_ready")))
                for h in range(GDN_HEADS):
                    ins = mm(PA[:, at(h)], e["y"][:, at(h * 2 + 1)], e["r1"][:, at(h)], start=True, stop=True)
                ins.then_inc(sem("delta1_psum"), 1)
                pe.wait_ge(sem("delta1_ready"), w.up(sem("delta1_ready")))
                for h in range(GDN_HEADS):
                    for t in range(TT):
                        o = PB[:, (h * TT + t) * P:(h * TT + t + 1) * P]
                        if t == 0:
                            ins = mm(o, e["d0"][:, at(h)], e["qk0"][:, at(h)], start=True, stop=True)
                        else:
                            mm(o, e["d0"][:, at(h)], e["qk01"][:, at(h)], start=True, stop=False)
                            ins = mm(o, e["d1"][:, at(h)], e["qk1"][:, at(h)], start=False, stop=True)
                ins.then_inc(sem("gdn_out_psum"), 1)
                pe.wait_ge(sem("head_squares"), w.up(sem("head_squares")))
                head_sums(GDN_HEADS, e["sq"], c("mean_head"), PA).then_inc(sem("head_means"), 1)
                pe.wait_ge(sem("head_roots"), w.up(sem("head_roots")))
                for i in range(6):
                    for t in range(TT):
                        ins = nc.tensor.transpose(PA[:, (i * TT + t) * P:(i * TT + t + 1) * P],
                                                  e["vb"][:, i * T + t * P:i * T + (t + 1) * P], ident)
                ins.then_inc(sem("swa_vt_psum"), 1)
                pe.wait_ge(sem("swa_vt_ready"), w.up(sem("swa_vt_ready")))
                attend(SWA_GROUPS * TT * P, "swa")
                pe.wait_ge(sem("gdn_done"), w.up(sem("gdn_done")))
                linear("even_out", e["mix"])

            def attend(keys, kind):
                nk = keys // P
                S_, W_ = PA[:, 0:1024], PA[:, 1024:2048]
                e = EVEN if kind == "swa" else ODD

                def scores(n):
                    h, t = n // TT, n % TT
                    if kind == "swa":
                        lo = (h % 2) * SWA_DH
                        for g in range(SWA_GROUPS):
                            at = (g * 2 + h // 2) * T
                            ins = mm(S_[:, g * T:(g + 1) * T],
                                     e["qb"][lo:lo + SWA_DH, at + t * P:at + (t + 1) * P],
                                     e["kb"][lo:lo + SWA_DH, at:at + T], start=True, stop=True)
                    else:
                        for i in range(2):
                            lo = i * 64
                            ins = mm(S_[:, i * 512:i * 512 + T],
                                     e["qc"][lo:lo + 64, h * T + t * P:h * T + (t + 1) * P],
                                     e["kc"][lo:lo + 64, h * T:(h + 1) * T], start=True, stop=True)
                    ins.then_inc(sem("attention_scores"), 1)

                scores(0)
                for n in range(4 * TT):
                    h = n // TT
                    pe.wait_ge(sem("attention_scores_taken"), w.up(sem("attention_scores_taken")))
                    if n + 1 < 4 * TT:
                        scores(n + 1)
                    pe.wait_ge(sem("attention_weights"), w.up(sem("attention_weights")))
                    for i in range(nk):
                        ins = nc.tensor.transpose(W_[:, i * P:(i + 1) * P],
                                                  e["prob"][n % 2][:, i * P:(i + 1) * P], ident)
                    ins.then_inc(sem("attention_wt_psum"), 1)
                    pe.wait_ge(sem("attention_wt_ready"), w.up(sem("attention_wt_ready")))
                    if kind == "swa":
                        lo = (h % 2) * SWA_DH
                        o = PB[lo:lo + SWA_DH, (n % 4) * 512:(n % 4) * 512 + P]
                        for i in range(nk):
                            g, kc = i // TT, i % TT
                            vt = ((g * 2 + h // 2) * TT + kc) * P + lo
                            ins = mm(o, e["vbt"][:, vt:vt + SWA_DH], e["probt"][:, i * P:(i + 1) * P],
                                     start=i == 0, stop=i == nk - 1)
                    else:
                        o = PB[:, (n % 4) * 512:(n % 4) * 512 + P]
                        for i in range(nk):
                            ins = mm(o, e["vct"][:, (h * TT + i) * P:(h * TT + i + 1) * P],
                                     e["probt"][:, i * P:(i + 1) * P], start=i == 0, stop=i == nk - 1)
                    ins.then_inc(sem("attention_out_psum"), 1)
                pe.wait_ge(sem("attention_done"), w.up(sem("attention_done")))

            def odd_mixer():
                e = ODD
                split_linear("odd_in")
                all_taken("odd_in")
                for k in range(DC):
                    ins = mm(PB[0:GATE_RANK, 0:T],
                             SM[:, scol["w_gd"][0] + k * 16:scol["w_gd"][0] + (k + 1) * 16],
                             X[:, k * T:(k + 1) * T], start=k == 0, stop=k == DC - 1)
                ins.then_inc(sem("gd_psum"), 1)
                pe.wait_ge(sem("gd_ready"), w.up(sem("gd_ready")))
                for i in range(2):
                    ins = mm(PB[:, 512 + i * 512:512 + i * 512 + T],
                             SM[0:GATE_RANK, scol["w_gate"][0] + i * P:scol["w_gate"][0] + (i + 1) * P],
                             e["gd"][0:GATE_RANK, :], start=True, stop=True)
                ins.then_inc(sem("gate_psum"), 1)
                pe.wait_ge(sem("gate_taken"), w.up(sem("gate_taken")))
                decay_attention(GLA)
                pe.wait_ge(sem("head_squares"), w.up(sem("head_squares")))
                head_sums(4, e["sq"], c("mean_head"), PA).then_inc(sem("head_means"), 1)
                pe.wait_ge(sem("head_roots"), w.up(sem("head_roots")))
                for h in range(DIFF_HEADS):
                    for t in range(TT):
                        ins = nc.tensor.transpose(PA[:, (h * TT + t) * P:(h * TT + t + 1) * P],
                                                  e["vc"][:, h * T + t * P:h * T + (t + 1) * P], ident)
                ins.then_inc(sem("diff_vt_psum"), 1)
                pe.wait_ge(sem("diff_vt_ready"), w.up(sem("diff_vt_ready")))
                attend(T, "diff")
                pe.wait_ge(sem("head_squares"), w.up(sem("head_squares")))
                head_sums(4, e["sq"], c("mean_head"), PA).then_inc(sem("head_means"), 1)
                pe.wait_ge(sem("head_roots"), w.up(sem("head_roots")))
                pe.wait_ge(sem("mix_ready"), w.up(sem("mix_ready")))
                linear("odd_out", e["mix"])

            pe.wait_ge(sem("consts_loaded"), w.up(sem("consts_loaded"), 16))
            ada(0, 2)
            pe.wait_ge(sem("mod_ready"), w.up(sem("mod_ready")))
            rms()
            pe.wait_ge(sem("h_ready"), w.up(sem("h_ready")))
            linear("hg_in", H)
            ada(2, 12)
            all_taken("hg_in")
            pe.wait_ge(sem("mod_ready"), w.up(sem("mod_ready")))
            decay_attention(HG[0])
            pe.wait_ge(sem("decay_out_taken"), w.up(sem("decay_out_taken")))
            decay_attention(HG[1])
            pe.wait_ge(sem("head_squares"), w.up(sem("head_squares")))
            head_sums(HG_HEADS, TMP, c("mean_head"), PA).then_inc(sem("head_means"), 1)
            pe.wait_ge(sem("head_roots"), w.up(sem("head_roots")))
            pe.wait_ge(sem("mix_ready"), w.up(sem("mix_ready")))
            linear("hg_out", HG_MIX)
            pe.wait_ge(sem("x_ready"), w.up(sem("x_ready")))
            rms()
            pe.wait_ge(sem("h_ready"), w.up(sem("h_ready")))
            peer(0)
            pe.wait_ge(sem("x_ready"), w.up(sem("x_ready")))
            rms()
            pe.wait_ge(sem("h_ready"), w.up(sem("h_ready")))
            linear("lru_in", H)
            all_taken("lru_in")
            r0, n = STREAM_AT["lru_gates"]
            for i in range(n):
                wt = tile(r0 + i)
                if i >= 2:
                    pe.wait_ge(sem("lru_gate_taken"), w.up(sem("lru_gate_taken")))
                for j in range(4):
                    m = (i % 2) * 4 + j
                    for k in range(2):
                        ins = mm(PA[:, (i % 2) * 1024 + j * T:(i % 2) * 1024 + (j + 1) * T],
                                 wt[:, (j * 2 + k) * P:(j * 2 + k + 1) * P],
                                 LRU["xc"][:, (2 * (m // 2) + k) * T:(2 * (m // 2) + k + 1) * T],
                                 start=k == 0, stop=k == 1)
                ins.then_inc(tile_done, 1)
            pe.wait_ge(sem("lru_gate_taken"), w.up(sem("lru_gate_taken")))
            pe.wait_ge(sem("lru_gate_taken"), w.up(sem("lru_gate_taken")))
            pe.wait_ge(sem("mix_ready"), w.up(sem("mix_ready")))
            linear("lru_out", LRU["h0"])
            pe.wait_ge(sem("x_ready"), w.up(sem("x_ready")))
            rms()
            pe.wait_ge(sem("h_ready"), w.up(sem("h_ready")))
            peer(1)
            pe.wait_ge(sem("x_ready"), w.up(sem("x_ready")))
            rms()
            pe.wait_ge(sem("x_normed"), w.up(sem("x_normed")))
            bias_rows()
            pe.wait_ge(sem("bias_rows_taken"), w.up(sem("bias_rows_taken")))
            even_mixer()
            layer_norm()
            pe.wait_ge(sem("x_normed"), w.up(sem("x_normed")))
            conv_ffn(0)
            layer_norm()
            pe.wait_ge(sem("x_normed"), w.up(sem("x_normed")))
            odd_mixer()
            layer_norm()
            pe.wait_ge(sem("x_normed"), w.up(sem("x_normed")))
            conv_ffn(1)
            layer_norm()

        @block.scalar
        def _(act):
            w = Tally()
            fn = nc.scalar.activation

            def split_high(run, k, it=0, step=8):
                n, s = STREAM_AT[run][0] + k, SPLIT_AT[run][0] + k
                act.wait_ge(loaded[n % RING], it * (16 * step // RING) + (n // RING + 1) * 16)
                for b in range(2):
                    if k >= 2 and b == 0:
                        act.wait_ge(sem("mid_tile"), it * step + (s - 1))
                    if k >= 2 and b == 1:
                        act.wait_ge(tile_done, it * step + (n - 1))
                    at = (n % RING) * TILE + b * HALF
                    fn(tile_half(w_high, s, b), ring[:, at:at + HALF],
                       ACT.Identity).then_inc(sem("high_ready"), 1)

            def all_taken(name):
                q0, n = product_at[name]
                act.wait_ge(taken, q0 + n)

            def evacuate(name, dst, func=ACT.Identity, first=0, last=None):
                q0, n = product_at[name]
                r0 = STREAM_AT[name][0]
                last = n if last is None else last
                if q0 + first > 0:
                    act.wait_ge(taken, q0 + first)

                def body(i, it):
                    act.wait_ge(tile_done, it * 8 + (r0 + i + 1))
                    fn(dst[:, bass.ds(it * (8 * T) + (i - first) * T, T)], product_slot(q0 + i),
                       func).then_inc(taken, 1)

                full = (last - first) // 8
                if full >= 2:
                    with act.Fori(0, full) as it:
                        for i in range(8):
                            body(first + i, it)
                else:
                    full = 0
                for i in range(first + 8 * full, last):
                    body(i, 0)

            def start_run(run):
                split_high(run, 0)
                split_high(run, 1)
                act.wait_ge(sem("x_normed"), w.up(sem("x_normed")))
                fn(h_high[:, :], X[:, :], ACT.Identity).then_inc(sem("h_high"), 1)

            def split_evacuate(run, first):
                q0, n = product_at[run]
                r0 = STREAM_AT[run][0]

                def copied(j, it=0):
                    if j == first:
                        act.wait_ge(taken, q0 + first)
                    act.wait_ge(tile_done, it * 4 + (r0 + j + 1))
                    fn(BIG[:, bass.ds(it * (4 * T) + j * T, T)], product_slot(q0 + j),
                       ACT.Identity).then_inc(taken, 1)

                def tile(k, it):
                    split_high(run, k, it, 4)
                    if k - 2 >= first:
                        copied(k - 2, it)

                start_run(run)
                spans(act, tile, (2, first + 2, first + 3, n) if first else (2, 3, n))
                copied(n - 2)
                copied(n - 1)

            def squares(src, dst, name):
                fn(dst, src, ACT.Square).then_inc(sem(name), 1)

            def root(layer_norm=False):
                act.wait_ge(sem("mean_square_ready"), w.up(sem("mean_square_ready")))
                fn(inv[:, :], PA[:, 0:T], ACT.Sqrt,
                   bias=c("eps", 1 if layer_norm else 0, 1)).then_inc(sem("root_ready"), 1)

            def rms():
                squares(X[:, :], TMP, "squares_ready")
                root()

            def layer_norm():
                act.wait_ge(sem("centered"), w.up(sem("centered")))
                squares(X[:, :], TMP, "squares_ready")
                root(True)

            def head_norm(o, sq, n):
                act.wait_ge(sem("heads_ready"), w.up(sem("heads_ready")))
                squares(o, sq, "head_squares")
                act.wait_ge(sem("head_means"), w.up(sem("head_means")))
                fn(sq, PA[:, 0:n * T], ACT.Sqrt, bias=c("eps", 0, 1)).then_inc(sem("head_roots"), 1)

            def decay_attention(cfg):
                n = cfg["heads"] * T
                act.wait_ge(sem("decay_vt_psum"), w.up(sem("decay_vt_psum")))
                fn(cfg["vt"], PA[:, 0:n], ACT.Identity).then_inc(sem("decay_vt_ready"), 1)
                for i in range(PAIR_LEVELS + 1):
                    e = cfg[("e", "e_next")[i % 2]]
                    act.wait_ge(sem("decay_diff"), w.up(sem("decay_diff")))
                    fn(e, e, ACT.Abs).then_inc(sem("act_step"), 1)
                    act.wait_ge(sem("act_step"), w.up(sem("act_step")))
                    fn(e, e, ACT.Exp, scale=-1.0).then_inc(sem("decay_exp"), 1)

            def peer(layer):
                evacuate(f"wq{layer}", big(0, 16 * T))
                r0, n = STREAM_AT[f"keys{layer}"]
                act.wait_ge(tile_done, r0 + n)
                for t, src in enumerate((PA, PB)):
                    fn(KEY_SCORES[t], src[:, :], ACT.Identity).then_inc(sem("key_scores"), 1)
                fn(h_high[:, :], H[:, :], ACT.Identity).then_inc(sem("h_high"), 1)
                r0, n = STREAM_AT[f"early{layer}"]

                def early(first, last):
                    def body(i, it):
                        act.wait_ge(tile_done, it * 8 + (r0 + i + 1))
                        fn(BIG[:, bass.ds(it * (8 * T) + (MAIN + i) * T, T)],
                           PB[:, (i % 4) * 512:(i % 4) * 512 + T],
                           ACT.Gelu_apprx_tanh).then_inc(sem("early_gelu"), 1)

                    full = (last - first) // 8
                    if full > 1:
                        with act.Fori(0, full) as it:
                            for i in range(8):
                                body(first + i, it)
                    else:
                        full = 0
                    for i in range(first + 8 * full, last):
                        body(i, 0)

                for t, (first, last) in enumerate(((0, 18), (18, 32))):
                    early(first, last)
                    act.wait_ge(sem("gate_diff"), w.up(sem("gate_diff")))
                    fn(GATE, GATE, ACT.Exp).then_inc(sem("gate_exp"), 1)
                early(32, n)
                act.wait_ge(sem("slots_psum"), w.up(sem("slots_psum")))
                fn(slots[:, :].rearrange("p (j t c) -> p t j c", j=3, t=TT),
                   PA[:, 0:6 * P].rearrange("p (t j c) -> p t j c", j=3, t=TT),
                   ACT.Identity).then_inc(sem("slots_ready"), 1)
                g0 = layer * 64
                gates = chunks(BIG[:, :])

                def group(r, it):
                    act.wait_ge(sem("gates_psum"), it * 4 + (g0 + r + 1))
                    fn(gates[:, 0:MAIN, bass.ds(it * 16 + r * 4, 4)],
                       PA[:, r * 512:(r + 1) * 512].rearrange("p (t j) -> p j t", t=4)[:, 0:MAIN, :],
                       ACT.Identity).then_inc(sem("gates_copied"), 1)

                with act.Fori(0, 16) as it:
                    for r in range(4):
                        group(r, it)
                r0, n = STREAM_AT[f"experts{layer}"]
                act.wait_ge(sem("h_split"), w.up(sem("h_split")))
                act.wait_ge(tile_done, r0)

                run = f"experts{layer}"

                def gelu(j, k, it=0):
                    act.wait_ge(tile_done, it * 8 + (r0 + k + 1))
                    if j >= 2:
                        act.wait_ge(sem("gated_ready"), it * 4 + (layer * NKEYS + j - 1))
                    fn(pair(act_v, j), PB[:, (j % 4) * 512:(j % 4) * 512 + T],
                       ACT.Gelu_apprx_tanh).then_inc(sem("gelu_ready"), 1)

                def column(j, it=0):
                    split_high(run, 2 * j, it)
                    gelu(j, 2 * j - 2, it)
                    split_high(run, 2 * j + 1, it)

                split_high(run, 0)
                split_high(run, 1)
                split_high(run, 2)
                gelu(0, 0)
                split_high(run, 3)
                gelu(1, 1)
                steps = (MAIN - 2) // 4
                with act.Fori(0, steps) as it:
                    for j in range(2, 6):
                        column(j, it)
                for j in range(4 * steps + 2, MAIN):
                    column(j)
                steps = EARLY // 4
                with act.Fori(0, steps) as it:
                    for k in range(2 * MAIN, 2 * MAIN + 4):
                        split_high(run, k, it, 4)

            def conv_ffn(i):
                run = f"up{i}"
                q0, r0 = product_at[run][0], STREAM_AT[run][0]
                wt, bias = p("ffn_conv_w", i * 132 + 2 * 44, 44), p("ffn_conv_b", i * 44, 44)

                def center(j, it=0):
                    act.wait_ge(tile_done, it * 4 + (r0 + j + 1))
                    fn(BIG[:, bass.ds(it * (4 * T) + j * T, T)], product_slot(q0 + j), ACT.Identity,
                       scale=wt[:, bass.ds(it * 4 + j, 1)],
                       bias=bias[:, bass.ds(it * 4 + j, 1)]).then_inc(sem("conv_center"), 1)

                def silu(j, it=0):
                    act.wait_ge(taken, it * 4 + (q0 + j + 1))
                    gate = BIG[:, bass.ds(it * (4 * T) + j * T, T)]
                    fn(gate, gate, ACT.Silu).then_inc(sem("ffn_gate_ready"), 1)

                def tile(k, it=0):
                    split_high(run, k, it, 4)
                    if 2 <= k < 2 * FC + 2:
                        center(k - 2, it)
                    if FC + 2 <= k < 2 * FC + 2:
                        silu(k - 2 - FC, it)

                start_run(run)
                spans(act, tile, (2, FC + 2, 2 * FC + 2, 3 * FC))

            def attend(kind, e, dst_chunk):
                def exp(n):
                    st, pr = stat[:, 16 + 4 * (n % 2):], e["prob"][n % 2]
                    act.wait_ge(sem("attention_max"), w.up(sem("attention_max")))
                    if kind == "swa":
                        fn(pr, pr, ACT.Exp, bias=st[:, 0:1], accum_out=st[:, 2:3])\
                            .then_inc(sem("attention_exp"), 1)
                    else:
                        for i in range(2):
                            fn(pr[:, i * T:(i + 1) * T], pr[:, i * T:(i + 1) * T], ACT.Exp,
                               bias=st[:, i:i + 1],
                               accum_out=st[:, 2 + i:3 + i]).then_inc(sem("attention_exp"), 1)

                exp(0)
                for n in range(4 * TT):
                    h, t = n // TT, n % TT
                    if n + 1 < 4 * TT:
                        exp(n + 1)
                    act.wait_ge(sem("attention_wt_psum"), w.up(sem("attention_wt_psum")))
                    nk = TT * (3 if kind == "swa" else 1)
                    fn(e["probt"], PA[:, 1024:1024 + nk * P],
                       ACT.Identity).then_inc(sem("attention_wt_ready"), 1)
                    act.wait_ge(sem("attention_out_psum"), w.up(sem("attention_out_psum")))
                    if kind == "swa":
                        rows = slice((h % 2) * SWA_DH, (h % 2 + 1) * SWA_DH)
                        at = (6 + h // 2) * T + t * P
                    else:
                        rows, at = slice(0, P), h * T + t * P
                    ins = fn(e["mix"][rows, at:at + P], PB[rows, (n % 4) * 512:(n % 4) * 512 + P],
                             ACT.Identity)
                    if n < 7:
                        ins.then_inc(sem("act_step"), 1)
                        act.wait_ge(sem("act_step"), w.up(sem("act_step")))
                ins.then_inc(sem("attention_done"), 1)

            def even_mixer():
                e = EVEN
                split_evacuate("even_in", 18)
                qkv = big(0, 18 * T)
                act.wait_ge(taken, product_at["even_in"][0] + 42)
                fn(qkv, qkv, ACT.Silu).then_inc(sem("qkv_silu"), 1)
                act.wait_ge(sem("qkv_silu"), w.up(sem("qkv_silu")))
                squares(e["q"], e["sq"], "qk_squares")
                act.wait_ge(sem("qk_lengths"), w.up(sem("qk_lengths")))
                fn(e["x"], PA[:, 0:6 * T], ACT.Sqrt, bias=c("eps", 0, 1)).then_inc(sem("qk_roots"), 1)
                act.wait_ge(sem("qk_roots"), w.up(sem("qk_roots")))
                squares(e["k"], e["sq"], "qk_squares")
                act.wait_ge(sem("qk_lengths"), w.up(sem("qk_lengths")))
                fn(e["y"], PA[:, 0:6 * T], ACT.Sqrt, bias=c("eps", 0, 1)).then_inc(sem("qk_roots"), 1)
                w.up(sem("qk_roots"))
                fn(e["z"], e["z"], ACT.Silu).then_inc(sem("gate_silu"), 1)
                act.wait_ge(sem("ba_ready"), w.up(sem("ba_ready")))
                b_ = e["ba"].rearrange("p (t n) -> p t n", t=2)
                fn(e["beta"].rearrange("p (t n) -> p t n", t=2), b_[:, :, 0:6], ACT.Sigmoid)\
                    .then_inc(sem("beta_ready"), 1)
                fn(e["ea"], p("gdn_a_log", 0, 6), ACT.Exp).then_inc(sem("a_ready"), 1)
                fn(e["t1"], e["t0"], ACT.Abs).then_inc(sem("act_step"), 1)
                act.wait_ge(sem("act_step"), w.up(sem("act_step")))
                fn(e["t1"], e["t1"], ACT.Exp, scale=-1.0).then_inc(sem("act_step"), 1)
                act.wait_ge(sem("act_step"), w.up(sem("act_step")))
                fn(e["t1"], e["t1"], ACT.Ln, bias=c("ones", 0, 1)).then_inc(sem("softplus_ln"), 1)
                act.wait_ge(sem("gdn_vt_psum"), w.up(sem("gdn_vt_psum")))
                act.wait_ge(sem("beta_ready"), w.up(sem("beta_ready")))
                for h in range(GDN_HEADS):
                    for t in range(TT):
                        i = h * TT + t
                        ins = fn(e["vt"][:, i * P:(i + 1) * P], PA[:, i * P:(i + 1) * P], ACT.Identity,
                                 scale=e["beta"][:, t * 6 + h:t * 6 + h + 1])
                ins.then_inc(sem("gdn_vt_ready"), 1)
                for h in range(GDN_HEADS):
                    act.wait_ge(sem("decay_diff_h"), w.up(sem("decay_diff_h")))
                    fn(e["dt"][:, h * 384:(h + 1) * 384], e["dt"][:, h * 384:(h + 1) * 384],
                       ACT.Exp).then_inc(sem("gdn_decay"), 1)
                act.wait_ge(sem("m_psum"), w.up(sem("m_psum")))
                for i in range(12):
                    h, t = i // 2, i % 2
                    ins = fn(e["n"][:, i * P:(i + 1) * P], PA[:, i * P:(i + 1) * P], ACT.Identity,
                             scale=e["beta"][:, t * 6 + h:t * 6 + h + 1])
                ins.then_inc(sem("n_ready"), 1)
                act.wait_ge(sem("nt_psum"), w.up(sem("nt_psum")))
                fn(e["nt"], PB[:, 0:12 * P], ACT.Identity).then_inc(sem("nt_ready"), 1)
                for lev in range(1, PAIR_LEVELS):
                    for g in range(2):
                        part = slice(g * 6 * P, (g + 1) * 6 * P)
                        act.wait_ge(sem("inv_p1"), w.up(sem("inv_p1")))
                        fn(e["p1"][:, part], PA[:, g * 1024:g * 1024 + 6 * P],
                           ACT.Identity).then_inc(sem("inv_p1_ready"), 1)
                        act.wait_ge(sem("inv_p2"), w.up(sem("inv_p2")))
                        fn(e["p2"][:, part], PB[:, g * 1024:g * 1024 + 6 * P],
                           ACT.Identity).then_inc(sem("inv_p2_ready"), 1)
                act.wait_ge(sem("delta0_psum"), w.up(sem("delta0_psum")))
                fn(e["d0"], PA[:, 0:6 * P], ACT.Identity).then_inc(sem("delta0_ready"), 1)
                act.wait_ge(sem("delta1_psum"), w.up(sem("delta1_psum")))
                fn(e["d1"], PA[:, 0:6 * P], ACT.Identity).then_inc(sem("delta1_ready"), 1)
                act.wait_ge(sem("gdn_out_psum"), w.up(sem("gdn_out_psum")))
                fn(e["mix"][:, 0:6 * T], PB[:, 0:6 * T], ACT.Identity).then_inc(sem("heads_ready"), 1)
                head_norm(e["mix"][:, 0:6 * T], e["sq"], 6)
                act.wait_ge(sem("swa_vt_psum"), w.up(sem("swa_vt_psum")))
                fn(e["vbt"], PA[:, 0:12 * P], ACT.Identity).then_inc(sem("swa_vt_ready"), 1)
                attend("swa", e, 6)

            def odd_mixer():
                e = ODD
                split_evacuate("odd_in", 0)
                act.wait_ge(sem("gd_psum"), w.up(sem("gd_psum")))
                fn(e["gd"][0:GATE_RANK, :], PB[0:GATE_RANK, 0:T], ACT.Identity).then_inc(sem("gd_ready"), 1)
                act.wait_ge(taken, product_at["odd_in"][0] + 24)
                fn(e["r"], e["r"], ACT.Silu).then_inc(sem("gate_silu"), 1)
                act.wait_ge(sem("gate_taken"), w.up(sem("gate_taken")))
                fn(e["g2"], e["g1"], ACT.Abs).then_inc(sem("act_step"), 1)
                act.wait_ge(sem("act_step"), w.up(sem("act_step")))
                fn(e["g2"], e["g2"], ACT.Exp, scale=-1.0).then_inc(sem("act_step"), 1)
                act.wait_ge(sem("act_step"), w.up(sem("act_step")))
                fn(e["g2"], e["g2"], ACT.Ln, bias=c("ones", 0, 1)).then_inc(sem("softplus_ln"), 1)
                decay_attention(GLA)
                head_norm(e["mix"][:, 4 * T:8 * T], e["sq"], 4)
                act.wait_ge(sem("diff_vt_psum"), w.up(sem("diff_vt_psum")))
                fn(e["vct"], PA[:, 0:8 * P], ACT.Identity).then_inc(sem("diff_vt_ready"), 1)
                act.wait_ge(sem("lam_sums"), w.up(sem("lam_sums")))
                fn(stat[:, 8:10], stat[:, 6:8], ACT.Exp).then_inc(sem("lam_exp"), 1)
                attend("diff", e, 0)
                act.wait_ge(sem("attention_done"), 2)
                squares(e["mix"][:, 0:4 * T], e["sq"], "head_squares")
                act.wait_ge(sem("head_means"), w.up(sem("head_means")))
                fn(e["sq"], PA[:, 0:4 * T], ACT.Sqrt, bias=c("eps", 0, 1)).then_inc(sem("head_roots"), 1)

            act.wait_ge(sem("params_loaded"), w.up(sem("params_loaded"), 16))
            act.wait_ge(sem("consts_loaded"), w.up(sem("consts_loaded"), 16))
            fn(coef[:, 0:DC], p("c", 0, DC), ACT.Silu).then_inc(sem("cond_ready"), 1)
            act.wait_ge(sem("lb_shifted"), w.up(sem("lb_shifted")))
            fn(coef[:, 40:48], coef[:, 40:48], ACT.Exp).then_inc(sem("lb_exp"), 1)
            act.wait_ge(sem("x_loaded"), w.up(sem("x_loaded"), 16))
            rms()
            evacuate("hg_in", big(0, 40 * T))
            all_taken("hg_in")
            fn(HG_G, HG_G, ACT.Silu).then_inc(sem("gate_silu"), 1)
            act.wait_ge(sem("ada_used"), 12 * DC)
            for d in range(2):
                cfg = HG[d]
                if d == 1:
                    act.wait_ge(sem("decay_out_taken"), w.up(sem("decay_out_taken")))
                logit = cfg["logit"] if d == 0 else chunks(cfg["logit"])[:, :, ::-1]
                fn(cfg["e"] if d == 0 else chunks(cfg["e"]), logit, ACT.Sigmoid)\
                    .then_inc(sem("gate_sigmoid"), 1)
                act.wait_ge(sem("gate_clamped"), w.up(sem("gate_clamped")))
                fn(cfg["e"], cfg["e"], ACT.Ln).then_inc(sem("log_gate"), 1)
                decay_attention(cfg)
            head_norm(HG_MIX, TMP, HG_HEADS)
            act.wait_ge(sem("x_ready"), w.up(sem("x_ready")))
            rms()
            peer(0)
            act.wait_ge(sem("x_ready"), w.up(sem("x_ready")))
            rms()
            evacuate("lru_in", LRU["y"], ACT.Gelu_apprx_tanh, first=8)
            act.wait_ge(sem("lam_negated"), w.up(sem("lam_negated")))
            fn(coef[:, 80:96], coef[:, 64:80], ACT.Abs).then_inc(sem("act_step"), 1)
            act.wait_ge(sem("act_step"), w.up(sem("act_step")))
            fn(coef[:, 80:96], coef[:, 80:96], ACT.Exp, scale=-1.0).then_inc(sem("act_step"), 1)
            act.wait_ge(sem("act_step"), w.up(sem("act_step")))
            fn(coef[:, 80:96], coef[:, 80:96], ACT.Ln, bias=c("ones", 0, 1)).then_inc(sem("softplus_ln"), 1)
            r0, n = STREAM_AT["lru_gates"]
            for i in range(n):
                d, kind, half = i // 4, (i // 2) % 2, i % 2
                act.wait_ge(tile_done, r0 + i + 1)
                for j in range(4):
                    m = half * 4 + j
                    ins = fn(LRU["gate"][d * 2 + kind][:, m * T:(m + 1) * T],
                             PA[:, half * 1024 + j * T:half * 1024 + (j + 1) * T], ACT.Sigmoid,
                             bias=p(("lru_b_a", "lru_b_x")[kind], d * DC + m, 1))
                ins.then_inc(sem("lru_gate_taken"), 1)
            for d in range(2):
                act.wait_ge(sem("log_a"), w.up(sem("log_a")))
                fn(LRU["a"], LRU["la"], ACT.Exp).then_inc(sem("lru_a"), 1)
                fn(LRU["m"], LRU["la"], ACT.Tanh, scale=-1.0).then_inc(sem("lru_tanh"), 1)
                act.wait_ge(sem("mult_square"), w.up(sem("mult_square")))
                fn(LRU["m"], LRU["m"], ACT.Sqrt).then_inc(sem("lru_mult"), 1)
            act.wait_ge(sem("x_ready"), w.up(sem("x_ready")))
            rms()
            peer(1)
            act.wait_ge(sem("x_ready"), w.up(sem("x_ready")))
            rms()
            act.wait_ge(sem("bias_rows_psum"), w.up(sem("bias_rows_psum")))
            fn(ROWS, PA[:, :], ACT.Identity).then_inc(sem("bias_rows_taken"), 1)
            act.wait_ge(sem("bias_rows_stored"), w.up(sem("bias_rows_stored"), 16))
            even_mixer()
            act.wait_ge(sem("x_ready"), w.up(sem("x_ready")))
            layer_norm()
            conv_ffn(0)
            act.wait_ge(sem("x_ready"), w.up(sem("x_ready")))
            layer_norm()
            odd_mixer()
            act.wait_ge(sem("x_ready"), w.up(sem("x_ready")))
            layer_norm()
            conv_ffn(1)
            act.wait_ge(sem("x_ready"), w.up(sem("x_ready")))
            layer_norm()

        @block.vector
        def _(dve):
            w = Tally()
            v = nc.vector
            tt, ts, stt = v.tensor_tensor, v.tensor_scalar, v.scalar_tensor_tensor

            def all_taken(name):
                q0, n = product_at[name]
                dve.wait_ge(taken, q0 + n)

            def loop(n, body):
                full = n // 8
                if full >= 2:
                    with dve.Fori(0, full) as it:
                        for i in range(8):
                            body(i, it)
                else:
                    full = 0
                for i in range(8 * full, n):
                    body(i, 0)

            def convolution(name, n, dst, weight, taps, shifts, bias, u=8):
                q0, r0 = product_at[name][0], STREAM_AT[name][0]
                s0, per = w.value(sem("conv_step")), len(shifts) - 1
                if q0 > 0:
                    dve.wait_ge(taken, q0)
                order = [taps.index(0)] + [i for i in range(len(taps)) if taps[i] != 0]

                def body(i, it):
                    dve.wait_ge(tile_done, it * u + (r0 + i + 1))
                    ps = product_slot(q0 + i)
                    for q, tap in enumerate(order):
                        sh = taps[tap]
                        wc = weight(tap)[:, bass.ds(it * u + i, 1)]
                        out_ = dst[:, bass.ds(it * (u * T) + (i * T + max(0, -sh)), T - abs(sh))]
                        src = ps[:, max(0, sh):T - max(0, -sh)]
                        if q:
                            dve.wait_ge(sem("conv_step"), it * (u * per) + (s0 + i * per + q))
                            ins = stt(out_, src, wc, out_, ALU.mult, ALU.add)
                        elif bias is None:
                            ins = ts(out_, src, wc, None, ALU.mult)
                        else:
                            ins = ts(out_, src, wc, bias[:, bass.ds(it * u + i, 1)], ALU.mult, ALU.add)
                        ins.then_inc(sem("conv_step") if q < per else taken, 1)

                w.up(sem("conv_step"), n * per)
                return body

            def start_run(run):
                split_low(run, 0)
                split_low(run, 1)
                dve.wait_ge(sem("h_high"), w.up(sem("h_high")))
                tt(h_low[:, :], X[:, :], h_high[:, :].bitcast(F32), ALU.subtract)\
                    .then_inc(sem("h_split"), 1)

            def add_product(name, gate=None):
                q0, n = product_at[name]
                r0 = STREAM_AT[name][0]
                dve.wait_ge(taken, q0)
                for m in range(n):
                    dve.wait_ge(tile_done, r0 + m + 1)
                    add_chunk(m, product_slot(q0 + m), gate).then_inc(taken, 1)
                dve.wait_ge(taken, q0 + n)
                v.tensor_copy(stat[:, 15:16], X[:, 0:1]).then_inc(sem("x_ready"), 1)

            def add_chunk(m, src, gate):
                xm = X[:, m * T:(m + 1) * T]
                if gate is None:
                    return stt(xm, xm, ALPHA, src, ALU.mult, ALU.add)
                return stt(xm, src, gate[:, m:m + 1], xm, ALU.mult, ALU.add)

            def add_sums(stream, gate=None):
                r0, n = STREAM_AT[stream]
                dve.wait_ge(tile_done, r0 + n)
                for m in range(DC):
                    ins = add_chunk(m, PA[:, m * T:(m + 1) * T], gate)
                ins.then_inc(sem("x_ready"), 1)

            def modulation(layer, sub, part):
                at = (layer * 6 + sub * 3 + part) * DC
                return mod[:, at:at + DC]

            def gains(layer, sub):
                at = 8 + (layer * 2 + sub) * DC
                return coef[:, at:at + DC]

            def ada(first, last):
                def part(g):
                    for k in range(DC):
                        dve.wait_ge(ada_loaded[k], (g + 1) * 16)
                        dst = ADA_SUMS[:, bass.ds(g * D, D)]
                        src, cond = ADA_RING[:, k * TILE:(k + 1) * TILE], coef[:, k:k + 1]
                        if k:
                            dve.wait_ge(sem("ada_used"), g * DC + k)
                            ins = stt(dst, src, cond, dst, ALU.mult, ALU.add)
                        else:
                            ins = ts(dst, src, cond, None, ALU.mult)
                        ins.then_inc(sem("ada_used"), 1)
                    dve.wait_ge(sem("ada_used"), g * DC + DC)
                    v.tensor_copy(stat[:, 14:15], ADA_SUMS[:, 0:1]).then_inc(sem("ada_sums_ready"), 1)

                with dve.Fori(first, last) as g:
                    part(g)

            def modulate(first, last):
                dve.wait_ge(sem("ada_psum"), w.up(sem("ada_psum")))
                cols = slice(first * DC, last * DC)
                tt(mod[:, cols], PA[:, cols], p("b_ada", first * DC, (last - first) * DC), ALU.add)\
                    .then_inc(sem("dve_step"), 1)
                dve.wait_ge(sem("dve_step"), w.up(sem("dve_step")))
                for layer in range(2):
                    for sub in range(2):
                        if first <= layer * 6 + sub * 3 + 1 < last:
                            ins = stt(gains(layer, sub), modulation(layer, sub, 1), 1.0,
                                      p("norm_g", (layer * 2 + sub) * DC, DC), ALU.add, ALU.mult)
                ins.then_inc(sem("mod_ready"), 1)
                dve.wait_ge(sem("mod_ready"), w.up(sem("mod_ready")))

            def normalize(dst, gain, shift, name):
                dve.wait_ge(sem("root_ready"), w.up(sem("root_ready")))
                v.reciprocal(inv[:, :], inv[:, :]).then_inc(sem("dve_step"), 1)
                dve.wait_ge(sem("dve_step"), w.up(sem("dve_step")))
                tt(chunks(dst), chunks(X[:, :]), over(inv[:, :], DC), ALU.mult).then_inc(sem("dve_step"), 1)
                dve.wait_ge(sem("dve_step"), w.up(sem("dve_step")))
                for k in range(DC):
                    dk = dst[:, k * T:(k + 1) * T]
                    if shift is None:
                        ins = ts(dk, dk, gain[:, k:k + 1], None, ALU.mult)
                    else:
                        ins = ts(dk, dk, gain[:, k:k + 1], shift[:, k:k + 1], ALU.mult, ALU.add)
                if name == "x_normed":
                    ins.then_inc(sem("dve_step"), 1)
                    dve.wait_ge(sem("dve_step"), w.up(sem("dve_step")))
                    ins = v.tensor_copy(stat[:, 13:14], X[:, 0:1])
                ins.then_inc(sem(name), 1)

            def layer_norm(i):
                dve.wait_ge(sem("mean_ready"), w.up(sem("mean_ready")))
                tt(chunks(X[:, :]), chunks(X[:, :]), over(PA[:, 0:T], DC), ALU.subtract)\
                    .then_inc(sem("centered"), 1)
                dve.wait_ge(sem("centered"), w.up(sem("centered")))
                normalize(X[:, :], p("ln_g", i * DC, DC), p("ln_b", i * DC, DC), "x_normed")

            def head_norm(o, sq, n, gain, gate):
                dve.wait_ge(sem("head_roots"), w.up(sem("head_roots")))
                v.reciprocal(sq, sq).then_inc(sem("dve_step"), 1)
                dve.wait_ge(sem("dve_step"), w.up(sem("dve_step")))
                tt(o, o, sq, ALU.mult).then_inc(sem("dve_step"), 1)
                dve.wait_ge(sem("dve_step"), w.up(sem("dve_step")))
                if gate is not None:
                    dve.wait_ge(sem("gate_silu"), w.up(sem("gate_silu")))
                for h in range(n):
                    oh = o[:, h * T:(h + 1) * T]
                    if gate is None:
                        ins = ts(oh, oh, gain(h), 1.0 - LAM_INIT, ALU.mult, ALU.mult)
                    else:
                        ins = stt(oh, oh, gain(h), gate[:, h * T:(h + 1) * T], ALU.mult, ALU.mult)
                return ins

            def cumulate(cfg):
                for i in range(cfg["chunks"]):
                    ins = v.tensor_tensor_scan(cfg["b"][:, i * T:(i + 1) * T], wide(c("ones", 0, 1), P, T),
                                               cfg["e"][:, i * T:(i + 1) * T], 0.0, ALU.mult, ALU.add)
                ins.then_inc(sem("dve_step"), 1)
                dve.wait_ge(sem("dve_step"), w.up(sem("dve_step")))

            def decay_attention(cfg):
                b, k_, q_, kh, qh = (cfg[x] for x in ("b", "k", "q", "kh", "qh"))
                es = [cfg["e"], cfg["e_next"]]
                per = cfg["heads"] // cfg["chunks"]
                nm = cfg["chunks"] * TT

                def by_rows(x, n):
                    return x.rearrange("p (r n c) -> p r n c", r=per, n=n)

                def diff(lev, e):
                    size = 2 << lev if lev < DIAGONAL else T
                    bv, ev = (x.rearrange("p (n l) -> p n l", l=size) for x in (b, e))
                    ref = bv[:, :, size // 2 - 1:size // 2]
                    tt(ev, bv, wide(ref, P, b.shape[1] // size, size), ALU.subtract)\
                        .then_inc(sem("decay_diff"), 1)

                v.memset(cfg["at"], 0.0).then_inc(sem("dve_step"), 1)
                dve.wait_ge(sem("dve_step"), w.up(sem("dve_step")))

                def masked(lev):
                    src = (PB, PA)[lev % 2]
                    if lev == CROSS:
                        n = cfg["chunks"]
                        got = by_rows(src[:, :], 2048 // per // P)[:, :, 0:n, :]
                        v.tensor_copy(by_rows(cfg["ax"], n), got).then_inc(sem("decay_masked"), 1)
                    else:
                        mask = ident if lev == DIAGONAL else c("pairs", lev * P, P)
                        got = by_rows(src[:, :], 2048 // per // P)[:, :, 0:nm, :]
                        v.copy_predicated(by_rows(cfg["at"], nm),
                                          wide(mask.unsqueeze(1).unsqueeze(1), P, per, nm, P).bitcast(U32),
                                          got).then_inc(sem("decay_masked"), 1)
                    dve.wait_ge(sem("decay_masked"), w.up(sem("decay_masked")))

                order = [*range(PAIR_LEVELS), CROSS]
                diff(0, es[0])
                diff(1, es[1])
                for lev in range(CROSS + 1):
                    if lev:
                        dve.wait_ge(sem("decay_scores"), w.up(sem("decay_scores")))
                    if lev != DIAGONAL:
                        i = order.index(lev)
                        dve.wait_ge(sem("decay_exp"), w.up(sem("decay_exp")))
                        tt(kh, k_, es[i % 2], ALU.mult)
                        tt(qh, q_, es[i % 2], ALU.mult).then_inc(sem("decay_keys_ready"), 1)
                        if i + 2 < len(order):
                            dve.wait_ge(sem("decay_keys_ready"), w.up(sem("decay_keys_ready")))
                            diff(order[i + 2], es[i % 2])
                        else:
                            w.up(sem("decay_keys_ready"))
                    if lev:
                        masked(lev - 1)
                dve.wait_ge(sem("decay_scores"), w.up(sem("decay_scores")))
                masked(CROSS)
                dve.wait_ge(sem("decay_out"), w.up(sem("decay_out")))

            def top16(scores, spare, n, width, val, idx):
                def row(a, i):
                    return a[:, i * width:(i + 1) * width]
                for half in range(2):
                    src = spare if half else scores
                    for i in range(n):
                        ins = v.max(val[:, i * 16 + half * 8:i * 16 + half * 8 + 8], row(src, i))
                    ins.then_inc(sem("dve_step"), 1)
                    dve.wait_ge(sem("dve_step"), w.up(sem("dve_step")))
                    for i in range(n):
                        at = slice(i * 16 + half * 8, i * 16 + half * 8 + 8)
                        ins = v.max_index(idx[:, at], val[:, at], row(src, i))
                        if not half:
                            ins = v.match_replace(row(spare, i), val[:, at], row(src, i), -3e38)
                    ins.then_inc(sem("dve_step"), 1)
                    dve.wait_ge(sem("dve_step"), w.up(sem("dve_step")))

            def peer(layer):
                nh, hk = PEER_HEADS, PEER_HEADS * TOPK
                idx, cpos, high, low = (x.bitcast(U32) for x in (IDX, CPOS, HIGH, LOW))
                dve.wait_ge(sem("key_scores"), w.up(sem("key_scores"), TT))
                dve.wait_ge(sem("h_high"), w.up(sem("h_high")))
                tt(h_low[:, :], H[:, :], h_high[:, :].bitcast(F32), ALU.subtract)\
                    .then_inc(sem("h_split"), 1)
                for t in range(TT):
                    top16(KEY_SCORES[t], SPARE, 2 * nh, NKEYS, VAL, idx)
                    v.tensor_copy(IDX_F, idx).then_inc(sem("dve_step"), 1)
                    dve.wait_ge(sem("dve_step"), w.up(sem("dve_step")))
                    s = VAL.rearrange("p (h s a) -> p h s a", s=2, a=TOPK)
                    tt(CAND.rearrange("p (h a b) -> p h a b", a=TOPK, b=TOPK),
                       wide(s[:, :, 0, :].unsqueeze(3), P, nh, TOPK, TOPK),
                       wide(s[:, :, 1, :].unsqueeze(2), P, nh, TOPK, TOPK), ALU.add).then_inc(sem("dve_step"), 1)
                    dve.wait_ge(sem("dve_step"), w.up(sem("dve_step")))
                    top16(CAND, CAND_SPARE, nh, TOPK * TOPK, CVAL, cpos)
                    v.tensor_scalar(high, cpos, 4, None, ALU.logical_shift_right)
                    v.tensor_scalar(low, cpos, 15, None, ALU.bitwise_and).then_inc(sem("dve_step"), 1)
                    dve.wait_ge(sem("dve_step"), w.up(sem("dve_step")))
                    v.tensor_copy(HIGH_F, high)
                    v.tensor_copy(LOW_F, low).then_inc(sem("dve_step"), 1)
                    dve.wait_ge(sem("dve_step"), w.up(sem("dve_step")))
                    ids = IDX_F.rearrange("p (h s a) -> p h s a", s=2, a=TOPK)
                    for side, rank in enumerate((HIGH_F, LOW_F)):
                        pick = PICK.rearrange("p (n a) -> p n a", a=TOPK)
                        tt(pick, wide(rank.unsqueeze(2), P, hk, TOPK), over(c("iota16"), hk),
                           ALU.is_equal).then_inc(sem("dve_step"), 1)
                        dve.wait_ge(sem("dve_step"), w.up(sem("dve_step")))
                        pick4 = PICK.rearrange("p (h k a) -> p h k a", k=TOPK, a=TOPK)
                        tt(pick4, pick4, wide(ids[:, :, side, :].unsqueeze(2), P, nh, TOPK, TOPK),
                           ALU.mult).then_inc(sem("dve_step"), 1)
                        dve.wait_ge(sem("dve_step"), w.up(sem("dve_step")))
                        v.tensor_reduce(chosen(t, side), pick, AX.X, ALU.add).then_inc(sem("dve_step"), 1)
                        dve.wait_ge(sem("dve_step"), w.up(sem("dve_step")))
                    cv = CVAL.rearrange("p (h k) -> p h k", k=TOPK)
                    gt = GATE.rearrange("p (h k) -> p h k", k=TOPK)
                    tt(gt, cv, wide(cv[:, :, 0:1], P, nh, TOPK), ALU.subtract).then_inc(sem("gate_diff"), 1)
                    dve.wait_ge(sem("gate_exp"), w.up(sem("gate_exp")))
                    v.tensor_reduce(GSUM, gt, AX.X, ALU.add).then_inc(sem("dve_step"), 1)
                    dve.wait_ge(sem("dve_step"), w.up(sem("dve_step")))
                    v.reciprocal(GSUM, GSUM).then_inc(sem("dve_step"), 1)
                    dve.wait_ge(sem("dve_step"), w.up(sem("dve_step")))
                    tt(chosen(t, 2).rearrange("p (h k) -> p h k", k=TOPK), gt,
                       wide(GSUM.unsqueeze(2), P, nh, TOPK), ALU.mult).then_inc(sem("chosen_ready"), 1)
                dve.wait_ge(sem("slots_ready"), w.up(sem("slots_ready")))
                g0 = layer * 64

                def group(r, it):
                    if not isinstance(it, int) or g0 + r >= 2:
                        dve.wait_ge(sem("gates_psum"), it * 4 + (g0 + r - 1))
                    for j in range(4):
                        at = ((r % 2) * 4 + j) * P
                        tok = it * 16 + (r * 4 + j)
                        ts(onehot_a[:, at:at + P], c("iota"), slots[:, bass.ds(tok, 1)],
                           slots[:, bass.ds(tok + 2 * T, 1)], ALU.is_equal, ALU.mult)
                    four = chunks(onehot_b[:, (r % 2) * 4 * P:(r % 2 + 1) * 4 * P], P)
                    column = slots[:, bass.ds(it * 16 + (r * 4 + T), 4)]
                    ins = tt(four, over(c("iota"), 4), wide(column.unsqueeze(2), P, 4, P), ALU.is_equal)
                    ins.then_inc(sem("onehots_ready"), 1)

                gates = chunks(BIG[:, :])

                def fold(g, it):
                    dve.wait_ge(sem("gates_copied"), it * 4 + (g0 + g + 1))
                    dst = gates[:, MAIN:, bass.ds(it * 16 + g * 4, 4)]
                    bank = PA[:, (g % 4) * 512:(g % 4 + 1) * 512]
                    tt(dst, bank.rearrange("p (t j) -> p j t", t=4)[:, MAIN:, :], dst, ALU.mult)\
                        .then_inc(sem("gates_folded"), 1)

                dve.wait_ge(sem("early_gelu"), (layer + 1) * EARLY)
                for r in range(4):
                    group(r, 0)
                    if r >= 2:
                        fold(r - 2, 0)
                with dve.Fori(1, 16) as it:
                    for r in range(4):
                        group(r, it)
                        fold(r - 2, it)
                fold(62, 0)
                fold(63, 0)
                r0, n = STREAM_AT[f"experts{layer}"]
                dve.wait_ge(sem("gates_psum"), g0 + 64)

                run, c0 = f"experts{layer}", layer * NKEYS

                def gated(j, it=0):
                    dve.wait_ge(sem("gelu_ready"), it * 4 + (layer * MAIN + j + 1))
                    a = pair(act_v, j)
                    tt(a, a, BIG[:, bass.ds(it * (4 * T) + j * T, T)], ALU.mult).then_inc(sem("gated"), 1)
                    dve.wait_ge(sem("gated"), it * 4 + (layer * MAIN + j + 1))
                    split_gated(c0 + j, a, r0 + down_at(j - 2) if j >= 2 else None, it, 8)

                def column(j, it=0):
                    split_low(run, 2 * j, it)
                    split_low(run, 2 * j + 1, it)
                    gated(j, it)

                def late(j, it=0):
                    split_low(run, down_at(j), it, 4)
                    split_gated(c0 + j, BIG[:, bass.ds(it * (4 * T) + j * T, T)],
                                r0 + down_at(j - 2), it)

                split_low(run, 0)
                split_low(run, 1)
                split_low(run, 2)
                gated(0)
                split_low(run, 3)
                gated(1)
                steps = (MAIN - 2) // 4
                with dve.Fori(0, steps) as it:
                    for j in range(2, 6):
                        column(j, it)
                for j in range(4 * steps + 2, MAIN):
                    column(j)
                for j in range(MAIN, MAIN + 2):
                    late(j)
                steps = (EARLY - 2) // 4
                with dve.Fori(0, steps) as it:
                    for j in range(MAIN + 2, MAIN + 6):
                        late(j, it)
                for j in range(MAIN + 2 + 4 * steps, NKEYS):
                    late(j)
                add_sums(f"late{layer}", modulation(layer, 1, 2))

            def split_low(run, k, it=0, step=8):
                n, s = STREAM_AT[run][0] + k, SPLIT_AT[run][0] + k
                for b in range(2):
                    dve.wait_ge(sem("high_ready"), it * (2 * step) + (2 * s + b + 1))
                    at = (n % RING) * TILE + b * HALF
                    tt(tile_half(w_low, s, b), ring[:, at:at + HALF], tile_half(w_high, s, b).bitcast(F32),
                       ALU.subtract).then_inc(sem("low_ready"), 1)

            def split_gated(j, a, used, it=0, step=4):
                if used is not None:
                    dve.wait_ge(tile_done, it * step + (used + 1))
                v.tensor_copy(pair(a_high, j), a).then_inc(sem("gated_high"), 1)
                dve.wait_ge(sem("gated_high"), it * 4 + (j + 1))
                tt(pair(a_low, j), a, pair(a_high, j).bitcast(F32), ALU.subtract)\
                    .then_inc(sem("gated_ready"), 1)

            def conv_ffn(i):
                run = f"up{i}"
                q0, r0, c0 = product_at[run][0], STREAM_AT[run][0], 2 * NKEYS + i * FC
                wt = [p("ffn_conv_w", i * 132 + tap * 44, 44) for tap in range(2)]
                s0 = w.value(sem("conv_step"))
                w.up(sem("conv_step"), 2 * FC)

                def taps(j, it):
                    dve.wait_ge(sem("conv_center"), it * 4 + (i * 2 * FC + j + 1))
                    for tap, sh in ((1, 1), (0, 2)):
                        if tap == 0:
                            dve.wait_ge(sem("conv_step"), it * 4 + (s0 + j + 1))
                        dst = BIG[:, bass.ds(it * (4 * T) + (j * T + sh), T - sh)]
                        stt(dst, product_slot(q0 + j)[:, 0:T - sh], wt[tap][:, bass.ds(it * 4 + j, 1)], dst,
                            ALU.mult, ALU.add).then_inc((taken, sem("conv_step"))[tap], 1)

                def gate(j, it):
                    dve.wait_ge(taken, it * 4 + (q0 + FC + j + 1))
                    dve.wait_ge(sem("ffn_gate_ready"), it * 4 + (i * FC + j + 1))
                    hidden = BIG[:, bass.ds(it * (4 * T) + j * T, T)]
                    tt(hidden, hidden, BIG[:, bass.ds(it * (4 * T) + (FC + j) * T, T)], ALU.mult)\
                        .then_inc(sem("ffn_hidden_ready"), 1)

                def tile(k, it):
                    split_low(run, k, it, 4)
                    if 2 <= k < 2 * FC + 2:
                        taps(k - 2, it)
                    if FC + 2 <= k < 2 * FC + 2:
                        gate(k - 2 - FC, it)
                    if k >= 2 * FC:
                        j = k - 2 * FC
                        dve.wait_ge(sem("ffn_hidden_ready"), it * 4 + (i * FC + j + 1))
                        split_gated(c0 + j, BIG[:, bass.ds(it * (4 * T) + j * T, T)],
                                    r0 + k - 2 if j >= 2 else None, it)

                start_run(run)
                spans(dve, tile, (2, FC + 2, 2 * FC, 2 * FC + 2, 3 * FC))
                add_sums(f"down{i}")

            def attend(kind, e):
                groups = 3 if kind == "swa" else 2
                sums = 1 if kind == "swa" else 2

                def biased(n):
                    h, t = n // TT, n % TT
                    st, prob = stat[:, 16 + 4 * (n % 2):], e["prob"][n % 2]
                    pr = chunks(prob)
                    if n >= 2:
                        dve.wait_ge(sem("attention_wt_psum"), w.up(sem("attention_wt_psum")))
                    dve.wait_ge(sem("attention_scores"), w.up(sem("attention_scores")))
                    bias = over(e["bias"][:, (t * 4 + h) * T:(t * 4 + h + 1) * T], groups)
                    src = chunks(PA[:, 0:3 * T]) if kind == "swa" else chunks(PA[:, 0:1024], 512)[:, :, 0:T]
                    stt(pr, src, SWA_DH ** -0.5, bias, ALU.mult, ALU.add)\
                        .then_inc(sem("attention_scores_taken"), 1)
                    dve.wait_ge(sem("attention_scores_taken"), w.up(sem("attention_scores_taken")))
                    if kind == "swa":
                        tt(prob, prob, e["neg"][:, t * 3 * T:(t + 1) * 3 * T],
                           ALU.add).then_inc(sem("dve_step"), 1)
                        dve.wait_ge(sem("dve_step"), w.up(sem("dve_step")))
                        v.reduce_max(st[:, 0:1], prob, AX.X).then_inc(sem("dve_step"), 1)
                    else:
                        tt(pr, pr, over(e["neg"][:, t * T:(t + 1) * T], 2),
                           ALU.add).then_inc(sem("dve_step"), 1)
                        dve.wait_ge(sem("dve_step"), w.up(sem("dve_step")))
                        v.reduce_max(st[:, 0:2], pr, AX.X).then_inc(sem("dve_step"), 1)
                    dve.wait_ge(sem("dve_step"), w.up(sem("dve_step")))
                    ts(st[:, 0:sums], st[:, 0:sums], -1.0, None, ALU.mult).then_inc(sem("attention_max"), 1)

                def weights(n):
                    st, prob = stat[:, 16 + 4 * (n % 2):], e["prob"][n % 2]
                    pr = chunks(prob)
                    dve.wait_ge(sem("attention_exp"), w.up(sem("attention_exp"), sums))
                    v.reciprocal(st[:, 2:2 + sums], st[:, 2:2 + sums]).then_inc(sem("dve_step"), 1)
                    dve.wait_ge(sem("dve_step"), w.up(sem("dve_step")))
                    if kind == "swa":
                        ts(prob, prob, st[:, 2:3], None, ALU.mult).then_inc(sem("attention_weights"), 1)
                    else:
                        tt(st[:, 3:4], st[:, 3:4], stat[:, 4:5], ALU.mult).then_inc(sem("dve_step"), 1)
                        dve.wait_ge(sem("dve_step"), w.up(sem("dve_step")))
                        ts(pr[:, 0, :], pr[:, 0, :], st[:, 2:3], None, ALU.mult).then_inc(sem("dve_step"), 1)
                        dve.wait_ge(sem("dve_step"), w.up(sem("dve_step")))
                        stt(pr[:, 0, :], pr[:, 1, :], st[:, 3:4], pr[:, 0, :], ALU.mult, ALU.add)\
                            .then_inc(sem("attention_weights"), 1)

                biased(0)
                for n in range(4 * TT):
                    if n + 1 < 4 * TT:
                        biased(n + 1)
                    weights(n)
                for _ in range(2):
                    w.up(sem("attention_wt_psum"))

            def even_mixer():
                e = EVEN
                dve.wait_ge(sem("bias_rows_stored"), w.up(sem("bias_rows_stored"), 16))
                convolved = convolution("even_in", 18, BIG[:, :], lambda tap: p("gdn_conv_w", tap * 18, 18),
                                        [-3, -2, -1, 0], [0] * 4, None, 4)

                def tile(k, it):
                    split_low("even_in", k, it, 4)
                    if k - 2 < 18:
                        convolved(k - 2, it)

                start_run("even_in")
                spans(dve, tile, (2, 20, 42))
                dve.wait_ge(sem("ba_psum"), w.up(sem("ba_psum")))
                for t in range(TT):
                    ins = v.tensor_copy(e["ba"][:, t * 12:(t + 1) * 12], PB[:, t * 512:t * 512 + 12])
                ins.then_inc(sem("dve_step"), 1)
                dve.wait_ge(sem("dve_step"), w.up(sem("dve_step")))
                ba = e["ba"].rearrange("p (t n) -> p t n", t=2)
                tt(e["t0"].rearrange("p (t n) -> p t n", t=2), ba[:, :, 6:12],
                   over(p("gdn_dt_bias", 0, 6), TT), ALU.add).then_inc(sem("ba_ready"), 1)
                dve.wait_ge(sem("ba_ready"), w.up(sem("ba_ready")))
                for i, (x, y) in enumerate((("q", "x"), ("k", "y"))):
                    dve.wait_ge(sem("qk_roots"), w.up(sem("qk_roots")))
                    v.reciprocal(e[y], e[y]).then_inc(sem("dve_step"), 1)
                    dve.wait_ge(sem("dve_step"), w.up(sem("dve_step")))
                    if i == 0:
                        ins = stt(e["q"], e["q"], float(P) ** -0.5, e[y], ALU.mult, ALU.mult)
                        ins.then_inc(sem("dve_step"), 1)
                        dve.wait_ge(sem("dve_step"), w.up(sem("dve_step")))
                    else:
                        tt(e["k"], e["k"], e[y], ALU.mult).then_inc(sem("qk_normed"), 1)
                        dve.wait_ge(sem("qk_normed"), w.up(sem("qk_normed")))
                dve.wait_ge(sem("softplus_ln"), w.up(sem("softplus_ln")))
                stt(e["t0"], e["t0"], 0.0, e["t1"], ALU.max, ALU.add).then_inc(sem("dve_step"), 1)
                dve.wait_ge(sem("dve_step"), w.up(sem("dve_step")))
                dve.wait_ge(sem("a_ready"), w.up(sem("a_ready")))
                g2 = e["g"].rearrange("p (t n) -> p t n", t=2)
                stt(g2, e["t0"].rearrange("p (t n) -> p t n", t=2), -1.0, over(e["ea"], 2),
                    ALU.mult, ALU.mult).then_inc(sem("dve_step"), 1)
                dve.wait_ge(sem("dve_step"), w.up(sem("dve_step")))
                dve.wait_ge(sem("beta_ready"), w.up(sem("beta_ready")))
                ts(e["nbeta"], e["beta"], -1.0, None, ALU.mult).then_inc(sem("g_ready"), 1)
                dve.wait_ge(sem("g_ready"), w.up(sem("g_ready")))
                dve.wait_ge(sem("gam_col_psum"), w.up(sem("gam_col_psum")))
                for t in range(TT):
                    ins = v.tensor_copy(e["gam"][:, t * 6:t * 6 + 6], PB[:, 1024 + t * 8:1024 + t * 8 + 6])
                ins.then_inc(sem("dve_step"), 1)
                dve.wait_ge(sem("dve_step"), w.up(sem("dve_step")))
                for h in range(GDN_HEADS):
                    dve.wait_ge(sem("gam_row_psum"), w.up(sem("gam_row_psum")))
                    src, dt = PB[:, (h % 2) * 512:(h % 2) * 512 + T], e["dt"][:, h * 384:(h + 1) * 384]
                    ts(dt[:, 0:T], src, e["gam"][:, h:h + 1], 0.0, ALU.subtract, ALU.min)
                    ts(dt[:, T:T + P], src[:, P:T], e["gam"][:, 6 + h:7 + h], 0.0, ALU.subtract, ALU.min)\
                        .then_inc(sem("decay_taken"), 1)
                    dve.wait_ge(sem("decay_taken"), w.up(sem("decay_taken")))
                    v.tensor_copy(stat[:, 12:13], dt[:, 0:1]).then_inc(sem("decay_diff_h"), 1)
                dve.wait_ge(sem("gdn_decay"), w.up(sem("gdn_decay"), GDN_HEADS))
                dts = e["dt"].rearrange("p (h c) -> p h c", h=GDN_HEADS)
                up_incl = over(c("tri"), GDN_HEADS)
                mt = e["mt"].rearrange("p (h t c) -> p h t c", t=TT, c=P)
                for i in range(2):
                    for j in range(3):
                        n = i * 3 + j
                        dve.wait_ge(sem("pair_psum"), w.up(sem("pair_psum")))
                        src = chunks((PA, PB)[n % 2][:, 0:6 * P], P)
                        dcy = dts[:, :, j * P:(j + 1) * P]
                        if i == 0:
                            dst = chunks(e["m01"], P) if j == 1 else mt[:, :, 0 if j == 0 else 1, :]
                        else:
                            dst = chunks((e["qk0"], e["qk01"], e["qk1"])[j], P)
                        ins = tt(dst, src, dcy, ALU.mult)
                        if j != 1:
                            ins.then_inc(sem("dve_step"), 1)
                            dve.wait_ge(sem("dve_step"), w.up(sem("dve_step")))
                            ins = tt(dst, dst, up_incl, ALU.mult)
                            if i == 0:
                                ins.then_inc(sem("dve_step"), 1)
                                dve.wait_ge(sem("dve_step"), w.up(sem("dve_step")))
                                ins = tt(dst, dst, over(c("strict"), GDN_HEADS), ALU.mult)
                        ins.then_inc(sem("pair_taken"), 1)
                dve.wait_ge(sem("pair_taken"), w.up(sem("pair_taken"), 6))
                n3, nt3, x3, y3, c3, ct3 = (chunks(e[k], P) for k in ("n", "nt", "x", "y", "c", "ct"))
                dve.wait_ge(sem("low_masks_loaded"), w.up(sem("low_masks_loaded"), 16))
                dve.wait_ge(sem("n_ready"), w.up(sem("n_ready")))
                dve.wait_ge(sem("nt_ready"), w.up(sem("nt_ready")))

                def blocks(lev, g):
                    own = slice(6 * g, 6 * g + 6)
                    tt(c3[:, own], n3[:, own], over(e["low"][:, lev * P:(lev + 1) * P], 6), ALU.mult)
                    return tt(ct3[:, own], nt3[:, own], over(c("pairs", lev * P, P), 6), ALU.mult)

                for g in range(2):
                    blocks(0, g).then_inc(sem("dve_step"), 1)
                dve.wait_ge(sem("dve_step"), w.up(sem("dve_step"), 2))
                tt(x3, over(ident, 12), c3, ALU.subtract)
                tt(y3, over(ident, 12), ct3, ALU.subtract).then_inc(sem("dve_step"), 1)
                dve.wait_ge(sem("dve_step"), w.up(sem("dve_step")))
                for g in range(2):
                    blocks(1, g).then_inc(sem("inverse_step"), 1)
                for lev in range(1, PAIR_LEVELS):
                    if lev < PAIR_LEVELS - 1:
                        for g in range(2):
                            dve.wait_ge(sem("inv_p2"), w.up(sem("inv_p2")))
                            blocks(lev + 1, g)
                    for g in range(2):
                        dve.wait_ge(sem("inverse_step"), w.up(sem("inverse_step")))
                        dve.wait_ge(sem("inv_xpx"), w.up(sem("inv_xpx")))
                        dve.wait_ge(sem("inv_ypy"), w.up(sem("inv_ypy")))
                        part, src = slice(g * 6 * P, (g + 1) * 6 * P), slice(g * 1024, g * 1024 + 6 * P)
                        tt(e["x"][:, part], e["x"][:, part], PA[:, src], ALU.subtract)
                        tt(e["y"][:, part], e["y"][:, part], PB[:, src], ALU.subtract)\
                            .then_inc(sem("inverse_step"), 1)
                dve.wait_ge(sem("carry_psum"), w.up(sem("carry_psum")))
                vt = e["vt"].rearrange("p (h t c) -> p h t c", t=TT, c=P)
                for h in range(GDN_HEADS):
                    ins = stt(e["r1"][:, h * P:(h + 1) * P], PB[:, h * P:(h + 1) * P],
                              e["nbeta"][:, 6 + h:7 + h], vt[:, h, 1, :], ALU.mult, ALU.add)
                ins.then_inc(sem("carry_ready"), 1)
                head_norm(e["mix"][:, 0:6 * T], e["sq"], 6, lambda h: p("gdn_norm_w"), e["z"])\
                    .then_inc(sem("gdn_done"), 1)
                dve.wait_ge(sem("attention_tables_loaded"), w.up(sem("attention_tables_loaded"), 48))
                attend("swa", e)
                dve.wait_ge(sem("attention_done"), w.up(sem("attention_done")))
                add_product("even_out")

            def odd_mixer():
                e = ODD
                start_run("odd_in")
                spans(dve, lambda k, it: split_low("odd_in", k, it, 4), (2, 24))
                dve.wait_ge(sem("gate_psum"), w.up(sem("gate_psum")))
                for i in range(2):
                    ins = ts(e["g1"][:, i * T:(i + 1) * T], PB[:, 512 + i * 512:512 + i * 512 + T],
                             p("gla_b_gate", i, 1), None, ALU.add)
                ins.then_inc(sem("gate_taken"), 1)
                dve.wait_ge(sem("gate_taken"), w.up(sem("gate_taken")))
                all_taken("odd_in")
                dve.wait_ge(sem("softplus_ln"), w.up(sem("softplus_ln")))
                stt(e["g1"], e["g1"], 0.0, e["g2"], ALU.min, ALU.subtract).then_inc(sem("dve_step"), 1)
                dve.wait_ge(sem("dve_step"), w.up(sem("dve_step")))
                ts(GLA["e"], e["g1"], 1.0 / GLA_TAU, None, ALU.mult)
                ts(GLA["q"], GLA["q"], GLA_DK ** -0.5, None, ALU.mult).then_inc(sem("dve_step"), 1)
                dve.wait_ge(sem("dve_step"), w.up(sem("dve_step")))
                cumulate(GLA)
                decay_attention(GLA)
                o = e["mix"][:, 4 * T:8 * T]
                v.tensor_copy(o, PA[:, 0:4 * T]).then_inc(sem("heads_ready"), 1)
                dve.wait_ge(sem("heads_ready"), w.up(sem("heads_ready")))
                head_norm(o, e["sq"], 4, lambda h: p("gla_norm_w"), e["r"]).then_inc(sem("dve_step"), 1)
                dve.wait_ge(sem("dve_step"), w.up(sem("dve_step")))
                dve.wait_ge(sem("attention_tables_loaded"), w.up(sem("attention_tables_loaded"), 64))
                lv = e["lamv"].rearrange("p (a b c) -> p a b c", a=2, b=2)
                tt(lv[:, :, 0, :], lv[:, :, 0, :], lv[:, :, 1, :], ALU.mult).then_inc(sem("dve_step"), 1)
                dve.wait_ge(sem("dve_step"), w.up(sem("dve_step")))
                v.tensor_reduce(stat[:, 6:8], lv[:, :, 0, :], AX.X, ALU.add).then_inc(sem("lam_sums"), 1)
                dve.wait_ge(sem("lam_exp"), w.up(sem("lam_exp")))
                tt(stat[:, 4:5], stat[:, 9:10], stat[:, 8:9], ALU.subtract).then_inc(sem("dve_step"), 1)
                dve.wait_ge(sem("dve_step"), w.up(sem("dve_step")))
                ts(stat[:, 4:5], stat[:, 4:5], -LAM_INIT, None, ALU.add).then_inc(sem("dve_step"), 1)
                dve.wait_ge(sem("dve_step"), w.up(sem("dve_step")))
                attend("diff", e)
                head_norm(e["mix"][:, 0:4 * T], e["sq"], 4, lambda h: p("diff_norm_w"), None).then_inc(sem("dve_step"), 1)
                dve.wait_ge(sem("dve_step"), w.up(sem("dve_step")))
                v.tensor_copy(stat[:, 11:12], e["mix"][:, 0:1]).then_inc(sem("mix_ready"), 1)
                add_product("odd_out")

            dve.wait_ge(sem("params_loaded"), w.up(sem("params_loaded"), 16))
            dve.wait_ge(sem("consts_loaded"), w.up(sem("consts_loaded"), 16))
            lb, om = coef[:, 40:48], coef[:, 48:56]
            tt(lb, p("hg_lb"), p("hg_lb"), ALU.subtract).then_inc(sem("lb_shifted"), 1)
            dve.wait_ge(sem("lb_exp"), w.up(sem("lb_exp")))
            v.reciprocal(om, lb).then_inc(sem("dve_step"), 1)
            dve.wait_ge(sem("dve_step"), w.up(sem("dve_step")))
            tt(lb, lb, om, ALU.mult).then_inc(sem("dve_step"), 1)
            dve.wait_ge(sem("dve_step"), w.up(sem("dve_step")))
            tt(lb, lb, lb, ALU.subtract).then_inc(sem("dve_step"), 1)
            dve.wait_ge(sem("dve_step"), w.up(sem("dve_step")))
            ts(om, lb, -1.0, 1.0, ALU.mult, ALU.add).then_inc(sem("dve_step"), 1)
            dve.wait_ge(sem("dve_step"), w.up(sem("dve_step")))
            dve.wait_ge(sem("cond_ready"), w.up(sem("cond_ready")))
            ada(0, 2)
            modulate(0, 2)
            dve.wait_ge(sem("x_loaded"), w.up(sem("x_loaded"), 16))
            normalize(H[:, :], gains(0, 0), modulation(0, 0, 0), "h_ready")
            ada(2, 12)
            all_taken("hg_in")
            for d in range(2):
                cfg = HG[d]
                if d == 1:
                    v.tensor_copy(chunks(cfg["q"]), chunks(HG[0]["q"])[:, :, ::-1])
                dve.wait_ge(sem("gate_sigmoid"), w.up(sem("gate_sigmoid")))
                if d == 1:
                    v.tensor_copy(chunks(cfg["v"]), chunks(HG[0]["v"])[:, :, ::-1])\
                        .then_inc(sem("decay_v_ready"), 1)
                for m in range(DC):
                    s_ = slice(m * T, (m + 1) * T)
                    ins = ts(cfg["k"][:, s_], cfg["e"][:, s_], om[:, m:m + 1], lb[:, m:m + 1],
                             ALU.mult, ALU.add)
                ins.then_inc(sem("dve_step"), 1)
                dve.wait_ge(sem("dve_step"), w.up(sem("dve_step")))
                ts(cfg["e"], cfg["k"], 2.0 ** -63, None, ALU.max).then_inc(sem("gate_clamped"), 1)
                ts(cfg["k"], cfg["k"], -1.0, 1.0, ALU.mult, ALU.add)
                dve.wait_ge(sem("log_gate"), w.up(sem("log_gate")))
                cumulate(cfg)
                if d == 0:
                    modulate(2, 12)
                decay_attention(cfg)
                if d == 0:
                    v.tensor_copy(HG_MIX, PA[:, :]).then_inc(sem("decay_out_taken"), 1)
                    dve.wait_ge(sem("decay_out_taken"), w.up(sem("decay_out_taken")))
                else:
                    tt(chunks(HG_MIX), chunks(HG_MIX), chunks(PA[:, :])[:, :, ::-1], ALU.add)\
                        .then_inc(sem("heads_ready"), 1)
                    dve.wait_ge(sem("heads_ready"), w.up(sem("heads_ready")))
            head_norm(HG_MIX, TMP, HG_HEADS, lambda h: p("hg_norm_g", h, 1), HG_G)\
                .then_inc(sem("mix_ready"), 1)
            add_product("hg_out", modulation(0, 0, 2))
            normalize(H[:, :], gains(0, 1), modulation(0, 1, 0), "h_ready")
            peer(0)
            normalize(H[:, :], gains(1, 0), modulation(1, 0, 0), "h_ready")
            nlam, ln1, rate = coef[:, 64:80], coef[:, 80:96], coef[:, 96:112]
            ts(nlam, p("lru_lam"), -1.0, None, ALU.mult).then_inc(sem("lam_negated"), 1)
            loop(DC, convolution("lru_in", DC, LRU["xc"], lambda tap: p("lru_conv_w", tap * DC, DC),
                                 [-2, -1, 0, 1], [0] * 4, p("lru_conv_b")))
            dve.wait_ge(sem("lam_negated"), w.up(sem("lam_negated")))
            dve.wait_ge(sem("softplus_ln"), w.up(sem("softplus_ln")))
            stt(rate, nlam, 0.0, ln1, ALU.max, ALU.add).then_inc(sem("dve_step"), 1)
            dve.wait_ge(sem("dve_step"), w.up(sem("dve_step")))
            ts(rate, rate, -LRU_C, None, ALU.mult).then_inc(sem("dve_step"), 1)
            dve.wait_ge(sem("dve_step"), w.up(sem("dve_step")))
            dve.wait_ge(sem("lru_gate_taken"), w.up(sem("lru_gate_taken"), 8))
            all_taken("lru_in")
            for d in range(2):
                la, a, m_, h_ = LRU["la"], LRU["a"], LRU["m"], (LRU["h0"], LRU["h1"])[d]
                for m in range(DC):
                    s_ = slice(m * T, (m + 1) * T)
                    ins = ts(la[:, s_], LRU["gate"][2 * d][:, s_], rate[:, d * DC + m:d * DC + m + 1],
                             None, ALU.mult)
                ins.then_inc(sem("log_a"), 1)
                dve.wait_ge(sem("lru_a"), w.up(sem("lru_a")))
                dve.wait_ge(sem("lru_tanh"), w.up(sem("lru_tanh")))
                tt(la, a, a, ALU.mult).then_inc(sem("dve_step"), 1)
                dve.wait_ge(sem("dve_step"), w.up(sem("dve_step")))
                stt(m_, la, 1.0, m_, ALU.add, ALU.mult).then_inc(sem("mult_square"), 1)
                dve.wait_ge(sem("mult_square"), w.up(sem("mult_square")))
                tt(la, LRU["gate"][2 * d + 1], LRU["xc"], ALU.mult).then_inc(sem("dve_step"), 1)
                dve.wait_ge(sem("dve_step"), w.up(sem("dve_step")))
                dve.wait_ge(sem("lru_mult"), w.up(sem("lru_mult")))
                tt(m_, m_, la, ALU.mult).then_inc(sem("dve_step"), 1)
                dve.wait_ge(sem("dve_step"), w.up(sem("dve_step")))
                for m in range(DC):
                    s_ = slice(m * T, (m + 1) * T)
                    a1, u1, h1 = a[:, s_], m_[:, s_], h_[:, s_]
                    if d:
                        a1, u1, h1 = a1[:, ::-1], u1[:, ::-1], h1[:, ::-1]
                    ins = v.tensor_tensor_scan(h1, a1, u1, 0.0, ALU.mult, ALU.add)
                ins.then_inc(sem("dve_step"), 1)
                dve.wait_ge(sem("dve_step"), w.up(sem("dve_step")))
            tt(LRU["h0"], LRU["h0"], LRU["h1"], ALU.add).then_inc(sem("dve_step"), 1)
            dve.wait_ge(sem("dve_step"), w.up(sem("dve_step")))
            tt(LRU["h0"], LRU["h0"], LRU["y"], ALU.mult).then_inc(sem("mix_ready"), 1)
            add_product("lru_out", modulation(1, 0, 2))
            normalize(H[:, :], gains(1, 1), modulation(1, 1, 0), "h_ready")
            peer(1)
            dve.wait_ge(sem("x_ready"), w.up(sem("x_ready"), 4))
            normalize(X[:, :], p("final_g"), None, "x_normed")
            dve.wait_ge(sem("x_normed"), w.up(sem("x_normed")))
            even_mixer()
            layer_norm(0)
            dve.wait_ge(sem("x_normed"), w.up(sem("x_normed")))
            conv_ffn(0)
            layer_norm(1)
            dve.wait_ge(sem("x_normed"), w.up(sem("x_normed")))
            odd_mixer()
            layer_norm(2)
            dve.wait_ge(sem("x_normed"), w.up(sem("x_normed")))
            conv_ffn(1)
            layer_norm(3)
            dve.wait_ge(sem("x_normed"), w.up(sem("x_normed")))
            v.tensor_copy(stat[:, 12:13], X[:, 0:1]).then_inc(sem("result_ready"), 1)

        @block.gpsimd
        def _(pool):
            w = Tally()

            def load_ada(k, g):
                pool.dma_start(ADA_RING[:, k * TILE:(k + 1) * TILE], ada_in[g, k])\
                    .then_inc(ada_loaded[k], 16)

            for k in range(DC):
                load_ada(k, 0)
            with pool.Fori(1, 12) as g:
                for k in range(DC):
                    pool.wait_ge(sem("ada_used"), g * DC + (k - DC + 1))
                    load_ada(k, g)

            def attention_bias(dst, n_tiles=TT):
                for t in range(n_tiles):
                    src = bass.AP(skew.tensor, 255 - P * t, [[4 * SKEW - 1, P], [SKEW, 4], [1, T]])
                    pool.dma_start(dst[:, t * 4 * T:(t + 1) * 4 * T].rearrange("p (h k) -> p h k", h=4),
                                   src).then_inc(sem("attention_tables_loaded"), 16)

            e = EVEN
            pool.wait_ge(sem("x_normed"), w.up(sem("x_normed")))
            pool.dma_start(REL, bias_in).then_inc(sem("bias_loaded"), 16)
            pool.dma_start(ONEHOT, masks_in[:, MASK_BUCKET:MASK_BUCKET + SKEW])\
                .then_inc(sem("bias_loaded"), 16)
            pool.dma_start(e["low"], masks_in[:, MASK_LOW:MASK_LOW + PAIR_LEVELS * P])\
                .then_inc(sem("low_masks_loaded"), 16)
            pool.wait_ge(sem("bias_rows_taken"), w.up(sem("bias_rows_taken")))
            pool.dma_start(skew, ROWS).then_inc(sem("bias_rows_stored"), 16)
            pool.wait_ge(sem("bias_rows_stored"), w.up(sem("bias_rows_stored"), 16))
            pool.wait_ge(sem("gdn_out_psum"), w.up(sem("gdn_out_psum")))
            attention_bias(e["bias"])
            pool.dma_start(e["neg"], masks_in[:, MASK_SWA:MASK_SWA + 6 * T])\
                .then_inc(sem("attention_tables_loaded"), 16)
            pool.wait_ge(sem("x_normed"), w.up(sem("x_normed"), 2))
            e = ODD
            attention_bias(e["bias"])
            pool.dma_start(e["neg"], masks_in[:, MASK_CAUSAL:MASK_CAUSAL + 2 * T])\
                .then_inc(sem("attention_tables_loaded"), 16)
            pool.dma_start(e["lamv"], lam_in).then_inc(sem("attention_tables_loaded"), 16)


def constants():
    i = np.arange(P)
    s, t = i[:, None], i[None, :]
    eye = np.eye(P)
    ones = np.ones((P, P))
    pairs = [((s >> (l + 1)) == (t >> (l + 1))) & (((s >> l) & 1) == 0) & (((t >> l) & 1) == 1)
             for l in range(PAIR_LEVELS)]
    parts = {
        "ident": eye, "ones": ones, "mean_d": ones / D, "mean_head": ones / P,
        "iota": np.tile(i, (P, 1)), "iota16": np.tile(np.arange(TOPK), (P, 1)),
        "tri": s <= t, "strict": s < t, "pairs": np.concatenate(pairs, 1),
        "eps": np.tile([1e-6, 1e-5], (P, 1)), "zero": np.zeros((P, P)),
    }
    consts = np.concatenate([np.asarray(parts[n], np.float32) for n, _ in CONSTS], 1)
    q, k = np.arange(T)[:, None], np.arange(T)[None, :]
    dist = q - k
    swa = np.zeros((TT, P, SWA_GROUPS, T), np.float32)
    for g, (window, dil) in enumerate(SWA_CONFIGS):
        ok = (dist >= 0) & (dist % dil == 0) & (dist // dil <= window // dil)
        swa[:, :, g] = np.where(ok, 0.0, NEG).reshape(TT, P, T)
    causal = np.where(dist >= 0, 0.0, NEG).reshape(TT, P, T)
    dd = np.maximum(255 - np.arange(SKEW), 0)
    exact = NUM_BUCKETS // 2
    f = np.float32
    large = exact + (np.log(np.maximum(dd, 1).astype(f) / f(exact)) / f(math.log(REL_MAX / exact))
                     * f(NUM_BUCKETS - exact)).astype(np.int32)
    bucket = np.where(dd < exact, dd, np.minimum(large, NUM_BUCKETS - 1))
    onehot = np.zeros((P, SKEW), np.float32)
    onehot[bucket, np.arange(SKEW)] = 1
    low = np.concatenate([m.T for m in pairs], 1)
    masks = np.concatenate([low, swa.transpose(1, 0, 2, 3).reshape(P, -1),
                            causal.transpose(1, 0, 2).reshape(P, -1), onehot], 1)
    return consts, np.ascontiguousarray(masks, np.float32)


def tiles_of(w):
    k, m = w.shape
    return w.reshape(k // P, P, m // P, P).transpose(2, 1, 0, 3).reshape(m // P, P, -1)


def column_chunks(v):
    return v.reshape(-1, P).T


def lay_out(a):
    a = {k: np.asarray(v) for k, v in a.items()}
    f = np.float32
    tiles = np.zeros((STREAM_USED, P, TILE), f)

    def put(name, arr):
        at, n = STREAM_AT[name]
        tiles[at:at + n] = arr

    for l in range(2):
        put(f"wq{l}", tiles_of(a["peer_w_q"][l]))
        put(f"keys{l}", a["peer_keys"][l].reshape(2, 8, NKEYS, P).transpose(0, 3, 1, 2).reshape(2, P, TILE))
        at, n = STREAM_AT[f"experts{l}"]
        up = a["peer_u"][l].reshape(NKEYS, NKEYS, DC, P).transpose(1, 3, 2, 0)
        down = a["peer_v"][l].reshape(NKEYS, NKEYS, D).transpose(1, 0, 2)
        tiles[at:at + 2] = up[:2].reshape(2, P, TILE)
        tiles[at + 2:at + n - 2:2] = up[2:MAIN].reshape(MAIN - 2, P, TILE)
        for j in range(MAIN):
            tiles[at + down_at(j)] = down[j]
        put(f"early{l}", up[MAIN:].reshape(EARLY, P, TILE))
        put(f"late{l}", down[MAIN:])
        put(f"up{l}", tiles_of(a["ffn_w_up_2"][l]))
        put(f"down{l}", a["ffn_w_down_2"][l].reshape(FC, P, D))
    put("hg_in", tiles_of(a["hg_w_in"][0]))
    put("hg_out", tiles_of(a["hg_w_out"][0]))
    put("lru_in", tiles_of(a["lru_w_in"][0]))
    put("lru_out", tiles_of(a["lru_w_out"][0]))
    g = np.stack([a["lru_w_a"][0], a["lru_w_x"][0]], 1)
    g = g.reshape(2, 2, 2, 2, 2, P, 2, P)
    put("lru_gates", g.transpose(0, 1, 2, 5, 3, 6, 4, 7).reshape(8, P, TILE))
    we, wo = a["w_in_even_2"][0], a["w_in_odd_2"][0]
    nba = 4 * GDN_HEADS * P
    put("even_in", tiles_of(np.concatenate([we[:, :nba], we[:, nba + 12:]], 1)))
    put("even_out", tiles_of(a["w_out_even_2"][0]))
    put("odd_in", tiles_of(wo[:, :24 * P]))
    put("odd_out", tiles_of(a["w_out_odd_2"][0]))

    vec = {
        "c": a["c"], "norm_g": a["norm_g"], "b_ada": a["b_ada"], "hg_lb": a["hg_lb"],
        "hg_norm_g": a["hg_norm_g"], "lru_conv_w": a["lru_conv_w"], "lru_conv_b": a["lru_conv_b"],
        "lru_b_a": a["lru_b_a"], "lru_b_x": a["lru_b_x"], "lru_lam": a["lru_lam"],
        "final_g": a["final_g"], "gdn_conv_w": a["gdn_conv_w_2"], "gdn_norm_w": a["gdn_norm_w_2"],
        "diff_norm_w": a["diff_norm_w_2"], "gla_b_gate": a["gla_b_gate_2"],
        "gla_norm_w": a["gla_norm_w_2"], "ffn_conv_w": a["ffn_conv_w_2"],
        "ffn_conv_b": a["ffn_conv_b_2"], "ln_g": a["ln_g_2"], "ln_b": a["ln_b_2"],
    }
    cols = {n: column_chunks(x) for n, x in vec.items()}
    for n in ("gdn_dt_bias", "gdn_a_log"):
        cols[n] = np.repeat(a[n + "_2"].reshape(1, GDN_HEADS), P, 0)
    for n, size in PARAMS:
        assert cols[n].shape == (P, size), (n, cols[n].shape)
    params = np.concatenate([cols[n] for n, _ in PARAMS], 1)

    def by_rows(w):
        return w.reshape(DC, P, -1).transpose(1, 0, 2).reshape(P, -1)

    gate = np.zeros((P, 2 * P), f)
    gate[:GATE_RANK] = a["gla_w_gate_2"][0]
    small = np.concatenate([by_rows(we[:, nba:nba + 12]), by_rows(wo[:, 24 * P:]), gate], 1)
    bias = np.zeros((P, 4, P), f)
    bias[:NUM_BUCKETS] = a["rel_bias_2"][:, :, None]
    consts, masks = constants()
    x = a["x"][0].reshape(T, DC, P).transpose(2, 1, 0).reshape(P, -1)
    lam = np.repeat(a["diff_lambda_2"][0].reshape(1, -1), P, 0)
    ada = a["w_ada"].reshape(2, DC, P, 6, D).transpose(0, 3, 1, 2, 4).reshape(12, DC, P, D)
    return {"tiles": tiles, "ada": ada, "x": x, "params": params, "consts": consts, "small": small, "masks": masks,
            "lam": lam, "bias": bias.reshape(P, -1)}


ORDER = ["tiles", "ada", "x", "params", "consts", "small", "masks", "lam", "bias"]


def kernel(**inputs):
    import concourse.bacc as _bacc
    from concourse.bass_utils import run_bass_kernel_spmd as _run

    nc = _bacc.Bacc("TRN2", target_bir_lowering=False, num_devices=1)
    arrays = {n: np.ascontiguousarray(v) for n, v in lay_out(inputs).items()}
    args = [nc.dram_tensor(n, arrays[n].shape, F32, kind="ExternalInput").ap() for n in ORDER]
    skew = nc.dram_tensor("skew", (P, 4 * SKEW), F32, kind="Internal").ap()
    out = nc.dram_tensor("out", (P, DC * T), F32, kind="ExternalOutput").ap()
    build(nc, *args, skew, out)
    r = _run(nc, [arrays], core_ids=[0])
    got = r.results[0]["out"]
    return np.ascontiguousarray(got.reshape(P, DC, T).transpose(2, 1, 0).reshape(1, T, D))
```
